# Optimizing a Trainium2 kernel written in Bass

```python
import jax, jax.numpy as jnp
from jax import lax
import numpy as np

D_MODEL = 1024
BATCH = 1
SEQ = 256
DEPTH = 2

CHUNK = 64
HEAD_DIM = 128
EPS = 1e-6
N_HEADS_A = 4
A_WIDTH = N_HEADS_A * HEAD_DIM
IDX_HEADS = 8
IDX_DIM = 64
IDX_TOPK_MAX = 256
N_HEADS_B = 4
GLA_DK = 64
GLA_DV = 128
GLA_GATE_RANK = 16
GLA_TAU = 16.0
B_WIDTH = N_HEADS_B * GLA_DV
N_HEADS_C = 8
C_WIDTH = N_HEADS_C * HEAD_DIM
SB_QBLOCK = 128
ROPE_THETA = 500000.0
ROPE_FRACTION = 4
D_FF = 4 * D_MODEL
N_EVEN = (DEPTH + 1) // 2
N_ODD = DEPTH // 2
AB_SIZES = (
    A_WIDTH, A_WIDTH, A_WIDTH,
    IDX_HEADS * IDX_DIM, IDX_DIM, IDX_HEADS,
    N_HEADS_B * GLA_DK, N_HEADS_B * GLA_DK,
    B_WIDTH,
    GLA_GATE_RANK,
    B_WIDTH,
)
AB_PROJ = sum(AB_SIZES)


def _split(a, sizes):
    out, o = [], 0
    for s in sizes:
        out.append(a[..., o:o + s])
        o += s
    return out

def rmsnorm(x, g):
    xf = x.astype(jnp.float32)
    y = xf * lax.rsqrt(jnp.mean(xf * xf, axis=-1, keepdims=True) + EPS)
    return (y * g.astype(jnp.float32)).astype(x.dtype)

def rope_partial(x, pos):
    d = x.shape[-1]
    rot = d // ROPE_FRACTION
    half = rot // 2
    inv = jnp.power(ROPE_THETA, -jnp.arange(half, dtype=jnp.float32) * 2.0 / rot)
    ang = pos.astype(jnp.float32)[:, None] * inv[None, :]
    cos = jnp.cos(ang)[None, :, None, :]
    sin = jnp.sin(ang)[None, :, None, :]
    xf = x.astype(jnp.float32)
    x1, x2, rest = xf[..., :half], xf[..., half:rot], xf[..., rot:]
    out = jnp.concatenate([x1 * cos - x2 * sin, x2 * cos + x1 * sin, rest], axis=-1)
    return out.astype(x.dtype)

def dsa_attention(q, k, v, iq, ik, iw):
    bsz, s_len, n_h, d_h = q.shape
    topk = min(IDX_TOPK_MAX, s_len // 4)
    n_blk = s_len // CHUNK
    key_pos = jnp.arange(s_len)

    def blk_fn(args):
        c, qb, iqb, iwb = args
        logits = jnp.einsum('bthd,bsd->bths', iqb, ik).astype(jnp.float32) * IDX_DIM ** -0.5
        score = jnp.einsum('bths,bth->bts', jax.nn.relu(logits),
                           iwb.astype(jnp.float32) * IDX_HEADS ** -0.5)
        limit = (c + 1) * CHUNK
        score = jnp.where((key_pos < limit)[None, None, :], score, -jnp.inf)
        _, idx = lax.top_k(score, topk)
        valid = idx < limit
        ks = jax.vmap(lambda a, i: a[i])(k, idx)
        vs = jax.vmap(lambda a, i: a[i])(v, idx)
        s = jnp.einsum('bthd,btkhd->bthk', qb, ks).astype(jnp.float32) * HEAD_DIM ** -0.5
        s = jnp.where(valid[:, :, None, :], s, -jnp.inf)
        p = jax.nn.softmax(s, axis=-1)
        return jnp.einsum('bthk,btkhd->bthd', p.astype(v.dtype), vs)

    def to_blocks(a):
        return a.reshape(bsz, n_blk, CHUNK, *a.shape[2:]).swapaxes(0, 1)

    out = lax.map(blk_fn, (jnp.arange(n_blk), to_blocks(q), to_blocks(iq), to_blocks(iw)))
    return out.swapaxes(0, 1).reshape(bsz, s_len, n_h, d_h)

def gla_chunked(q, k, v, lg):
    bsz, s_len, n_h, dk = q.shape
    dv = v.shape[-1]
    n_c = s_len // CHUNK
    causal = jnp.tril(jnp.ones((CHUNK, CHUNK), dtype=bool))

    def chunks(a):
        return a.astype(jnp.float32).reshape(bsz, n_c, CHUNK, n_h, a.shape[-1]).transpose(1, 0, 3, 2, 4)

    def step(state, inp):
        qc, kc, vc, gc = inp
        b = jnp.cumsum(gc, axis=2)
        o_inter = jnp.einsum('bhtd,bhde->bhte', qc * jnp.exp(b), state)
        diff = b[:, :, :, None, :] - b[:, :, None, :, :]
        decay = jnp.exp(jnp.where(causal[:, :, None], diff, -jnp.inf))
        att = jnp.einsum('bhtd,bhsd,bhtsd->bhts', qc, kc, decay)
        o = o_inter + jnp.einsum('bhts,bhse->bhte', att, vc)
        b_last = b[:, :, -1:, :]
        state = (jnp.exp(b_last[:, :, 0, :])[..., None] * state
                 + jnp.einsum('bhsd,bhse->bhde', kc * jnp.exp(b_last - b), vc))
        return state, o

    s0 = jnp.zeros((bsz, n_h, dk, dv), jnp.float32)
    _, o = lax.scan(step, s0, (chunks(q), chunks(k), chunks(v), chunks(lg)))
    return o.transpose(1, 0, 3, 2, 4).reshape(bsz, s_len, n_h, dv)

def stick_breaking(q, k, v):
    bsz, s_len, n_h, d_h = q.shape
    n_blk = s_len // SB_QBLOCK
    key_pos = jnp.arange(s_len)

    def blk_fn(args):
        i, qb = args
        z = jnp.einsum('bthd,bshd->bhts', qb, k).astype(jnp.float32) * d_h ** -0.5
        t_pos = i * SB_QBLOCK + jnp.arange(SB_QBLOCK)
        mask = key_pos[None, :] < t_pos[:, None]
        lo = jnp.where(mask, jax.nn.log_sigmoid(-z), 0.0)
        rc = lax.cumsum(lo, axis=3, reverse=True)
        log_a = jax.nn.log_sigmoid(z) + (rc - lo)
        a = jnp.where(mask, jnp.exp(log_a), 0.0)
        return jnp.einsum('bhts,bshd->bthd', a.astype(v.dtype), v)

    qb = q.reshape(bsz, n_blk, SB_QBLOCK, n_h, d_h).swapaxes(0, 1)
    out = lax.map(blk_fn, (jnp.arange(n_blk), qb))
    return out.swapaxes(0, 1).reshape(bsz, s_len, n_h, d_h)

def mixer_ab(n, pos, w_in, gq, gk, w_gate_up, b_gate, g_gla, w_out):
    bsz, s_len, _ = n.shape
    proj = n @ w_in
    (qa, ka, va, iq, ik, iw, qb, kb, vb, g_low, og) = _split(proj, AB_SIZES)
    qa = rope_partial(rmsnorm(qa.reshape(bsz, s_len, N_HEADS_A, HEAD_DIM), gq), pos)
    ka = rope_partial(rmsnorm(ka.reshape(bsz, s_len, N_HEADS_A, HEAD_DIM), gk), pos)
    va = va.reshape(bsz, s_len, N_HEADS_A, HEAD_DIM)
    iq = rope_partial(iq.reshape(bsz, s_len, IDX_HEADS, IDX_DIM), pos)
    ik = rope_partial(ik[:, :, None, :], pos)[:, :, 0, :]
    oa = dsa_attention(qa, ka, va, iq, ik, iw).reshape(bsz, s_len, A_WIDTH)
    qb = qb.reshape(bsz, s_len, N_HEADS_B, GLA_DK) * GLA_DK ** -0.5
    kb = kb.reshape(bsz, s_len, N_HEADS_B, GLA_DK)
    vb = vb.reshape(bsz, s_len, N_HEADS_B, GLA_DV)
    gate = (g_low @ w_gate_up + b_gate).astype(jnp.float32)
    lg = (jax.nn.log_sigmoid(gate) / GLA_TAU).reshape(bsz, s_len, N_HEADS_B, GLA_DK)
    ob = gla_chunked(qb, kb, vb, lg).astype(n.dtype)
    ob = rmsnorm(ob, g_gla).reshape(bsz, s_len, B_WIDTH) * jax.nn.silu(og)
    return jnp.concatenate([oa, ob], axis=-1) @ w_out

def mixer_c(n, w_in, gq, gk, w_out):
    bsz, s_len, _ = n.shape
    q, k, v = _split(n @ w_in, (C_WIDTH, C_WIDTH, C_WIDTH))
    q = rmsnorm(q.reshape(bsz, s_len, N_HEADS_C, HEAD_DIM), gq)
    k = rmsnorm(k.reshape(bsz, s_len, N_HEADS_C, HEAD_DIM), gk)
    v = v.reshape(bsz, s_len, N_HEADS_C, HEAD_DIM)
    return stick_breaking(q, k, v).reshape(bsz, s_len, C_WIDTH) @ w_out

def squared_relu_mlp(n, w_up, w_down):
    return jnp.square(jax.nn.relu(n @ w_up)) @ w_down

def first_inputs(seed: int = 0) -> dict:
    key = jax.random.key(seed)
    ks = jax.random.split(key, 16)
    f32 = jnp.float32

    def w(k, shape, fan_in):
        return jax.random.normal(k, shape, f32) * fan_in ** -0.5

    def gain(k, shape):
        return 1.0 + 0.02 * jax.random.normal(k, shape, f32)

    return {
        "x": jax.random.normal(ks[0], (BATCH, SEQ, D_MODEL), f32),
        "g_mix": gain(ks[1], (DEPTH, D_MODEL)),
        "g_ffn": gain(ks[2], (DEPTH, D_MODEL)),
        "w_in_ab": w(ks[3], (N_EVEN, D_MODEL, AB_PROJ), D_MODEL),
        "gq_a": gain(ks[4], (N_EVEN, HEAD_DIM)),
        "gk_a": gain(ks[5], (N_EVEN, HEAD_DIM)),
        "w_gate_up": w(ks[6], (N_EVEN, GLA_GATE_RANK, N_HEADS_B * GLA_DK), GLA_GATE_RANK),
        "b_gate": 0.1 * jax.random.normal(ks[7], (N_EVEN, N_HEADS_B * GLA_DK), f32),
        "g_gla": gain(ks[8], (N_EVEN, GLA_DV)),
        "w_out_ab": w(ks[9], (N_EVEN, A_WIDTH + B_WIDTH, D_MODEL), A_WIDTH + B_WIDTH),
        "w_in_c": w(ks[10], (N_ODD, D_MODEL, 3 * C_WIDTH), D_MODEL),
        "gq_c": gain(ks[11], (N_ODD, HEAD_DIM)),
        "gk_c": gain(ks[12], (N_ODD, HEAD_DIM)),
        "w_out_c": w(ks[13], (N_ODD, C_WIDTH, D_MODEL), C_WIDTH),
        "w_up": w(ks[14], (DEPTH, D_MODEL, D_FF), D_MODEL),
        "w_down": w(ks[15], (DEPTH, D_FF, D_MODEL), D_FF),
    }

def first_block(x, g_mix, g_ffn, w_in_ab, gq_a, gk_a, w_gate_up, b_gate, g_gla, w_out_ab,
              w_in_c, gq_c, gk_c, w_out_c, w_up, w_down):
    pos = jnp.arange(x.shape[1])
    h = x
    for layer in range(DEPTH):
        n = rmsnorm(h, g_mix[layer])
        if layer % 2 == 0:
            i = layer // 2
            h = h + mixer_ab(n, pos, w_in_ab[i], gq_a[i], gk_a[i], w_gate_up[i],
                             b_gate[i], g_gla[i], w_out_ab[i])
        else:
            i = layer // 2
            h = h + mixer_c(n, w_in_c[i], gq_c[i], gk_c[i], w_out_c[i])
        h = h + squared_relu_mlp(rmsnorm(h, g_ffn[layer]), w_up[layer], w_down[layer])
    return h


DEPTH_2 = 1

N_META = 16
FOURIER_GROUPS = 4
FOURIER_GROUP_DIM = 128
FOURIER_WIDTH = FOURIER_GROUPS * FOURIER_GROUP_DIM
CONV_HEADS = 8
CONV_HEAD_DIM = 64
CONV_WIDTH = CONV_HEADS * CONV_HEAD_DIM
CONV_TAPS = 3
N_BRANCHES = 2
D_FF_2 = 2816
RMS_EPS = 1e-6
IN_COLS = FOURIER_WIDTH + 3 * CONV_WIDTH + N_BRANCHES * D_MODEL


def rmsnorm_2(x, g):
    xf = x.astype(jnp.float32)
    var = jnp.mean(xf * xf, axis=-1, keepdims=True)
    return (xf * lax.rsqrt(var + RMS_EPS) * g.astype(jnp.float32)).astype(x.dtype)

def centred_dwconv(x, w, b):
    half = CONV_TAPS // 2
    L = x.shape[1]
    xp = jnp.pad(x, ((0, 0), (half, half), (0, 0)))
    y = b
    for k in range(CONV_TAPS):
        y = y + xp[:, k:k + L] * w[k]
    return y

def fourier_mix(u):
    bn, L, _ = u.shape
    ug = u.astype(jnp.float32).reshape(bn, L, FOURIER_GROUPS, FOURIER_GROUP_DIM)
    f = jnp.fft.fft2(ug, axes=(1, 3), norm="ortho").real
    return f.reshape(bn, L, FOURIER_WIDTH).astype(u.dtype)

def second_inputs(seed: int = 0) -> dict:
    key = jax.random.key(seed)
    ks = jax.random.split(key, 20)
    f32 = jnp.float32

    def normal(k, shape, fan_in):
        return jax.random.normal(k, shape, f32) * (fan_in ** -0.5)

    def gain(k, shape):
        return 1.0 + 0.02 * jax.random.normal(k, shape, f32)

    def bias(k, shape):
        return 0.01 * jax.random.normal(k, shape, f32)

    return {
        "x": jax.random.normal(ks[0], (BATCH, SEQ, D_MODEL), f32),
        "meta_tokens": jax.random.normal(ks[1], (N_META, D_MODEL), f32),
        "g_mix_pre": gain(ks[2], (DEPTH_2, D_MODEL)),
        "w_in": normal(ks[3], (DEPTH_2, D_MODEL, IN_COLS), D_MODEL),
        "b_gates": bias(ks[4], (DEPTH_2, N_BRANCHES * D_MODEL)),
        "w_fourier": normal(ks[5], (DEPTH_2, FOURIER_WIDTH, D_MODEL), FOURIER_WIDTH),
        "conv_w_mix": normal(ks[6], (DEPTH_2, CONV_TAPS, CONV_WIDTH), CONV_TAPS),
        "conv_b_mix": bias(ks[7], (DEPTH_2, CONV_WIDTH)),
        "w_conv_out": normal(ks[8], (DEPTH_2, CONV_WIDTH, D_MODEL), CONV_WIDTH),
        "w_out": normal(ks[9], (DEPTH_2, D_MODEL, D_MODEL), D_MODEL),
        "g_mix_post": gain(ks[10], (DEPTH_2, D_MODEL)),
        "g_ffn_pre": gain(ks[11], (DEPTH_2, D_MODEL)),
        "w_up": normal(ks[12], (DEPTH_2, D_MODEL, 2 * D_FF_2), D_MODEL),
        "conv_w_ffn": normal(ks[13], (DEPTH_2, CONV_TAPS, 2 * D_FF_2), CONV_TAPS),
        "conv_b_ffn": bias(ks[14], (DEPTH_2, 2 * D_FF_2)),
        "w_down": normal(ks[15], (DEPTH_2, D_FF_2, D_MODEL), D_FF_2),
        "g_ffn_post": gain(ks[16], (DEPTH_2, D_MODEL)),
    }

def second_block(x, meta_tokens, g_mix_pre, w_in, b_gates, w_fourier, conv_w_mix, conv_b_mix,
              w_conv_out, w_out, g_mix_post, g_ffn_pre, w_up, conv_w_ffn, conv_b_ffn,
              w_down, g_ffn_post):
    bn = x.shape[0]
    meta = jnp.broadcast_to(meta_tokens[None].astype(x.dtype), (bn, N_META, D_MODEL))
    h_res = jnp.concatenate([meta, x], axis=1)
    L = h_res.shape[1]

    splits = [FOURIER_WIDTH,
              FOURIER_WIDTH + CONV_WIDTH,
              FOURIER_WIDTH + 2 * CONV_WIDTH,
              FOURIER_WIDTH + 3 * CONV_WIDTH]

    for l in range(DEPTH_2):
        h = rmsnorm_2(h_res, g_mix_pre[l])
        proj = h @ w_in[l]
        u_a, c_g, b_g, v_b, gate_logits = jnp.split(proj, splits, axis=-1)

        y_a = fourier_mix(u_a) @ w_fourier[l]

        conv_in = c_g * v_b
        y_b = (b_g * centred_dwconv(conv_in, conv_w_mix[l], conv_b_mix[l])) @ w_conv_out[l]

        gates = jax.nn.sigmoid((gate_logits + b_gates[l]).reshape(bn, L, N_BRANCHES, D_MODEL))
        merged = gates[:, :, 0] * y_a + gates[:, :, 1] * y_b
        mix_out = merged @ w_out[l]
        h_res = h_res + rmsnorm_2(mix_out, g_mix_post[l])

        h2 = rmsnorm_2(h_res, g_ffn_pre[l])
        up = centred_dwconv(h2 @ w_up[l], conv_w_ffn[l], conv_b_ffn[l])
        a, v = jnp.split(up, 2, axis=-1)
        ffn_out = (jax.nn.gelu(a) * v) @ w_down[l]
        h_res = h_res + rmsnorm_2(ffn_out, g_ffn_post[l])

    return h_res[:, N_META:]


def setup_inputs(seed=0):
    out = dict(first_inputs(seed))
    for name, value in second_inputs(seed + 1).items():
        if name != "x":
            out[name + "_2"] = value
    return out


def reference(
    x, g_mix, g_ffn, w_in_ab, gq_a, gk_a, w_gate_up, b_gate, g_gla, w_out_ab, w_in_c, gq_c,
    gk_c, w_out_c, w_up, w_down, meta_tokens_2, g_mix_pre_2, w_in_2, b_gates_2, w_fourier_2,
    conv_w_mix_2, conv_b_mix_2, w_conv_out_2, w_out_2, g_mix_post_2, g_ffn_pre_2, w_up_2,
    conv_w_ffn_2, conv_b_ffn_2, w_down_2, g_ffn_post_2,
):
    x = first_block(
        x, g_mix, g_ffn, w_in_ab, gq_a, gk_a, w_gate_up, b_gate, g_gla, w_out_ab, w_in_c, gq_c,
        gk_c, w_out_c, w_up, w_down,
    )
    return second_block(
        x, meta_tokens_2, g_mix_pre_2, w_in_2, b_gates_2, w_fourier_2, conv_w_mix_2,
        conv_b_mix_2, w_conv_out_2, w_out_2, g_mix_post_2, g_ffn_pre_2, w_up_2, conv_w_ffn_2,
        conv_b_ffn_2, w_down_2, g_ffn_post_2,
    )


_drawn_inputs = setup_inputs


def setup_inputs(seed=0):
    import zlib

    import numpy as np

    out = dict(_drawn_inputs(seed))
    spreads = {}
    factors = {'gq_a': 8.0,
     'gk_a': 8.0,
     'g_gla': 4.907,
     'gq_c': 8.0,
     'gk_c': 8.0,
     'g_mix_pre_2': 3.952,
     'b_gates_2': 25.782,
     'conv_b_mix_2': 64.0,
     'g_mix_post_2': 6.33,
     'g_ffn_pre_2': 4.785,
     'conv_b_ffn_2': 26.752,
     'g_ffn_post_2': 27.361}
    for name, (base, spread) in spreads.items():
        noise = np.random.default_rng([zlib.crc32(name.encode()), seed]).standard_normal(out[name].shape)
        drawn = base * np.exp(spread * noise) if base else spread * noise
        out[name] = __import__('jax').numpy.asarray(drawn.astype(out[name].dtype))
    for name, factor in factors.items():
        out[name] = (out[name] * factor).astype(out[name].dtype)
    return out
```

```python
from contextlib import ExitStack

import numpy as np

import concourse.bass as bass
from concourse import mybir

ALU = mybir.AluOpType
ACT = mybir.ActivationFunctionType
AX = mybir.AxisListType
F32 = mybir.dt.float32

P = 128
D = 1024
S = 256
EPS = 1e-6
META = 16
L2 = META + S
X0 = 14
N2 = L2 - X0
SLOT = 4096
NSLOT = 4
BIGNEG = -1.0e30

VEC_COLS = [
    ("g_mix0", 8), ("g_ffn0", 8), ("g_mix1", 8), ("g_ffn1", 8), ("b_gate", 2), ("g_gla", 1),
    ("gq_c", 1), ("gk_c", 1), ("g_mix_pre", 8), ("b_gates", 16), ("conv_w_mix", 12),
    ("conv_b_mix", 4), ("g_mix_post", 8), ("g_ffn_pre", 8), ("conv_w_ffn", 132), ("conv_b_ffn", 44),
    ("gq_row", 128), ("gk_row", 128),
]
CST_COLS = [
    ("ident", 128), ("ones", 128), ("cosA", 32), ("sinA", 32), ("cosI", 16), ("sinI", 16),
    ("inval", 512), ("gmask", 1024), ("smask", 384), ("dftc", 256), ("dftl", 1088), ("eps", 1),
]


def offsets(cols):
    out, at = {}, 0
    for name, n in cols:
        out[name] = (at, n)
        at += n
    return out, at


VEC, NVEC = offsets(VEC_COLS)
CST, NCST = offsets(CST_COLS)


def tile_sizes():
    n = [4096, 704] + [4096] * 6
    n += [4096] * (2 + 16)
    n += [4096] * (6 + 2 + 16)
    n += [4096] * (8 + 2 + 2 + 11)
    n += [4096] * 5 + [2048]
    return n


def constants():
    c = np.zeros((P, NCST), np.float32)

    def put(name, a):
        o, n = CST[name]
        c[:, o:o + n] = a.reshape(P, n)

    put("eps", np.full((P, 1), EPS, np.float32))
    put("ident", np.eye(P, dtype=np.float32))
    put("ones", np.ones((P, P), np.float32))
    pos = np.arange(S, dtype=np.float32)
    for tag, rot in (("A", 32), ("I", 16)):
        half = rot // 2
        inv = np.power(np.float32(500000.0), -np.arange(half, dtype=np.float32) * np.float32(2.0) / np.float32(rot))
        ang = (pos[:, None] * inv[None, :].astype(np.float32)).astype(np.float32).astype(np.float64)
        put("cos" + tag, np.cos(ang).astype(np.float32).reshape(2, P, half).transpose(1, 0, 2))
        put("sin" + tag, np.sin(ang).astype(np.float32).reshape(2, P, half).transpose(1, 0, 2))
    t = np.arange(S)
    limit = (t // 64 + 1) * 64
    inval = np.where(t[None, :] < limit[:, None], 0.0, -1.0e37).astype(np.float32)
    put("inval", inval.reshape(2, P, S).transpose(1, 0, 2))
    s, t = np.arange(P)[:, None], np.arange(P)[None, :]
    masks = []
    for hs in (64, 32, 16, 8, 4, 2, 1):
        masks.append((s // (2 * hs) == t // (2 * hs)) & (s % (2 * hs) < hs) & (t % (2 * hs) >= hs))
    masks.append(s == t)
    put("gmask", np.stack(masks, 1).astype(np.float32))
    tri = np.where(s < t, 0.0, BIGNEG).astype(np.float32)
    put("smask", np.concatenate([tri, np.zeros((P, P), np.float32), tri], 1))
    k = np.outer(np.arange(P), np.arange(P)) % P
    scale = 1.0 / np.sqrt(L2 * P)
    put("dftc", np.concatenate([np.cos(2 * np.pi * k / P), np.sin(2 * np.pi * k / P)], 1).astype(np.float32))
    k = np.outer(np.arange(L2), np.arange(L2)) % L2
    dl = np.stack([np.cos(2 * np.pi * k / L2), -np.sin(2 * np.pi * k / L2)], 1) * scale
    dl = dl.astype(np.float32)
    put("dftl", dl[META:].reshape(2, P, 2, L2).transpose(1, 0, 2, 3))
    tri_s = (s > t).astype(np.float32)
    return c, np.ascontiguousarray(dl[:META].reshape(META, 2 * L2)), tri_s


class Bank:
    def __init__(self, t):
        self.t = t
        self.free = []
        self.held = False


class Slot:
    def __init__(self, t, sem):
        self.t = t
        self.sem = sem
        self.n = 0
        self.free = []


def block_kernel(nc, W, V, C, CM, TRI, X, MT, WG, GP, OUT):
    ctx = ExitStack()
    with ctx:
        def sb(name, shape):
            return ctx.enter_context(nc.sbuf_tensor(name, shape, F32))

        def sem(name):
            return ctx.enter_context(nc.semaphore(name))

        queues = {k: [] for k in ("pe", "act", "dve", "pool", "sp")}
        sems = {k: sem("s_" + k) for k in ("pe", "act", "dve", "pool")}
        count = {k: 0 for k in sems}

        def op(e, fn, waits, inc=True):
            tok = None
            if inc:
                count[e] += 1
                tok = (sems[e], count[e])
            queues[e].append((list(waits), fn, (sems[e], 1) if inc else None))
            return tok

        def dve(fn, *waits):
            return op("dve", fn, waits)

        def act(fn, *waits):
            return op("act", fn, waits)

        def pool(fn, *waits):
            return op("pool", fn, waits)

        def dma(fn, waits, s, q="sp"):
            queues[q].append((list(waits), fn, (s, 16)))

        def mm(out, lhsT, rhs, start, stop, waits=(), inc=False):
            return op("pe", lambda e: e.matmul(out, lhsT, rhs, start=start, stop=stop), waits, inc)

        def tr(out, in_, idn, waits=(), inc=False):
            return op("pe", lambda e: e.transpose(out, in_, idn), waits, inc)

        banks = [Bank(ctx.enter_context(nc.psum_tensor(f"bank{i}", [P, 512], F32))) for i in range(8)]
        bank_at = [0]

        def take(hold=False):
            while banks[bank_at[0] % 8].held:
                bank_at[0] += 1
            b = banks[bank_at[0] % 8]
            b.held = hold
            bank_at[0] += 1
            return b

        slots = [Slot(sb(f"slot{i}", [P, SLOT]), sem(f"s_w{i}")) for i in range(NSLOT)]
        sizes = tile_sizes()
        starts = [0]
        for n in sizes:
            starts.append(starts[-1] + n * P)
        tile_at = [0]

        def load():
            i = tile_at[0]
            tile_at[0] += 1
            s = slots[i % NSLOT]
            n = sizes[i]
            src = W[starts[i]:starts[i + 1]].rearrange("(p n) -> p n", p=P)
            dma(lambda e: e.dma_start(s.t[:, 0:n], src), s.free, s.sem)
            s.n += 16
            s.free = []
            return s, s.t[:, 0:n], (s.sem, s.n)

        h = sb("h", [P, 2, D])
        nT = sb("nT", [P, 8 * L2])
        nTa = nT[:, 0:8 * S].rearrange("p (k t) -> p k t", k=8)
        nT2 = nT[:, :].rearrange("p (k t) -> p k t", k=8)
        xn = sb("xn", [P, 2, D])
        catT = sb("catT", [P, 8, S])
        big = sb("big", [P, 32 * S])
        vec = sb("vec", [P, NVEC])
        cst = sb("cst", [P, NCST])
        tri = sb("tri_sb", [P, P])
        R = sb("R", [P, 14400])
        small = sb("small", [P, 256])

        def vcol(name, i=0, n=1):
            o = VEC[name][0] + i
            return vec[:, o:o + n]

        def const(name):
            o, n = CST[name]
            return cst[:, o:o + n]

        ident = const("ident")
        eps = const("eps")

        s_c = sem("s_c")
        s_x = sem("s_x")
        s_o = sem("s_o")
        s_g = sem("s_g")
        wg = sb("wg", [16, 256])
        dma(lambda e: e.dma_start(h[:, 0, :], X[0:P, :]), [], s_x, "act")
        dma(lambda e: e.dma_start(h[:, 1, :], X[P:2 * P, :]), [], s_x, "act")
        dma(lambda e: e.dma_start(cst[:, :], C), [], s_c, "act")
        dma(lambda e: e.dma_start(vec[:, :], V), [], s_c, "act")
        dma(lambda e: e.dma_start(wg[:, :], WG), [], s_c, "act")
        dma(lambda e: e.dma_start(tri[:, :], TRI), [], s_c, "act")
        TX = (s_x, 32)
        TC = (s_c, 64)

        class Area:
            def __init__(self):
                self.at = 0

            def __call__(self, n):
                a = R[:, self.at:self.at + n]
                self.at += n
                assert self.at <= 14400, self.at
                return a

        def inv_rms(ss, rs, n, *waits):
            t = act(lambda e: e.activation(rs, ss, ACT.Ln, bias=eps, scale=1.0 / n), TC, *waits)
            return act(lambda e: e.activation(rs, rs, ACT.Exp, scale=-0.5), t)

        def bc(ap, shape):
            return ap.to_broadcast(shape)

        def norm_T(gname, ready):
            ts = []
            for tt in range(2):
                a = act(lambda e, tt=tt: e.activation(xn[:, tt, :], h[:, tt, :], ACT.Square,
                                                      accum_out=small[:, tt:tt + 1]), *ready)
                r = inv_rms(small[:, tt:tt + 1], small[:, 2 + tt:3 + tt], D, a)
                ts.append(dve(lambda e, tt=tt: e.tensor_scalar(xn[:, tt, :], h[:, tt, :], small[:, 2 + tt:3 + tt],
                                                               None, ALU.mult), r))
            out = []
            for q in range(4):
                b = take()
                for kk in range(2):
                    for tt in range(2):
                        t = tr(b.t[:, kk * 256 + tt * P:kk * 256 + tt * P + P],
                               xn[:, tt, (2 * q + kk) * P:(2 * q + kk + 1) * P], ident,
                               [ts[tt], TC] + b.free, inc=(kk == 1 and tt == 1))
                if q % 2 == 0:
                    for kk in range(2):
                        k = 2 * q + kk
                        u = act(lambda e, k=k, kk=kk, b=b: e.activation(nTa[:, k, :], b.t[:, kk * 256:kk * 256 + 256],
                                                                        ACT.Copy, scale=vcol(gname, k)), t)
                else:
                    u = dve(lambda e, q=q, b=b: e.tensor_tensor(
                        nTa[:, 2 * q:2 * q + 2, :], b.t[:, :].rearrange("p (k t) -> p k t", k=2),
                        bc(vcol(gname, 2 * q, 2).rearrange("p (k o) -> p k o", o=1), [P, 2, S]), ALU.mult), t)
                b.free = [u]
                out.append(u)
            return out

        def proj_tok(w, tk, slot, ready, n=512, c0=0, width=512, last=True):
            wv = w.rearrange("p (k n) -> p k n", k=8)
            out = []
            for tt in range(2):
                b = take()
                for k in range(8):
                    t = mm(b.t[:, 0:n], nTa[:, k, tt * P:tt * P + P], wv[:, k, c0:c0 + n], k == 0, k == 7,
                           [tk] + ready + b.free, inc=(k == 7))
                out.append((b, t))
            if last:
                slot.free = [out[-1][1]]
            return out

        def out_tok(lhs, ntile, per, ready):
            bs = [take() for _ in range(4)]
            total = ntile * per
            for i in range(ntile):
                slot, w, tk = load()
                wv = w.rearrange("p (k n) -> p k n", n=D)
                for kk in range(wv.shape[1]):
                    k = i * per + kk
                    for j in range(4):
                        tt, c = j // 2, j % 2
                        t = mm(bs[j].t[:, :], lhs(k)[:, tt * P:tt * P + P], wv[:, kk, c * 512:c * 512 + 512],
                               k == 0, k == total - 1, [tk] + ready(k) + bs[j].free, inc=(kk == per - 1))
                slot.free = [t]
            res = []
            for j in range(4):
                tt, c = j // 2, j % 2
                u = dve(lambda e, j=j, tt=tt, c=c: e.tensor_tensor(h[:, tt, c * 512:c * 512 + 512],
                                                                  h[:, tt, c * 512:c * 512 + 512], bs[j].t[:, :],
                                                                  ALU.add), t)
                bs[j].free = [u]
                res.append(u)
            return res

        def mlp(gname, ready):
            tn = norm_T(gname, ready)
            ff = big[:, :].rearrange("p (k t) -> p k t", k=32)
            tf = []
            for i in range(8):
                slot, w, tk = load()
                wv = w.rearrange("p (k n) -> p k n", k=8)
                for half in range(2):
                    b = take()
                    for m in range(2):
                        c = (half * 2 + m) * P
                        for k in range(8):
                            t = mm(b.t[:, m * 256:m * 256 + 256], wv[:, k, c:c + P], nTa[:, k, :], k == 0, k == 7,
                                   [tk] + tn + b.free, inc=(k == 7))
                    m0 = i * 4 + half * 2
                    r = act(lambda e, b=b, m0=m0: e.activation(big[:, m0 * 256:m0 * 256 + 512], b.t[:, :], ACT.Relu), t)
                    u = dve(lambda e, m0=m0: e.tensor_tensor(big[:, m0 * 256:m0 * 256 + 512],
                                                             big[:, m0 * 256:m0 * 256 + 512],
                                                             big[:, m0 * 256:m0 * 256 + 512], ALU.mult), r)
                    b.free = [r]
                    tf += [u, u]
                slot.free = [t]
            return out_tok(lambda k: ff[:, k, :], 8, 4, lambda k: [tf[k]])

        A = Area()
        IQ = A(2 * 576)
        IKD = A(256)
        IQT = A(1024).rearrange("p (b t) -> p b t", b=4)
        IKT = A(256)
        RL = A(1024).rearrange("p (j n) -> p j n", j=2)
        SC = A(512).rearrange("p (t n) -> p t n", t=2)
        SEL = A(512)
        SELv = SEL.rearrange("p (t n) -> p t n", t=2)
        QKT = A(2048).rearrange("p (k t) -> p k t", k=8)
        VA = A(1024).rearrange("p (t n) -> p t n", t=2)
        VB = A(1024).rearrange("p (t n) -> p t n", t=2)
        OG = A(1024).rearrange("p (t n) -> p t n", t=2)
        QK0 = A(1024).rearrange("p (j n) -> p j n", j=2)
        BB = A(512)
        DE = A(512)
        SS = A(1024).rearrange("p (j n) -> p j n", j=2)
        PT = A(768).rearrange("p (j n) -> p j n", j=2)
        AM = IQ[:, 0:1024]
        AM2 = A(256)
        T4 = [DE[:, 0:288], DE[:, 0:0]]
        RT = SS.rearrange("p j n -> p (j n)")
        GL = A(256)
        IQv = IQ.rearrange("p (t h d) -> p t h d", t=2, h=9)
        QA = xn[:, :, :].rearrange("p t (h d) -> p t h d", h=8)
        QKE = big[:, :].rearrange("p (l j n) -> p l j n", l=8, j=2)
        zero = pool(lambda e: e.memset(big[:, :], 0.0))

        tn = norm_T("g_mix0", [TX])

        slot, w, tk = load()
        cp = []
        for tt, (b, t) in enumerate(proj_tok(w, tk, slot, tn)):
            u = act(lambda e, tt=tt, b=b: e.activation(IQ[:, tt * 576:tt * 576 + 512], b.t[:, :], ACT.Copy), t)
            b.free = [u]
            cp.append(u)
        slot, w, tk = load()
        IW = small[:, 16:32]
        for tt, (b, t) in enumerate(proj_tok(w, tk, slot, tn, n=72, last=False)):
            u = act(lambda e, tt=tt, b=b: e.activation(IQ[:, tt * 576 + 512:tt * 576 + 576], b.t[:, 0:64], ACT.Copy), t)
            v = act(lambda e, tt=tt, b=b: e.activation(IW[:, tt * 8:tt * 8 + 8], b.t[:, 64:72], ACT.Copy,
                                                       scale=8.0 ** -0.5), t)
            b.free = [u, v]
            cp += [u]
        tiw = v
        b = take()
        wv = w.rearrange("p (k n) -> p k n", k=8)
        for k in range(8):
            t = mm(b.t[0:16, 0:256], wv[:, k, 72:88], nTa[:, k, :], k == 0, k == 7, [tk] + tn + b.free, inc=(k == 7))
        slot.free = [t]
        tgl = act(lambda e, b=b: e.activation(GL[0:16, :], b.t[0:16, 0:256], ACT.Copy), t)
        b.free = [tgl]
        slot, w, tk = load()
        wv = w.rearrange("p (k n) -> p k n", k=8)
        tqk = []
        for j in range(2):
            b = take()
            for p in range(2):
                c = (j * 2 + p) * P
                for k in range(8):
                    t = mm(b.t[:, p * 256:p * 256 + 256], wv[:, k, c:c + P], nTa[:, k, :], k == 0, k == 7,
                           [tk] + tn + b.free, inc=(k == 7))
            u = act(lambda e, b=b, j=j: e.activation(QK0[:, j, :], b.t[:, :], ACT.Copy, scale=0.125 if j == 0 else 1.0), t)
            b.free = [u]
            tqk.append(u)
        slot.free = [t]
        b = take()
        for p in range(2):
            t = mm(b.t[:, p * 256:p * 256 + 256], wg[:, p * P:p * P + P], GL[0:16, :], True, True,
                   [tgl, TC] + b.free, inc=True)
        us = []
        for p in range(2):
            us.append(act(lambda e, p=p, b=b: e.activation(BB[:, p * 256:p * 256 + 256], b.t[:, p * 256:p * 256 + 256],
                                                           ACT.Identity, bias=vcol("b_gate", p)), t))
        b.free = us
        u = act(lambda e: e.activation(DE, BB, ACT.Abs), *us)
        u = act(lambda e: e.activation(DE, DE, ACT.Exp, scale=-1.0), u)
        u = act(lambda e: e.activation(DE, DE, ACT.Ln, bias=1.0), u)
        u = dve(lambda e: e.scalar_tensor_tensor(out=DE, in0=BB, scalar=0.0, in1=DE, op0=ALU.min, op1=ALU.subtract), u)
        tb = []
        for p in range(2):
            tb.append(dve(lambda e, p=p: e.tensor_tensor_scan(
                BB[:, p * 256:p * 256 + 256], DE[:, p * 256:p * 256 + 256], DE[:, p * 256:p * 256 + 256], 0.0,
                ALU.add, ALU.bypass), u))

        def rope(view, H, half, cname, sname, ready):
            cs = bc(const(cname).rearrange("p (t o n) -> p t o n", t=2, o=1), [P, 2, H, half])
            sn = bc(const(sname).rearrange("p (t o n) -> p t o n", t=2, o=1), [P, 2, H, half])
            n = 2 * H * half
            tmp = [RT[:, i * 256:i * 256 + n].rearrange("p (t h n) -> p t h n", t=2, h=H) if n <= 256 else None
                   for i in range(4)]
            x1 = view[:, :, :, 0:half]
            x2 = view[:, :, :, half:2 * half]
            a = dve(lambda e: e.tensor_tensor(tmp[0], x1, cs, ALU.mult), *ready)
            b_ = dve(lambda e: e.tensor_tensor(tmp[1], x2, sn, ALU.mult), *ready)
            c_ = dve(lambda e: e.tensor_tensor(tmp[2], x2, cs, ALU.mult), *ready)
            d_ = dve(lambda e: e.tensor_tensor(tmp[3], x1, sn, ALU.mult), *ready)
            f = dve(lambda e: e.tensor_tensor(x1, tmp[0], tmp[1], ALU.subtract), a, b_, d_)
            g = dve(lambda e: e.tensor_tensor(x2, tmp[2], tmp[3], ALU.add), c_, d_)
            return [f, g]

        tro = rope(IQv, 9, 8, "cosI", "sinI", cp + [TC])
        tik = []
        for tt in range(2):
            for j in range(2):
                tik.append(dve(lambda e, tt=tt, j=j: e.tensor_copy(IKD[:, tt * P + j * 64:tt * P + j * 64 + 64],
                                                                   IQ[:, tt * 576 + 512:tt * 576 + 576]), *tro))

        qa_ready = []
        ssA = small[:, 32:48].rearrange("p (j t h) -> p j t h", j=2, t=2)
        for j, grow in enumerate(("gq_row", "gk_row")):
            slot, w, tk = load()
            for tt, (b, t) in enumerate(proj_tok(w, tk, slot, tn)):
                q = QA[:, tt, 4 * j:4 * j + 4, :]
                a = act(lambda e, q=q, b=b: e.activation(q, b.t[:, :].rearrange("p (h d) -> p h d", h=4), ACT.Square), t)
                sq = ssA[:, j, tt, :]
                u = dve(lambda e, q=q, sq=sq: e.tensor_reduce(sq, q, AX.X, ALU.add), a)
                u = inv_rms(sq, sq, P, u)
                u = dve(lambda e, q=q, sq=sq, b=b: e.tensor_tensor(
                    q, b.t[:, :].rearrange("p (h d) -> p h d", h=4),
                    bc(sq.rearrange("p (h o) -> p h o", o=1), [P, 4, P]), ALU.mult), u)
                b.free = [u]
                g = VEC[grow][0]
                u = dve(lambda e, q=q, g=g: e.tensor_tensor(
                    q, q, bc(vec[:, g:g + P].rearrange("p (o d) -> p o d", o=1), [P, 4, P]), ALU.mult), u)
                qa_ready.append(u)
            if j == 0:
                tiq = []
                for tt in range(2):
                    b = take()
                    for m in range(4):
                        t = tr(b.t[:, m * P:m * P + P], IQ[:, tt * 576 + m * P:tt * 576 + m * P + P], ident,
                               tro + b.free, inc=(m == 3))
                    u = act(lambda e, tt=tt, b=b: e.activation(IQT[:, :, tt * P:tt * P + P],
                                                               b.t[:, :].rearrange("p (m t) -> p m t", m=4), ACT.Copy), t)
                    b.free = [u]
                    tiq.append(u)
                b = take()
                for tt in range(2):
                    t = tr(b.t[:, tt * P:tt * P + P], IKD[:, tt * P:tt * P + P], ident, tik + b.free, inc=(tt == 1))
                u = act(lambda e, b=b: e.activation(IKT, b.t[:, 0:256], ACT.Copy), t)
                b.free = [u]
                tiq.append(u)
        tqr = rope(QA, 8, 16, "cosA", "sinA", qa_ready + [TC])

        tsc = None
        rl_free = [[], []]
        n = 0
        for tt in range(2):
            for m2, e2 in ((0, 0), (0, 1), (1, 0), (1, 1)):
                b = take()
                for j in range(2):
                    t = mm(b.t[:, j * 256:j * 256 + 256], IQT[e2 * 64:e2 * 64 + 64, 2 * m2 + j, tt * P:tt * P + P],
                           IKT[e2 * 64:e2 * 64 + 64, :], True, True, tiq + b.free, inc=(j == 1))
                rl = RL[:, n % 2, :]
                a = act(lambda e, rl=rl, b=b: e.activation(rl, b.t[:, :], ACT.Relu, scale=0.125), t, *rl_free[n % 2])
                b.free = [a]
                for j in range(2):
                    hd = 2 * (2 * m2 + j) + e2
                    acc = SC[:, tt, :]
                    o = CST["inval"][0] + tt * 256
                    in1 = cst[:, o:o + 256] if hd == 0 else acc
                    tsc = dve(lambda e, rl=rl, j=j, tt=tt, hd=hd, in1=in1, acc=acc: e.scalar_tensor_tensor(
                        out=acc, in0=rl[:, j * 256:j * 256 + 256], scalar=IW[:, tt * 8 + hd:tt * 8 + hd + 1],
                        in1=in1, op0=ALU.mult, op1=ALU.add), a, tiw, TC, *([tsc] if tsc else []))
                rl_free[n % 2] = [tsc]
                n += 1
        tsel = [pool(lambda e: e.memset(SEL[:, P:256], BIGNEG))]
        for tt in range(2):
            wd = P * (tt + 1)
            wk = SC[:, tt, 0:wd]
            u = tsc
            for r in range(8):
                m8 = small[:, 48 + 8 * r:56 + 8 * r]
                u = dve(lambda e, wk=wk, m8=m8: e.max(m8, wk), u)
                u = dve(lambda e, wk=wk, m8=m8: e.match_replace(wk, m8, wk, -3.0e38), u)
            tsel.append(dve(lambda e, wk=wk, tt=tt, wd=wd: e.tensor_scalar(SELv[:, tt, 0:wd], wk, -2.0e38, BIGNEG,
                                                                          ALU.is_gt, ALU.mult), u))

        tva = []
        slot, w, tk = load()
        for tt, (b, t) in enumerate(proj_tok(w, tk, slot, tn)):
            u = act(lambda e, tt=tt, b=b: e.activation(VA[:, tt, :], b.t[:, :], ACT.Copy), t)
            b.free = [u]
            tva.append(u)
        tvb = []
        slot, w, tk = load()
        for tt, (b, t) in enumerate(proj_tok(w, tk, slot, tn)):
            u = act(lambda e, tt=tt, b=b: e.activation(VB[:, tt, :], b.t[:, :], ACT.Copy), t)
            b.free = [u]
            tvb.append(u)
        tog = []
        slot, w, tk = load()
        for tt, (b, t) in enumerate(proj_tok(w, tk, slot, tn)):
            g = OG[:, tt, :]
            u = act(lambda e, g=g, b=b: e.activation(g, b.t[:, :], ACT.Exp, scale=-1.0), t)
            u = dve(lambda e, g=g: e.tensor_scalar(g, g, 1.0, None, ALU.add), u)
            u = dve(lambda e, g=g: e.reciprocal(g, g), u)
            u = dve(lambda e, g=g, b=b: e.tensor_tensor(g, g, b.t[:, :], ALU.mult), u)
            b.free = [u]
            tog.append(u)

        tlev = []
        tprev = []
        for l, hs in enumerate((128, 64, 32, 16, 8, 4, 2, 1)):
            nb = 256 // hs
            bv = BB.rearrange("p (b u s) -> p b u s", u=2, s=hs)
            dv = DE.rearrange("p (b u s) -> p b u s", u=2, s=hs)
            mid = bc(bv[:, :, 0, hs - 1:hs], [P, nb, hs])
            u1 = dve(lambda e, bv=bv, dv=dv, mid=mid: e.tensor_tensor(dv[:, :, 1, :], bv[:, :, 1, :], mid, ALU.subtract),
                     *tb, *tprev)
            u2 = dve(lambda e, bv=bv, dv=dv, mid=mid: e.tensor_tensor(dv[:, :, 0, :], mid, bv[:, :, 0, :], ALU.subtract),
                     *tb, *tprev)
            a = act(lambda e: e.activation(DE, DE, ACT.Exp, scale=1.0 / 16.0), u1, u2)
            tl = []
            for j, side in ((0, 1), (1, 0)):
                ov = QKE[:, l, j, :].rearrange("p (b u s) -> p b u s", u=2, s=hs)[:, :, side, :]
                iv = QK0[:, j, :].rearrange("p (b u s) -> p b u s", u=2, s=hs)[:, :, side, :]
                tl.append(dve(lambda e, ov=ov, iv=iv, dv=dv, side=side: e.tensor_tensor(ov, iv, dv[:, :, side, :], ALU.mult),
                              a, zero, *tqk))
            tprev = tl
            tlev.append(tl)

        tq = []
        for tt in range(2):
            for j in range(2):
                b = take()
                for hd in range(4):
                    t = tr(b.t[:, hd * P:hd * P + P], QA[:, tt, 4 * j + hd, :], ident, tqr + b.free, inc=(hd == 3))
                u = act(lambda e, b=b, j=j, tt=tt: e.activation(QKT[:, 4 * j:4 * j + 4, tt * P:tt * P + P],
                                                                b.t[:, :].rearrange("p (m t) -> p m t", m=4), ACT.Copy), t)
                b.free = [u]
                tq.append(u)

        tcat = []
        am_free = [[], []]
        AMs = [AM, None]
        gm = const("gmask")
        ob_bank = []
        tob = []
        for tt in range(2):
            ob = take(hold=True)
            for hd in range(4):
                p, e2 = hd // 2, hd % 2
                lo = e2 * 64
                tm = []
                for half in range(2):
                    b = take()
                    for i in range(4):
                        l = half * 4 + i + 1
                        src = QKE[:, l] if l < 8 else QK0
                        kx = src[lo:lo + 64, 1, p * 256 + tt * P:p * 256 + tt * P + P]
                        qx = src[lo:lo + 64, 0, p * 256 + tt * P:p * 256 + tt * P + P]
                        t = mm(b.t[:, i * P:i * P + P], kx, qx, True, True,
                               (tlev[l] if l < 8 else tqk) + [zero] + b.free, inc=(i == 3))
                    o = AM[:, half * 512:half * 512 + 512]
                    u = dve(lambda e, o=o, b=b, half=half: e.tensor_tensor(o, b.t[:, :], gm[:, half * 512:half * 512 + 512],
                                                                          ALU.mult), t, *am_free[0])
                    b.free = [u]
                    tm.append(u)
                if tt == 1:
                    b = take()
                    t = mm(b.t[:, 0:P], QKE[lo:lo + 64, 0, 1, p * 256:p * 256 + P],
                           QKE[lo:lo + 64, 0, 0, p * 256 + P:p * 256 + 256], True, True, tlev[0] + [zero] + b.free, inc=True)
                    u = act(lambda e, b=b: e.activation(AM2[:, 0:P], b.t[:, 0:P], ACT.Copy), t, *am_free[1])
                    b.free = [u]
                    tm.append(u)
                oo = ob.t[:, hd * P:hd * P + P]
                for i in range(8):
                    t = mm(oo, AM[:, i * P:i * P + P], VB[:, tt, hd * P:hd * P + P], i == 0, i == 7 and tt == 0,
                           tm + tvb + ob.free, inc=(i == 7))
                if tt == 1:
                    t = mm(oo, AM2[:, 0:P], VB[:, 0, hd * P:hd * P + P], False, True, [], inc=True)
                am_free = [[t], [t]]
            obv = ob.t[:, :].rearrange("p (h d) -> p h d", h=4)
            y = SS[:, tt, :]
            yv = y.rearrange("p (h d) -> p h d", h=4)
            a = act(lambda e, y=y, ob=ob: e.activation(y, ob.t[:, :], ACT.Square), t)
            ss = small[:, 112 + 4 * tt:116 + 4 * tt]
            u = dve(lambda e, ss=ss, yv=yv: e.tensor_reduce(ss, yv, AX.X, ALU.add), a)
            u = inv_rms(ss, ss, P, u)
            u = dve(lambda e, ss=ss, yv=yv, obv=obv: e.tensor_tensor(
                yv, obv, bc(ss.rearrange("p (h o) -> p h o", o=1), [P, 4, P]), ALU.mult), u)
            ob.free = [u]
            ob.held = False
            u = dve(lambda e, y=y, tt=tt: e.tensor_tensor(y, y, OG[:, tt, :], ALU.mult), u, tog[tt])
            b = take()
            for hd in range(4):
                t = tr(b.t[:, hd * P:hd * P + P], SS[:, tt, hd * P:hd * P + P], ident, [u] + b.free, inc=(hd == 3))
            u = act(lambda e, b=b, tt=tt: e.activation(catT[:, 4:8, tt * P:tt * P + P],
                                                       b.t[:, :].rearrange("p (m t) -> p m t", m=4), ACT.Copy,
                                                       scale=vcol("g_gla")), t)
            b.free = [u]
            tob += [u]

        scale = float(P) ** -0.5
        toa = []
        ss_free = [[u], [u]]
        pt_free = [[], []]
        for hd in range(4):
            b = take()
            for tt in range(2):
                t = mm(b.t[:, tt * 256:tt * 256 + 256], QKT[:, hd, tt * P:tt * P + P], QKT[:, 4 + hd, :], True, True,
                       tq + b.free, inc=(tt == 1))
            y = SS[:, hd % 2, :]
            yv = y.rearrange("p (t n) -> p t n", t=2)
            mx = small[:, 128 + 2 * hd:130 + 2 * hd]
            sm = small[:, 136 + 2 * hd:138 + 2 * hd]
            u = dve(lambda e, y=y, b=b: e.tensor_tensor(y, b.t[:, :], SEL, ALU.add), t, *tsel, *ss_free[hd % 2])
            b.free = [u]
            u = dve(lambda e, mx=mx, yv=yv: e.tensor_reduce(mx, yv, AX.X, ALU.max), u)
            u = dve(lambda e, mx=mx: e.tensor_scalar(mx, mx, -scale, None, ALU.mult), u)
            us = []
            for tt in range(2):
                us.append(act(lambda e, yv=yv, tt=tt, mx=mx, sm=sm: e.activation(
                    yv[:, tt, :], yv[:, tt, :], ACT.Exp, bias=mx[:, tt:tt + 1], scale=scale,
                    accum_out=sm[:, tt:tt + 1]), u))
            u = dve(lambda e, sm=sm: e.reciprocal(sm, sm), *us)
            u = dve(lambda e, sm=sm, yv=yv: e.tensor_tensor(yv, yv, bc(sm.rearrange("p (t o) -> p t o", o=1), [P, 2, 256]),
                                                            ALU.mult), u)
            b = take()
            for i, (tt, kb) in enumerate(((0, 0), (1, 0), (1, 1))):
                t = tr(b.t[:, i * P:i * P + P], yv[:, tt, kb * P:kb * P + P], ident, [u] + b.free, inc=(i == 2))
            ss_free[hd % 2] = [t]
            pt = PT[:, hd % 2, :]
            u = act(lambda e, pt=pt, b=b: e.activation(pt, b.t[:, 0:384], ACT.Copy), t, *pt_free[hd % 2])
            b.free = [u]
            b = take()
            t = mm(b.t[:, 0:256], VA[:, 0, hd * P:hd * P + P], pt[:, 0:256], True, False, [u] + tva + b.free)
            t = mm(b.t[:, P:256], VA[:, 1, hd * P:hd * P + P], pt[:, 256:384], False, True, [], inc=True)
            pt_free[hd % 2] = [t]
            u = act(lambda e, b=b, hd=hd: e.activation(catT[:, hd, :], b.t[:, 0:256], ACT.Copy), t)
            b.free = [u]
            toa.append(u)

        th = out_tok(lambda k: catT[:, k, :], 2, 4, lambda k: [toa[k]] if k < 4 else tob)
        th = mlp("g_ffn0", th)

        A = Area()
        QT = A(2048).rearrange("p (k t) -> p k t", k=8)
        KT = A(2048).rearrange("p (k t) -> p k t", k=8)
        VC = A(2048).rearrange("p (t n) -> p t n", t=2)
        QN = A(1024).rearrange("p (j n) -> p j n", j=2)
        ZB = [[A(384) for _ in range(4)] for _ in range(2)]
        tn = norm_T("g_mix1", th)
        gs = small[:, 144:145]
        tgs = dve(lambda e: e.tensor_scalar(gs, vcol("gq_c"), float(P) ** -0.5, None, ALU.mult), TC)
        tqk = [[], []]
        qn_free = [[], []]
        n = 0
        for j in range(2):
            for half in range(2):
                slot, w, tk = load()
                for tt, (b, t) in enumerate(proj_tok(w, tk, slot, tn)):
                    q = QN[:, n % 2, :]
                    qv = q.rearrange("p (h d) -> p h d", h=4)
                    ss = small[:, 148 + 4 * n:152 + 4 * n]
                    a = act(lambda e, q=q, b=b: e.activation(q, b.t[:, :], ACT.Square), t, *qn_free[n % 2])
                    u = dve(lambda e, qv=qv, ss=ss: e.tensor_reduce(ss, qv, AX.X, ALU.add), a)
                    u = inv_rms(ss, ss, P, u)
                    u = dve(lambda e, qv=qv, ss=ss, b=b: e.tensor_tensor(
                        qv, b.t[:, :].rearrange("p (h d) -> p h d", h=4),
                        bc(ss.rearrange("p (h o) -> p h o", o=1), [P, 4, P]), ALU.mult), u)
                    b.free = [u]
                    b = take()
                    for hd in range(4):
                        t = tr(b.t[:, hd * P:hd * P + P], q[:, hd * P:hd * P + P], ident, [u] + b.free, inc=(hd == 3))
                    qn_free[n % 2] = [t]
                    dst = (QT, KT)[j][:, half * 4:half * 4 + 4, tt * P:tt * P + P]
                    g = gs if j == 0 else vcol("gk_c")
                    u = act(lambda e, dst=dst, b=b, g=g: e.activation(
                        dst, b.t[:, :].rearrange("p (m t) -> p m t", m=4), ACT.Copy, scale=g), t, tgs)
                    b.free = [u]
                    tqk[half].append(u)
                    n += 1
        tv = [[], []]
        for half in range(2):
            slot, w, tk = load()
            for tt, (b, t) in enumerate(proj_tok(w, tk, slot, tn)):
                u = act(lambda e, tt=tt, b=b, half=half: e.activation(VC[:, tt, half * 512:half * 512 + 512], b.t[:, :],
                                                                      ACT.Copy), t)
                b.free = [u]
                tv[half].append(u)
        sm = const("smask")
        ones = const("ones")
        z_free = [[], []]
        tc_ = []
        for hd in range(8):
            half = hd // 4
            Z, E1, LL, AA = ZB[hd % 2]
            b = take()
            t = mm(b.t[:, 0:256], KT[:, hd, 0:P], QT[:, hd, :], True, True, tqk[half] + b.free)
            t = mm(b.t[:, 256:384], KT[:, hd, P:256], QT[:, hd, P:256], True, True, [], inc=True)
            uz = dve(lambda e, Z=Z, b=b: e.tensor_tensor(Z, b.t[:, 0:384], sm, ALU.add), t, *z_free[hd % 2])
            b.free = [uz]
            u = act(lambda e, Z=Z, E1=E1: e.activation(E1, Z, ACT.Abs), uz)
            u = act(lambda e, E1=E1: e.activation(E1, E1, ACT.Exp, scale=-1.0), u)
            ul = act(lambda e, E1=E1: e.activation(E1, E1, ACT.Ln, bias=1.0), u)
            u1 = dve(lambda e, Z=Z, E1=E1, LL=LL: e.scalar_tensor_tensor(out=LL, in0=Z, scalar=0.0, in1=E1, op0=ALU.max,
                                                                        op1=ALU.add), ul)
            u2 = dve(lambda e, Z=Z, E1=E1, AA=AA: e.scalar_tensor_tensor(out=AA, in0=Z, scalar=0.0, in1=E1, op0=ALU.min,
                                                                        op1=ALU.subtract), ul)
            b = take()
            t = mm(b.t[:, 0:256], tri[:, :], LL[:, 0:256], True, False, [u1, TC] + b.free)
            t = mm(b.t[:, P:256], ones, LL[:, 256:384], False, True, [])
            t = mm(b.t[:, 256:384], tri[:, :], LL[:, 256:384], True, True, [], inc=True)
            u = dve(lambda e, AA=AA, b=b: e.tensor_tensor(AA, AA, b.t[:, 0:384], ALU.subtract), t, u2)
            b.free = [u]
            u = act(lambda e, AA=AA: e.activation(AA, AA, ACT.Exp), u)
            b = take()
            t = mm(b.t[:, 0:256], VC[:, 0, hd * P:hd * P + P], AA[:, 0:256], True, False, [u] + tv[half] + b.free)
            t = mm(b.t[:, P:256], VC[:, 1, hd * P:hd * P + P], AA[:, 256:384], False, True, [], inc=True)
            z_free[hd % 2] = [t]
            u = act(lambda e, b=b, hd=hd: e.activation(catT[:, hd, :], b.t[:, 0:256], ACT.Copy), t)
            b.free = [u]
            tc_.append(u)
        th = out_tok(lambda k: catT[:, k, :], 2, 4, lambda k: [tc_[k]])
        th = mlp("g_ffn1", th)

        A = Area()
        HT = A(8 * L2).rearrange("p (k t) -> p k t", k=8)
        SQ = A(2 * L2).rearrange("p (j t) -> p j t", j=2)
        RS = A(L2)
        UT = A(4 * L2).rearrange("p (k t) -> p k t", k=4)
        GT = A(16 * N2).rearrange("p (k t) -> p k t", k=16)
        CG = A(4 * N2).rearrange("p (k t) -> p k t", k=4)
        FT = A(4 * N2).rearrange("p (k t) -> p k t", k=4)
        CV = xn[:, :, :].rearrange("p t n -> p (t n)")[:, 0:4 * N2].rearrange("p (k t) -> p k t", k=4)
        meta = big[0:META, 0:D]
        cm = big[0:META, D:D + 2 * L2]
        P1 = big[:, 2048:2048 + 3 * 256].rearrange("p (t n) -> p t n", t=3)
        dma(lambda e: e.dma_start(meta, MT), th, s_g)
        dma(lambda e: e.dma_start(cm, CM), th, s_g)
        TM = (s_g, 32)
        t_ht = []
        for q in range(4):
            b = take()
            for kk in range(2):
                for tt in range(2):
                    t = tr(b.t[:, kk * 256 + tt * P:kk * 256 + tt * P + P], h[:, tt, (2 * q + kk) * P:(2 * q + kk + 1) * P],
                           ident, th + b.free, inc=(kk == 1 and tt == 1))
            u = act(lambda e, b=b, q=q: e.activation(HT[:, 2 * q:2 * q + 2, META:L2],
                                                     b.t[:, :].rearrange("p (k t) -> p k t", k=2), ACT.Copy), t)
            b.free = [u]
            t_ht.append(u)
        b = take()
        for k in range(8):
            t = tr(b.t[:, k * META:k * META + META], meta[:, k * P:k * P + P], ident[0:META, 0:META], [TM] + b.free,
                   inc=(k == 7))
        u = act(lambda e, b=b: e.activation(HT[:, :, 0:META], b.t[:, 0:P].rearrange("p (k t) -> p k t", k=8), ACT.Copy), t)
        b.free = [u]
        t_ht.append(u)

        sq_free = [[], []]

        def rms_cols(src, ready, w):
            b = take()
            for k in range(8):
                s2 = SQ[:, k % 2, 0:w]
                a = act(lambda e, s2=s2, k=k: e.activation(s2, src(k), ACT.Square), *ready, *sq_free[k % 2])
                t = mm(b.t[:, 0:w], ones, s2, k == 0, k == 7, [a, TC] + b.free, inc=True)
                sq_free[k % 2] = [t]
            u = act(lambda e, b=b: e.activation(RS[:, 0:w], b.t[:, 0:w], ACT.Ln, bias=eps, scale=1.0 / D), t, *ready)
            b.free = [u]
            return act(lambda e: e.activation(RS[:, 0:w], RS[:, 0:w], ACT.Exp, scale=-0.5), u)

        tr_ = rms_cols(lambda k: HT[:, k, :], t_ht, L2)
        tn = []
        for k in range(8):
            tn.append(dve(lambda e, k=k: e.scalar_tensor_tensor(out=nT2[:, k, :], in0=HT[:, k, :],
                                                               scalar=vcol("g_mix_pre", k), in1=RS, op0=ALU.mult,
                                                               op1=ALU.mult), tr_))

        def proj_feat(wv, c, ready, tk, c0, kn=8, rhs=None):
            b = take()
            for k in range(kn):
                r = nT2[:, k, c0:L2] if rhs is None else rhs(k)
                t = mm(b.t[:, 0:L2 - c0], wv[:, k, c:c + P], r, k == 0, k == kn - 1, [tk] + ready + b.free,
                       inc=(k == kn - 1))
            return b, t

        slot, w, tk = load()
        wv = w.rearrange("p (k n) -> p k n", k=8)
        tu = []
        for m in range(4):
            b, t = proj_feat(wv, m * P, tn, tk, 0)
            u = act(lambda e, b=b, m=m: e.activation(UT[:, m, :], b.t[:, 0:L2], ACT.Copy), t)
            b.free = [u]
            tu.append(u)
        slot.free = [t]
        slot, w, tk = load()
        wv = w.rearrange("p (k n) -> p k n", k=8)
        tcg = []
        for m in range(4):
            b, t = proj_feat(wv, m * P, tn, tk, X0)
            u = act(lambda e, b=b, m=m: e.activation(CG[:, m, :], b.t[:, 0:N2], ACT.Copy), t)
            b.free = [u]
            tcg.append(u)
        slot.free = [t]
        slot, w, tk = load()
        wv = w.rearrange("p (k n) -> p k n", k=8)
        tcv = []
        for m in range(4):
            b, t = proj_feat(wv, m * P, tn, tk, X0)
            u = dve(lambda e, b=b, m=m: e.tensor_tensor(CG[:, m, :], CG[:, m, :], b.t[:, 0:N2], ALU.mult), t, tcg[m])
            b.free = [u]
            u = act(lambda e, m=m: e.activation(CV[:, m, :], CG[:, m, :], ACT.Identity, bias=vcol("conv_b_mix", m),
                                                scale=vcol("conv_w_mix", 4 + m)), u)
            u = dve(lambda e, m=m: e.scalar_tensor_tensor(out=CV[:, m, 1:N2], in0=CG[:, m, 0:N2 - 1],
                                                          scalar=vcol("conv_w_mix", m), in1=CV[:, m, 1:N2],
                                                          op0=ALU.mult, op1=ALU.add), u)
            u = dve(lambda e, m=m: e.scalar_tensor_tensor(out=CV[:, m, 0:N2 - 1], in0=CG[:, m, 1:N2],
                                                          scalar=vcol("conv_w_mix", 8 + m), in1=CV[:, m, 0:N2 - 1],
                                                          op0=ALU.mult, op1=ALU.add), u)
            tcv.append(u)
        slot.free = [t]
        slot, w, tk = load()
        wv = w.rearrange("p (k n) -> p k n", k=8)
        tyb = []
        for m in range(4):
            b, t = proj_feat(wv, m * P, tn, tk, X0)
            u = dve(lambda e, b=b, m=m: e.tensor_tensor(CV[:, m, :], CV[:, m, :], b.t[:, 0:N2], ALU.mult), t, tcv[m])
            b.free = [u]
            tyb.append(u)
        slot.free = [t]
        tgt = []
        nbg = small[:, 0:16]
        tnb = dve(lambda e: e.tensor_scalar(nbg, vcol("b_gates", 0, 16), -1.0, None, ALU.mult), TC)
        for i in range(4):
            slot, w, tk = load()
            wv = w.rearrange("p (k n) -> p k n", k=8)
            for m in range(4):
                g = i * 4 + m
                b, t = proj_feat(wv, m * P, tn, tk, X0)
                u = act(lambda e, b=b, g=g: e.activation(GT[:, g, :], b.t[:, 0:N2], ACT.Exp, bias=nbg[:, g:g + 1],
                                                         scale=-1.0), t, tnb)
                b.free = [u]
                u = dve(lambda e, g=g: e.tensor_scalar(GT[:, g, :], GT[:, g, :], 1.0, None, ALU.add), u)
                tgt.append(dve(lambda e, g=g: e.reciprocal(GT[:, g, :], GT[:, g, :]), u))
            slot.free = [t]
        dftc = const("dftc")
        o = CST["dftl"][0]
        dl = cst[:, o:o + 1088].rearrange("p (t j l) -> p t j l", t=2, j=2)
        cmv = cm.rearrange("p (j l) -> p j l", j=2)
        p1_free = []
        tft = []
        for g in range(4):
            us = []
            for i, (c, n) in enumerate(((META, P), (META + P, P), (0, META))):
                b = take()
                t = mm(b.t[0:n, 0:256], UT[:, g, c:c + n], dftc, True, True, [tu[g], TC] + b.free, inc=True)
                u = act(lambda e, b=b, n=n, i=i: e.activation(P1[0:n, i, :], b.t[0:n, 0:256], ACT.Copy), t, *p1_free)
                b.free = [u]
                us.append(u)
            b = take()
            n = 0
            for i in range(3):
                for j in range(2):
                    kp = P if i < 2 else META
                    rhs = dl[:, i, j, X0:L2] if i < 2 else cmv[:, j, X0:L2]
                    t = mm(b.t[:, 0:N2], P1[0:kp, i, j * P:j * P + P], rhs, n == 0, n == 5, us + [TM] + b.free,
                           inc=(n == 5))
                    n += 1
            p1_free = [t]
            u = act(lambda e, b=b, g=g: e.activation(FT[:, g, :], b.t[:, 0:N2], ACT.Copy), t)
            b.free = [u]
            tft.append(u)
        slot, w, tk = load()
        wv = w.rearrange("p (k n) -> p k n", k=4)
        tga = []
        for m in range(8):
            b, t = proj_feat(wv, m * P, tft, tk, X0, 4, lambda k: FT[:, k, :])
            u = dve(lambda e, b=b, m=m: e.tensor_tensor(GT[:, m, :], GT[:, m, :], b.t[:, 0:N2], ALU.mult), t, tgt[m])
            b.free = [u]
            tga.append(u)
        slot.free = [t]
        slot, w, tk = load()
        wv = w.rearrange("p (k n) -> p k n", k=4)
        tmg = []
        for m in range(8):
            b, t = proj_feat(wv, m * P, tyb, tk, X0, 4, lambda k: CV[:, k, :])
            u = dve(lambda e, b=b, m=m: e.tensor_tensor(GT[:, 8 + m, :], GT[:, 8 + m, :], b.t[:, 0:N2], ALU.mult), t,
                    tgt[8 + m])
            b.free = [u]
            tmg.append(dve(lambda e, m=m: e.tensor_tensor(GT[:, m, :], GT[:, m, :], GT[:, 8 + m, :], ALU.add), u, tga[m]))
        slot.free = [t]
        tmx = []
        for i in range(2):
            slot, w, tk = load()
            wv = w.rearrange("p (k n) -> p k n", k=8)
            for m in range(4):
                b, t = proj_feat(wv, m * P, tmg, tk, X0, 8, lambda k: GT[:, k, :])
                u = act(lambda e, b=b, g=i * 4 + m: e.activation(GT[:, 8 + g, :], b.t[:, 0:N2], ACT.Copy), t)
                b.free = [u]
                tmx.append(u)
            slot.free = [t]
        tr_ = rms_cols(lambda k: GT[:, 8 + k, :], tmx, N2)
        th2 = []
        for k in range(8):
            u = dve(lambda e, k=k: e.scalar_tensor_tensor(out=GT[:, 8 + k, :], in0=GT[:, 8 + k, :],
                                                          scalar=vcol("g_mix_post", k), in1=RS[:, 0:N2], op0=ALU.mult,
                                                          op1=ALU.mult), tr_)
            th2.append(dve(lambda e, k=k: e.tensor_tensor(HT[:, k, X0:L2], HT[:, k, X0:L2], GT[:, 8 + k, :], ALU.add), u))
        tr_ = rms_cols(lambda k: HT[:, k, X0:L2], th2, N2)
        tn = []
        for k in range(8):
            tn.append(dve(lambda e, k=k: e.scalar_tensor_tensor(out=nT2[:, k, X0:L2], in0=HT[:, k, X0:L2],
                                                               scalar=vcol("g_ffn_pre", k), in1=RS[:, 0:N2],
                                                               op0=ALU.mult, op1=ALU.mult), tr_))
        t_h = []
        for tt in range(2):
            for c in range(2):
                b = take()
                for m in range(4):
                    t = tr(b.t[:, m * P:m * P + P], HT[:, c * 4 + m, META + tt * P:META + tt * P + P], ident,
                           th2 + b.free, inc=(m == 3))
                u = act(lambda e, b=b, tt=tt, c=c: e.activation(h[:, tt, c * 512:c * 512 + 512], b.t[:, :], ACT.Copy), t)
                b.free = [u]
                t_h.append(u)
        ff = big[:, 0:22 * S].rearrange("p (k t) -> p k t", k=22)
        UPB = [[GT[:, 2 * j + i, 0:S] for i in range(2)] for j in range(4)]
        up_free = [[] for _ in range(4)]
        tf = []
        for i in range(11):
            slot, w, tk = load()
            wv = w.rearrange("p (k n) -> p k n", k=8)
            for m in range(2):
                n = 2 * i + m
                bufs = UPB[n % 4]
                us = []
                for av in range(2):
                    b, t = proj_feat(wv, av * 256 + m * P, tn, tk, X0)
                    ch = av * 22 + n
                    o = bufs[av]
                    u = act(lambda e, b=b, ch=ch, o=o: e.activation(o, b.t[:, 2:N2], ACT.Identity,
                                                                    bias=vcol("conv_b_ffn", ch),
                                                                    scale=vcol("conv_w_ffn", 44 + ch)), t, *up_free[n % 4])
                    u = dve(lambda e, b=b, ch=ch, o=o: e.scalar_tensor_tensor(
                        out=o, in0=b.t[:, 1:N2 - 1], scalar=vcol("conv_w_ffn", ch), in1=o, op0=ALU.mult, op1=ALU.add), u)
                    u = dve(lambda e, b=b, ch=ch, o=o: e.scalar_tensor_tensor(
                        out=o[:, 0:S - 1], in0=b.t[:, 3:N2], scalar=vcol("conv_w_ffn", 88 + ch), in1=o[:, 0:S - 1],
                        op0=ALU.mult, op1=ALU.add), u)
                    b.free = [u]
                    us.append(u)
                a = act(lambda e, o=bufs[0]: e.activation(o, o, ACT.Gelu_apprx_tanh), us[0])
                u = dve(lambda e, o=bufs, n=n: e.tensor_tensor(ff[:, n, :], o[0], o[1], ALU.mult), a, us[1])
                up_free[n % 4] = [u]
                tf.append(u)
            slot.free = [t]
        gp = HT.rearrange("p k t -> p (k t)")[:, 0:D]
        s_gp = sem("s_gp")
        dma(lambda e: e.dma_start(gp, GP), t_h + tn, s_gp)
        bs = [take() for _ in range(4)]
        for i in range(6):
            slot, w, tk = load()
            wv = w.rearrange("p (k n) -> p k n", n=D)
            for kk in range(wv.shape[1]):
                k = i * 4 + kk
                for j in range(4):
                    tt, c = j // 2, j % 2
                    t = mm(bs[j].t[:, :], ff[:, k, tt * P:tt * P + P], wv[:, kk, c * 512:c * 512 + 512], k == 0, k == 21,
                           [tk, tf[k]] + bs[j].free, inc=(kk == wv.shape[1] - 1))
            slot.free = [t]
        for tt in range(2):
            us = []
            for c in range(2):
                us.append(act(lambda e, tt=tt, c=c: e.activation(xn[:, tt, c * 512:c * 512 + 512], bs[2 * tt + c].t[:, :],
                                                                 ACT.Square, accum_out=small[:, 240 + 2 * tt + c:241 + 2 * tt + c]), t))
            u = dve(lambda e, tt=tt: e.tensor_tensor(small[:, 244 + tt:245 + tt], small[:, 240 + 2 * tt:241 + 2 * tt],
                                                     small[:, 241 + 2 * tt:242 + 2 * tt], ALU.add), *us)
            rs = small[:, 246 + tt:247 + tt]
            u = inv_rms(small[:, 244 + tt:245 + tt], rs, D, u)
            for c in range(2):
                o = xn[:, tt, c * 512:c * 512 + 512]
                v = dve(lambda e, tt=tt, c=c, o=o, rs=rs: e.scalar_tensor_tensor(
                    out=o, in0=bs[2 * tt + c].t[:, :], scalar=rs, in1=gp[:, c * 512:c * 512 + 512], op0=ALU.mult,
                    op1=ALU.mult), u, (s_gp, 16))
                v = dve(lambda e, tt=tt, c=c, o=o: e.tensor_tensor(o, o, h[:, tt, c * 512:c * 512 + 512], ALU.add), v, *t_h)
                dma(lambda e, tt=tt, c=c, o=o: e.dma_start(OUT[tt * P:tt * P + P, c * 512:c * 512 + 512], o), [v], s_o)
        assert tile_at[0] == len(sizes)

        def run(eng, name):
            seen = {}
            for waits, fn, inc in queues[name]:
                need = {}
                for tok in waits:
                    s, v = tok
                    need[id(s)] = (s, max(v, need.get(id(s), (s, 0))[1]))
                for key, (s, v) in need.items():
                    if seen.get(key, 0) < v:
                        eng.wait_ge(s, v)
                        seen[key] = v
                ins = fn(eng)
                if inc:
                    ins.then_inc(*inc)

        block = ctx.enter_context(nc.Block())

        @block.sync
        def _(eng):
            run(eng, "sp")
            eng.wait_ge(s_o, 64)

        @block.scalar
        def _(eng):
            run(eng, "act")

        @block.vector
        def _(eng):
            run(eng, "dve")

        @block.gpsimd
        def _(eng):
            run(eng, "pool")

        @block.tensor
        def _(eng):
            run(eng, "pe")


def weight_stream(a):
    out = []

    def kn(w, k0=0, k1=None):
        n = w.shape[1]
        return w.reshape(-1, P, n).transpose(1, 0, 2)

    def put(t):
        out.append(np.ascontiguousarray(t).reshape(-1))

    def cols(w, lo, hi):
        put(kn(w[:, lo:hi]))

    def rows(w, per=4):
        k = w.shape[0] // P
        for i in range(0, k, per):
            put(kn(w[i * P:min(i + per, k) * P]))

    w = a["w_in_ab"][0]
    cols(w, 1536, 2048)
    put(np.concatenate([kn(w[:, 2048:2120]), kn(w[:, 3144:3160])], axis=2))
    cols(w, 2120, 2632)
    cols(w, 0, 512)
    cols(w, 512, 1024)
    cols(w, 1024, 1536)
    cols(w, 2632, 3144)
    cols(w, 3160, 3672)
    rows(a["w_out_ab"][0])

    def mlp(l):
        for i in range(8):
            cols(a["w_up"][l], i * 512, i * 512 + 512)
        rows(a["w_down"][l])

    mlp(0)
    for i in range(6):
        cols(a["w_in_c"][0], i * 512, i * 512 + 512)
    rows(a["w_out_c"][0])
    mlp(1)
    w = a["w_in_2"][0]
    for c in (0, 512, 1536, 1024, 2048, 2560, 3072, 3584):
        cols(w, c, c + 512)
    rows(a["w_fourier_2"][0])
    rows(a["w_conv_out_2"][0])
    w = a["w_out_2"][0]
    cols(w, 0, 512)
    cols(w, 512, 1024)
    w = a["w_up_2"][0]
    for i in range(11):
        put(np.concatenate([kn(w[:, i * 256:i * 256 + 256]), kn(w[:, 2816 + i * 256:2816 + i * 256 + 256])], axis=2))
    rows(a["w_down_2"][0])
    return np.concatenate(out)


def vectors(a):
    v = np.zeros((P, NVEC), np.float32)

    def put(name, x):
        o, n = VEC[name]
        v[:, o:o + n] = np.asarray(x).reshape(-1, P).T

    for l in range(2):
        put(f"g_mix{l}", a["g_mix"][l])
        put(f"g_ffn{l}", a["g_ffn"][l])
    put("b_gate", a["b_gate"][0])
    put("g_gla", a["g_gla"][0])
    put("gq_c", a["gq_c"][0])
    put("gk_c", a["gk_c"][0])
    put("g_mix_pre", a["g_mix_pre_2"][0])
    put("b_gates", a["b_gates_2"][0])
    put("conv_w_mix", a["conv_w_mix_2"][0])
    put("conv_b_mix", a["conv_b_mix_2"][0])
    put("g_mix_post", a["g_mix_post_2"][0])
    put("g_ffn_pre", a["g_ffn_pre_2"][0])
    put("conv_w_ffn", a["conv_w_ffn_2"][0])
    put("conv_b_ffn", a["conv_b_ffn_2"][0])
    for name, key in (("gq_row", "gq_a"), ("gk_row", "gk_a")):
        o, n = VEC[name]
        v[:, o:o + n] = np.broadcast_to(a[key][0][None, :], (P, P))
    return v


def kernel(**inputs):
    import concourse.bacc as bacc
    from concourse.bass_utils import run_bass_kernel_spmd

    a = {k: np.asarray(v) for k, v in inputs.items()}
    c, cm, tri = constants()
    arrays = {
        "w_stream": weight_stream(a),
        "vectors": vectors(a),
        "consts": c,
        "consts_m": cm,
        "tri": tri,
        "x_rows": np.ascontiguousarray(a["x"][0]),
        "meta_rows": np.ascontiguousarray(a["meta_tokens_2"]),
        "gate_up": np.ascontiguousarray(a["w_gate_up"][0]),
        "g_post": np.ascontiguousarray(np.broadcast_to(a["g_ffn_post_2"][0][None, :], (P, D))),
    }
    nc = bacc.Bacc("TRN2", target_bir_lowering=False, num_devices=1)
    args = [nc.dram_tensor(k, v.shape, F32, kind="ExternalInput").ap() for k, v in arrays.items()]
    out = nc.dram_tensor("out_rows", (S, D), F32, kind="ExternalOutput").ap()
    block_kernel(nc, *args, out)
    r = run_bass_kernel_spmd(nc, [arrays], core_ids=[0])
    return r.results[0]["out_rows"].reshape(1, S, D)
```

```python
from contextlib import ExitStack

import numpy as np

import concourse.bass as bass
from concourse import mybir

ALU = mybir.AluOpType
ACT = mybir.ActivationFunctionType
AX = mybir.AxisListType
F32 = mybir.dt.float32
F32R = mybir.dt.float32r

P = 128
D = 1024
S = 256
EPS = 1e-6
META = 16
L2 = META + S
X0 = 14
N2 = L2 - X0
SLOT = 2048
NSLOT = 3
AHEAD = 2
BIGNEG = -1.0e30

VEC_COLS = [
    ("g_mix0", 8), ("g_ffn0", 8), ("g_mix1", 8), ("g_ffn1", 8), ("b_gate", 2), ("g_gla", 1),
    ("gq_c", 1), ("gk_c", 1), ("g_mix_pre", 8), ("b_gates", 16), ("conv_w_mix", 12),
    ("conv_b_mix", 4), ("g_mix_post", 8), ("g_ffn_pre", 8), ("conv_w_ffn", 132), ("conv_b_ffn", 44),
    ("gq_row", 128), ("gk_row", 128), ("ident", 128), ("eps", 1),
]
CST_COLS = [
    ("ones", 128), ("cosA", 32), ("sinA", 32), ("cosI", 16), ("sinI", 16),
    ("inval", 512), ("gmask", 1024), ("smask", 384), ("dftc", 256),
]


def offsets(cols):
    out, at = {}, 0
    for name, n in cols:
        out[name] = (at, n)
        at += n
    return out, at


VEC, NVEC = offsets(VEC_COLS)
CST, NCST = offsets(CST_COLS)


def tile_sizes():
    n = [2048] * 2 + [704] + [2048] * 12
    n += [2048] * (4 + 32)
    n += [2048] * (12 + 4 + 32)
    n += [2048] * (16 + 2 + 2 + 4 + 22 + 11)
    return n


def constants():
    c = np.zeros((P, NCST), np.float32)

    def put(name, a):
        o, n = CST[name]
        c[:, o:o + n] = a.reshape(P, n)

    put("ones", np.ones((P, P), np.float32))
    pos = np.arange(S, dtype=np.float32)
    for tag, rot in (("A", 32), ("I", 16)):
        half = rot // 2
        inv = np.power(np.float32(500000.0), -np.arange(half, dtype=np.float32) * np.float32(2.0) / np.float32(rot))
        ang = (pos[:, None] * inv[None, :].astype(np.float32)).astype(np.float32).astype(np.float64)
        put("cos" + tag, np.cos(ang).astype(np.float32).reshape(2, P, half).transpose(1, 0, 2))
        put("sin" + tag, np.sin(ang).astype(np.float32).reshape(2, P, half).transpose(1, 0, 2))
    t = np.arange(S)
    limit = (t // 64 + 1) * 64
    inval = np.where(t[None, :] < limit[:, None], 0.0, -1.0e37).astype(np.float32)
    put("inval", inval.reshape(2, P, S).transpose(1, 0, 2))
    s, t = np.arange(P)[:, None], np.arange(P)[None, :]
    masks = []
    for hs in (64, 32, 16, 8, 4, 2, 1):
        masks.append((s // (2 * hs) == t // (2 * hs)) & (s % (2 * hs) < hs) & (t % (2 * hs) >= hs))
    masks.append(s == t)
    put("gmask", np.stack(masks, 1).astype(np.float32))
    tri = np.where(s < t, 0.0, BIGNEG).astype(np.float32)
    put("smask", np.concatenate([tri, np.zeros((P, P), np.float32), tri], 1))
    k = np.outer(np.arange(P), np.arange(P)) % P
    scale = 1.0 / np.sqrt(L2 * P)
    put("dftc", np.concatenate([np.cos(2 * np.pi * k / P), np.sin(2 * np.pi * k / P)], 1).astype(np.float32))
    k = np.outer(np.arange(L2), np.arange(L2)) % L2
    dl = np.stack([np.cos(2 * np.pi * k / L2), -np.sin(2 * np.pi * k / L2)], 1) * scale
    dl = dl.astype(np.float32)
    dlx = np.ascontiguousarray(dl[META:].reshape(2, P, 2, L2).transpose(1, 0, 2, 3).reshape(P, 4 * L2))
    tri_s = (s >= t).astype(np.float32)
    return c, dlx, np.ascontiguousarray(dl[:META].reshape(META, 2 * L2)), tri_s


class Bank:
    def __init__(self, t):
        self.t = t
        self.free = []
        self.held = False


class Pair:

    def __init__(self, hi, lo):
        self.hi = hi
        self.lo = lo

    def __getitem__(self, i):
        return Pair(self.hi[i], self.lo[i])

    def view(self, pattern, **kw):
        return Pair(self.hi.rearrange(pattern, **kw), self.lo.rearrange(pattern, **kw))


def block_kernel(nc, W, V, C, DL, CM, TRI, X, MT, WG, GP, OUT):
    ctx = ExitStack()
    with ctx:
        base = -(-nc.sbuf_base // 64) * 64
        end = nc.sbuf_usable_end
        ctx.enter_context(nc.sbuf_tensor("arena", [P, (end - base) // 4 - 32], F32))
        place = [base]

        def at(name, n, off, dt=F32):
            assert off + 4 * n <= end, (name, off + 4 * n, end)
            return nc.alloc_sbuf_tensor_at(name, [P, n], dt, offset=off)[:, :]

        def sb(name, n, dt=F32):
            off = place[0]
            place[0] += -(-4 * n // 32) * 32
            return at(name, n, off, dt)

        def sem(name):
            return ctx.enter_context(nc.semaphore(name))

        queues = {k: [] for k in ("pe", "act", "dve", "pool", "sp")}
        sems = {k: sem("s_" + k) for k in ("pe", "act", "dve", "pool")}
        count = {k: 0 for k in sems}

        def op(e, fn, waits, inc=True):
            tok = None
            if inc:
                count[e] += 1
                tok = (sems[e], count[e])
            queues[e].append((list(waits), fn, (sems[e], 1) if inc else None))
            return tok

        def dve(fn, *waits):
            return op("dve", fn, waits)

        def act(fn, *waits):
            return op("act", fn, waits)

        def pool(fn, *waits):
            return op("pool", fn, waits)

        def dma(fn, waits, s, q="sp"):
            queues[q].append((list(waits), fn, (s, 16)))

        def mm(out, lhsT, rhs, start, stop, waits=(), inc=False):
            return op("pe", lambda e: e.matmul(out, lhsT, rhs, start=start, stop=stop), waits, inc)

        def mm3(out, lhsT, rhs, start, stop, waits=(), inc=False):
            mm(out, lhsT.hi, rhs.hi, start, False, waits)
            mm(out, lhsT.hi, rhs.lo, False, False)
            return mm(out, lhsT.lo, rhs.hi, False, stop, (), inc)

        def tr(out, in_, idn, waits=(), inc=False):
            return op("pe", lambda e: e.transpose(out, in_, idn), waits, inc)

        banks = [Bank(ctx.enter_context(nc.psum_tensor(f"bank{i}", [P, 512], F32))) for i in range(8)]
        bank_at = [0]

        def take(hold=False):
            while banks[bank_at[0] % 8].held:
                bank_at[0] += 1
            b = banks[bank_at[0] % 8]
            b.held = hold
            bank_at[0] += 1
            return b

        raw = [sb(f"raw{i}", SLOT) for i in range(NSLOT)]
        whi = [sb(f"whi{i}", SLOT, F32R) for i in range(NSLOT)]
        wlo = [sb(f"wlo{i}", SLOT, F32R) for i in range(NSLOT)]
        s_raw = [sem(f"s_raw{i}") for i in range(NSLOT)]
        split_done = []
        released = {}
        sizes = tile_sizes()
        starts = [0]
        for n in sizes:
            starts.append(starts[-1] + n * P)
        used = [0]

        def stage(i):
            j, n = i % NSLOT, sizes[i]
            src = W[starts[i]:starts[i + 1]].rearrange("(p n) -> p n", p=P)
            dma(lambda e: e.dma_start(raw[j][:, 0:n], src), [split_done[i - NSLOT]] if i >= NSLOT else [], s_raw[j])

        def split_tile(i):
            j, n = i % NSLOT, sizes[i]
            landed = (s_raw[j], 16 * (i // NSLOT + 1))
            free = [released[i - NSLOT]] if i >= NSLOT else []
            a = act(lambda e: e.activation(whi[j][:, 0:n], raw[j][:, 0:n], ACT.Copy), landed, *free)
            split_done.append(pool(lambda e: e.tensor_tensor(wlo[j][:, 0:n], raw[j][:, 0:n], whi[j][:, 0:n].bitcast(F32),
                                                            ALU.subtract), a, landed, *free))
            if i + NSLOT < len(sizes):
                stage(i + NSLOT)

        def use(k):
            i = used[0]
            used[0] += 1
            while len(split_done) < min(i + 1 + AHEAD, len(sizes)):
                split_tile(len(split_done))
            j, n = i % NSLOT, sizes[i]
            w = Pair(whi[j][:, 0:n], wlo[j][:, 0:n]).view("p (k n) -> p k n", k=k)
            return w, split_done[i], i

        h = sb("h", 2 * D).rearrange("p (t n) -> p t n", t=2)
        nrm = Pair(sb("nhi", 8 * L2, F32R), sb("nlo", 8 * L2, F32R))
        nTa = nrm[:, 0:8 * S].view("p (k t) -> p k t", k=8)
        nT2 = nrm.view("p (k t) -> p k t", k=8)
        o_xn = place[0]
        xn_ = sb("xn", 8 * N2)
        xn = xn_[:, 0:2 * D].rearrange("p (t n) -> p t n", t=2)
        o_clo = place[0]
        clo_ = sb("clo", 8 * S, F32R)
        place[0] = o_clo + -(-8 * N2 * 4 // 32) * 32
        catT = Pair(at("chi", 8 * S, o_xn, F32R), clo_).view("p (k t) -> p k t", k=8)
        vec = sb("vec", NVEC)
        cst = sb("cst", NCST)
        tri = sb("tri_sb", P)
        small = sb("small", 256)
        meta = sb("meta", D)[0:META, :]
        mnorm = sb("mnorm", D)[0:META, :]
        mtmp = sb("mtmp", 8 * META).rearrange("p (k t) -> p k t", k=8)
        room = place[0]

        class Area:

            def __init__(self, tag):
                self.at = room
                self.tag = tag
                self.n = 0

            def __call__(self, n, dt=F32):
                self.n += 1
                a = at(f"{self.tag}{self.n}", n, self.at, dt)
                self.at += -(-4 * n // 32) * 32
                return a

            def pair(self, n):
                return Pair(self(n, F32R), self(n, F32R))

        def vcol(name, i=0, n=1):
            o = VEC[name][0] + i
            return vec[:, o:o + n]

        def const(name):
            o, n = CST[name]
            return cst[:, o:o + n]

        ident = vcol("ident", 0, P)
        eps = vcol("eps")

        s_c = sem("s_c")
        s_x = sem("s_x")
        s_o = sem("s_o")
        s_g = sem("s_g")
        s_d = sem("s_d")
        A = Area("a")
        wg = A(256)[0:16, :]
        s_v = sem("s_v")
        s_x1 = sem("s_x1")
        dma(lambda e: e.dma_start(h[:, 0, :], X[0:P, :]), [], s_x)
        dma(lambda e: e.dma_start(h[:, 1, :], X[P:2 * P, :]), [], s_x1)
        dma(lambda e: e.dma_start(vec, V), [], s_v)
        TX = [[(s_x, 16)], [(s_x1, 16)]]
        TV = (s_v, 16)
        for i in range(NSLOT):
            stage(i)
        dma(lambda e: e.dma_start(cst, C), [], s_c)
        dma(lambda e: e.dma_start(wg, WG), [], s_c)
        dma(lambda e: e.dma_start(tri, TRI), [], s_c)
        TC = (s_c, 48)

        def inv_rms(ss, rs, n, *waits):
            t = act(lambda e: e.activation(rs, ss, ACT.Ln, bias=eps, scale=1.0 / n), TV, *waits)
            return act(lambda e: e.activation(rs, rs, ACT.Exp, scale=-0.5), t)

        def bc(ap, shape):
            return ap.to_broadcast(shape)

        def norm_T(gname, ready, dst, c0):
            ts = []
            for tt in range(2):
                a = act(lambda e, tt=tt: e.activation(xn[:, tt, :], h[:, tt, :], ACT.Square,
                                                      accum_out=small[:, tt:tt + 1]), *ready[tt])
                r = inv_rms(small[:, tt:tt + 1], small[:, 2 + tt:3 + tt], D, a)
                ts.append(dve(lambda e, tt=tt: e.tensor_scalar(xn[:, tt, :], h[:, tt, :], small[:, 2 + tt:3 + tt],
                                                               None, ALU.mult), r))
            out = []
            bs = [take(True) for _ in range(4)]
            for tt in range(2):
                for q, b in enumerate(bs):
                    for kk in range(2):
                        t = tr(b.t[:, kk * 256 + tt * P:kk * 256 + tt * P + P],
                               xn[:, tt, (2 * q + kk) * P:(2 * q + kk + 1) * P], ident,
                               [ts[tt], TV] + b.free, inc=(kk == 1))
                    b.token = t
            for q, b in enumerate(bs):
                xs = [b.t[:, 0:256], b.t[:, 256:512]]
                for kk, x in enumerate(xs):
                    o = dst[:, 2 * q + kk, c0:c0 + S]
                    u = act(lambda e, k=2 * q + kk, x=x, o=o: e.activation(o.hi, x, ACT.Copy, scale=vcol(gname, k)), b.token)
                for kk, x in enumerate(xs):
                    o = dst[:, 2 * q + kk, c0:c0 + S]
                    v = dve(lambda e, k=2 * q + kk, x=x, o=o: e.scalar_tensor_tensor(
                        out=o.lo, in0=x, scalar=vcol(gname, k), in1=o.hi.bitcast(F32),
                        op0=ALU.mult, op1=ALU.subtract), u)
                    out.append([v])
                drop(b, v)
            return out

        def proj_tok(tn, tiles=2):
            bs = [take(True), take(True)]
            for half in range(2):
                w, tk, i = use(4)
                for tt in range(2):
                    for kk in range(4):
                        k = half * 4 + kk
                        t = mm3(bs[tt].t[:, :], nTa[:, k, tt * P:tt * P + P], w[:, kk, :], k == 0, k == 7,
                                [tk] + tn[k] + bs[tt].free, inc=(kk == 3))
                    bs[tt].token = t
                released[i] = t
            return [(b, b.token) for b in bs]

        def drop(b, *toks):
            b.free = list(toks)
            b.held = False

        def out_tok(lhs, ntile, ready, n_k):
            bs = [take(True) for _ in range(4)]
            for it in range(ntile):
                w, tk, i = use(2)
                last = it == ntile - 1
                order = [(kk, j) for j in range(4) for kk in range(2)] if last else [(kk, j) for kk in range(2) for j in range(4)]
                for kk, j in order:
                    k = it * 2 + kk
                    tt, c = j // 2, j % 2
                    t = mm3(bs[j].t[:, :], lhs(k)[:, tt * P:tt * P + P], w[:, kk, c * 512:c * 512 + 512],
                            k == 0, k == n_k - 1, [tk] + ready(k) + bs[j].free, inc=(kk == 1))
                    bs[j].token = t
                released[i] = t
            return bs

        def add_h(bs):
            res = [[], []]
            for j, b in enumerate(bs):
                o = h[:, j // 2, j % 2 * 512:j % 2 * 512 + 512]
                u = dve(lambda e, b=b, o=o: e.tensor_tensor(o, o, b.t[:, :], ALU.add), b.token)
                drop(b, u)
                res[j // 2].append(u)
            return res

        def cat_evac(b, hd, t):
            o, x = catT[:, hd, :], b.t[:, 0:256]
            u = act(lambda e: e.activation(o.hi, x, ACT.Copy), t)
            u = dve(lambda e: e.tensor_tensor(o.lo, x, o.hi.bitcast(F32), ALU.subtract), u)
            b.free = [u]
            return u

        def mlp(gname, ready, tag, after_up=None):
            A = Area(tag)
            ffp = A.pair(32 * S)
            sq = [A(512), A(512)]
            sq_free = [[], []]
            ff = ffp.view("p (k t) -> p k t", k=32)
            tn = norm_T(gname, ready, nTa, 0)
            tf = []

            def rest(m, a):
                o = ffp[:, m * 512:m * 512 + 512]
                u = dve(lambda e, x=sq[m % 2]: e.tensor_tensor(x, x, x, ALU.mult), a)
                u = dve(lambda e, o=o, x=sq[m % 2]: e.tensor_tensor(o.lo, x, o.hi.bitcast(F32), ALU.subtract), u)
                sq_free[m % 2] = [u]
                tf.extend([u, u])

            last = None
            for m in range(16):
                w, tk, i = use(8)
                b = take()
                for c in range(2):
                    for k in range(8):
                        t = mm3(b.t[:, c * 256:c * 256 + 256], w[:, k, c * P:c * P + P], nTa[:, k, :], k == 0, k == 7,
                                [tk] + tn[k] + b.free, inc=(k == 7))
                released[i] = t
                u = act(lambda e, b=b, x=sq[m % 2]: e.activation(x, b.t[:, :], ACT.Relu), t, *sq_free[m % 2])
                b.free = [u]
                a = act(lambda e, m=m, x=sq[m % 2]: e.activation(ffp.hi[:, m * 512:m * 512 + 512], x, ACT.Square), u)
                if last:
                    rest(*last)
                last = (m, a)
            rest(*last)
            if after_up:
                after_up(t)
            return add_h(out_tok(lambda k: ff[:, k, :], 16, lambda k: [tf[k]], 32))

        IQ = A(2 * 576)
        IKD = A(256)
        IQT = A(1024).rearrange("p (b t) -> p b t", b=4)
        IKT = A(256)
        RL = A(1024).rearrange("p (j n) -> p j n", j=2)
        SC = A(512).rearrange("p (t n) -> p t n", t=2)
        SEL = A(512)
        SELv = SEL.rearrange("p (t n) -> p t n", t=2)
        QKT = A(2048).rearrange("p (k t) -> p k t", k=8)
        VA = A(1024).rearrange("p (t n) -> p t n", t=2)
        VB = A(1024).rearrange("p (t n) -> p t n", t=2)
        OG = A(1024).rearrange("p (t n) -> p t n", t=2)
        QK0 = A(1024).rearrange("p (j n) -> p j n", j=2)
        BB = A(512)
        DE = A(512)
        SS = A(1024).rearrange("p (j n) -> p j n", j=2)
        PT = A(768).rearrange("p (j n) -> p j n", j=2)
        AM = IQ[:, 0:1024]
        AM2 = A(256)
        RT = SS.rearrange("p j n -> p (j n)")
        GL = A(256)
        IQv = IQ.rearrange("p (t h d) -> p t h d", t=2, h=9)
        QA = xn.rearrange("p t (h d) -> p t h d", h=8)
        QKE = A(8 * 512).rearrange("p (l n) -> p l n", l=8)

        op("act", lambda e: e.preload_act_table_set("natural_log_exp_and_others"), [], inc=False)
        tn = norm_T("g_mix0", TX, nTa, 0)

        cp = []
        for tt, (b, t) in enumerate(proj_tok(tn)):
            u = act(lambda e, tt=tt, b=b: e.activation(IQ[:, tt * 576:tt * 576 + 512], b.t[:, :], ACT.Copy), t)
            drop(b, u)
            cp.append(u)
        w, tk, i = use(8)
        IW = small[:, 16:32]
        for tt in range(2):
            b = take()
            for k in range(8):
                t = mm3(b.t[:, 0:72], nTa[:, k, tt * P:tt * P + P], w[:, k, 16:88], k == 0, k == 7,
                        [tk] + tn[k] + b.free, inc=(k == 7))
            u = act(lambda e, tt=tt, b=b: e.activation(IQ[:, tt * 576 + 512:tt * 576 + 576], b.t[:, 0:64], ACT.Copy), t)
            v = act(lambda e, tt=tt, b=b: e.activation(IW[:, tt * 8:tt * 8 + 8], b.t[:, 64:72], ACT.Copy,
                                                       scale=8.0 ** -0.5), t)
            b.free = [v]
            cp += [u]
        tiw = v
        b = take()
        for k in range(8):
            t = mm3(b.t[0:88, 0:256], w[:, k, :], nTa[:, k, :], k == 0, k == 7, [tk] + tn[k] + b.free, inc=(k == 7))
        released[i] = t
        tgl = act(lambda e, b=b: e.activation(GL[0:16, :], b.t[0:16, 0:256], ACT.Copy), t)
        b.free = [tgl]
        tqk = []
        for j in range(2):
            b = take()
            w, tk, i = use(8)
            for p in range(2):
                for k in range(8):
                    t = mm3(b.t[:, p * 256:p * 256 + 256], w[:, k, p * P:p * P + P], nTa[:, k, :], k == 0, k == 7,
                            [tk] + tn[k] + b.free, inc=(k == 7))
            released[i] = t
            u = act(lambda e, b=b, j=j: e.activation(QK0[:, j, :], b.t[:, :], ACT.Copy, scale=0.125 if j == 0 else 1.0), t)
            b.free = [u]
            tqk.append(u)
        b = take()
        for p in range(2):
            t = mm(b.t[:, p * 256:p * 256 + 256], wg[:, p * P:p * P + P], GL[0:16, :], True, True,
                   [tgl, TC] + b.free, inc=True)
        us = []
        for p in range(2):
            us.append(act(lambda e, p=p, b=b: e.activation(BB[:, p * 256:p * 256 + 256], b.t[:, p * 256:p * 256 + 256],
                                                           ACT.Identity, bias=vcol("b_gate", p)), t))
        b.free = us
        u = act(lambda e: e.activation(DE, BB, ACT.Abs), *us)
        u = act(lambda e: e.activation(DE, DE, ACT.Exp, scale=-1.0), u)
        u = act(lambda e: e.activation(DE, DE, ACT.Ln, bias=1.0), u)
        u = dve(lambda e: e.scalar_tensor_tensor(out=DE, in0=BB, scalar=0.0, in1=DE, op0=ALU.min, op1=ALU.subtract), u)
        tb = []
        for p in range(2):
            tb.append(dve(lambda e, p=p: e.tensor_tensor_scan(
                BB[:, p * 256:p * 256 + 256], DE[:, p * 256:p * 256 + 256], DE[:, p * 256:p * 256 + 256], 0.0,
                ALU.add, ALU.bypass), u))

        def rope(view, H, half, cname, sname, ready):
            cs = bc(const(cname).rearrange("p (t o n) -> p t o n", t=2, o=1), [P, 2, H, half])
            sn = bc(const(sname).rearrange("p (t o n) -> p t o n", t=2, o=1), [P, 2, H, half])
            n = 2 * H * half
            tmp = [RT[:, i * 256:i * 256 + n].rearrange("p (t h n) -> p t h n", t=2, h=H) if n <= 256 else None
                   for i in range(4)]
            x1 = view[:, :, :, 0:half]
            x2 = view[:, :, :, half:2 * half]
            a = dve(lambda e: e.tensor_tensor(tmp[0], x1, cs, ALU.mult), *ready)
            b_ = dve(lambda e: e.tensor_tensor(tmp[1], x2, sn, ALU.mult), *ready)
            c_ = dve(lambda e: e.tensor_tensor(tmp[2], x2, cs, ALU.mult), *ready)
            d_ = dve(lambda e: e.tensor_tensor(tmp[3], x1, sn, ALU.mult), *ready)
            f = dve(lambda e: e.tensor_tensor(x1, tmp[0], tmp[1], ALU.subtract), a, b_, d_)
            g = dve(lambda e: e.tensor_tensor(x2, tmp[2], tmp[3], ALU.add), c_, d_)
            return [f, g]

        tro = rope(IQv, 9, 8, "cosI", "sinI", cp + [TC])
        tik = []
        for tt in range(2):
            for j in range(2):
                tik.append(dve(lambda e, tt=tt, j=j: e.tensor_copy(IKD[:, tt * P + j * 64:tt * P + j * 64 + 64],
                                                                   IQ[:, tt * 576 + 512:tt * 576 + 576]), *tro))

        qa_ready = []
        ssA = small[:, 32:48].rearrange("p (j t h) -> p j t h", j=2, t=2)
        for j, grow in enumerate(("gq_row", "gk_row")):
            for tt, (b, t) in enumerate(proj_tok(tn)):
                q = QA[:, tt, 4 * j:4 * j + 4, :]
                a = act(lambda e, q=q, b=b: e.activation(q, b.t[:, :].rearrange("p (h d) -> p h d", h=4), ACT.Square), t)
                sq = ssA[:, j, tt, :]
                u = dve(lambda e, q=q, sq=sq: e.tensor_reduce(sq, q, AX.X, ALU.add), a)
                u = inv_rms(sq, sq, P, u)
                u = dve(lambda e, q=q, sq=sq, b=b: e.tensor_tensor(
                    q, b.t[:, :].rearrange("p (h d) -> p h d", h=4),
                    bc(sq.rearrange("p (h o) -> p h o", o=1), [P, 4, P]), ALU.mult), u)
                drop(b, u)
                g = VEC[grow][0]
                u = dve(lambda e, q=q, g=g: e.tensor_tensor(
                    q, q, bc(vec[:, g:g + P].rearrange("p (o d) -> p o d", o=1), [P, 4, P]), ALU.mult), u)
                qa_ready.append(u)
            if j == 0:
                tiq = []
                for tt in range(2):
                    b = take()
                    for m in range(4):
                        t = tr(b.t[:, m * P:m * P + P], IQ[:, tt * 576 + m * P:tt * 576 + m * P + P], ident,
                               tro + b.free, inc=(m == 3))
                    u = act(lambda e, tt=tt, b=b: e.activation(IQT[:, :, tt * P:tt * P + P],
                                                               b.t[:, :].rearrange("p (m t) -> p m t", m=4), ACT.Copy), t)
                    b.free = [u]
                    tiq.append(u)
                b = take()
                for tt in range(2):
                    t = tr(b.t[:, tt * P:tt * P + P], IKD[:, tt * P:tt * P + P], ident, tik + b.free, inc=(tt == 1))
                u = act(lambda e, b=b: e.activation(IKT, b.t[:, 0:256], ACT.Copy), t)
                b.free = [u]
                tiq.append(u)
        tqr = rope(QA, 8, 16, "cosA", "sinA", qa_ready + [TC])

        tsc = None
        rl_free = [[], []]
        n = 0
        for tt in range(2):
            for m2, e2 in ((0, 0), (0, 1), (1, 0), (1, 1)):
                b = take()
                for j in range(2):
                    t = mm(b.t[:, j * 256:j * 256 + 256], IQT[e2 * 64:e2 * 64 + 64, 2 * m2 + j, tt * P:tt * P + P],
                           IKT[e2 * 64:e2 * 64 + 64, :], True, True, tiq + b.free, inc=(j == 1))
                rl = RL[:, n % 2, :]
                a = act(lambda e, rl=rl, b=b: e.activation(rl, b.t[:, :], ACT.Relu, scale=0.125), t, *rl_free[n % 2])
                b.free = [a]
                for j in range(2):
                    hd = 2 * (2 * m2 + j) + e2
                    acc = SC[:, tt, :]
                    o = CST["inval"][0] + tt * 256
                    in1 = cst[:, o:o + 256] if hd == 0 else acc
                    tsc = dve(lambda e, rl=rl, j=j, tt=tt, hd=hd, in1=in1, acc=acc: e.scalar_tensor_tensor(
                        out=acc, in0=rl[:, j * 256:j * 256 + 256], scalar=IW[:, tt * 8 + hd:tt * 8 + hd + 1],
                        in1=in1, op0=ALU.mult, op1=ALU.add), a, tiw, TC, *([tsc] if tsc else []))
                rl_free[n % 2] = [tsc]
                n += 1
        tsel = [pool(lambda e: e.memset(SEL[:, P:256], BIGNEG))]
        for tt in range(2):
            wd = P * (tt + 1)
            wk = SC[:, tt, 0:wd]
            u = tsc
            for r in range(8):
                m8 = small[:, 48 + 8 * r:56 + 8 * r]
                u = dve(lambda e, wk=wk, m8=m8: e.max(m8, wk), u)
                u = dve(lambda e, wk=wk, m8=m8: e.match_replace(wk, m8, wk, -3.0e38), u)
            tsel.append(dve(lambda e, wk=wk, tt=tt, wd=wd: e.tensor_scalar(SELv[:, tt, 0:wd], wk, -2.0e38, BIGNEG,
                                                                          ALU.is_gt, ALU.mult), u))

        tva = []
        for tt, (b, t) in enumerate(proj_tok(tn)):
            u = act(lambda e, tt=tt, b=b: e.activation(VA[:, tt, :], b.t[:, :], ACT.Copy), t)
            drop(b, u)
            tva.append(u)
        tvb = []
        for tt, (b, t) in enumerate(proj_tok(tn)):
            u = act(lambda e, tt=tt, b=b: e.activation(VB[:, tt, :], b.t[:, :], ACT.Copy), t)
            drop(b, u)
            tvb.append(u)
        op("act", lambda e: e.preload_act_table_set("sigmoid_and_others"), [], inc=False)
        tog = []
        for tt, (b, t) in enumerate(proj_tok(tn)):
            g = OG[:, tt, :]
            u = act(lambda e, g=g, b=b: e.activation(g, b.t[:, :], ACT.Sigmoid), t)
            u = dve(lambda e, g=g, b=b: e.tensor_tensor(g, g, b.t[:, :], ALU.mult), u)
            drop(b, u)
            tog.append(u)
        op("act", lambda e: e.preload_act_table_set("natural_log_exp_and_others"), [], inc=False)

        tlev = []
        tprev = []
        for l, hs in enumerate((128, 64, 32, 16, 8, 4, 2, 1)):
            nb = 256 // hs
            bv = BB.rearrange("p (b u s) -> p b u s", u=2, s=hs)
            dv = DE.rearrange("p (b u s) -> p b u s", u=2, s=hs)
            mid = bc(bv[:, :, 0, hs - 1:hs], [P, nb, hs])
            u1 = dve(lambda e, bv=bv, dv=dv, mid=mid: e.tensor_tensor(dv[:, :, 1, :], bv[:, :, 1, :], mid, ALU.subtract),
                     *tb, *tprev)
            u2 = dve(lambda e, bv=bv, dv=dv, mid=mid: e.tensor_tensor(dv[:, :, 0, :], mid, bv[:, :, 0, :], ALU.subtract),
                     *tb, *tprev)
            a = act(lambda e: e.activation(DE, DE, ACT.Exp, scale=1.0 / 16.0), u1, u2)
            tl = []
            for j, side in ((0, 1), (1, 0)):
                ov = QKE[:, l, :].rearrange("p (b u s) -> p b u s", u=2, s=hs)[:, :, side, :]
                iv = QK0[:, j, :].rearrange("p (b u s) -> p b u s", u=2, s=hs)[:, :, side, :]
                tl.append(dve(lambda e, ov=ov, iv=iv, dv=dv, side=side: e.tensor_tensor(ov, iv, dv[:, :, side, :], ALU.mult),
                              a, *tqk))
            tprev = tl
            tlev.append(tl)

        tq = []
        for tt in range(2):
            for j in range(2):
                b = take()
                for hd in range(4):
                    t = tr(b.t[:, hd * P:hd * P + P], QA[:, tt, 4 * j + hd, :], ident, tqr + b.free, inc=(hd == 3))
                u = act(lambda e, b=b, j=j, tt=tt: e.activation(QKT[:, 4 * j:4 * j + 4, tt * P:tt * P + P],
                                                                b.t[:, :].rearrange("p (m t) -> p m t", m=4), ACT.Copy), t)
                b.free = [u]
                tq.append(u)

        tcat = []
        am_free = [[], []]
        AMs = [AM, None]
        gm = const("gmask")
        ob_bank = []
        tob = []
        for tt in range(2):
            ob = take(hold=True)
            for hd in range(4):
                p, e2 = hd // 2, hd % 2
                lo = e2 * 64
                tm = []
                for half in range(2):
                    b = take()
                    for i in range(4):
                        l = half * 4 + i + 1
                        c = p * 256 + tt * P
                        kx = QKE[lo:lo + 64, l, c:c + P] if l < 8 else QK0[lo:lo + 64, 1, c:c + P]
                        qx = QKE[lo:lo + 64, l, c:c + P] if l < 8 else QK0[lo:lo + 64, 0, c:c + P]
                        t = mm(b.t[:, i * P:i * P + P], kx, qx, True, True,
                               (tlev[l] if l < 8 else tqk) + b.free, inc=(i == 3))
                    o = AM[:, half * 512:half * 512 + 512]
                    u = dve(lambda e, o=o, b=b, half=half: e.tensor_tensor(o, b.t[:, :], gm[:, half * 512:half * 512 + 512],
                                                                          ALU.mult), t, *am_free[0])
                    b.free = [u]
                    tm.append(u)
                if tt == 1:
                    b = take()
                    t = mm(b.t[:, 0:P], QKE[lo:lo + 64, 0, p * 256:p * 256 + P],
                           QKE[lo:lo + 64, 0, p * 256 + P:p * 256 + 256], True, True, tlev[0] + b.free, inc=True)
                    u = act(lambda e, b=b: e.activation(AM2[:, 0:P], b.t[:, 0:P], ACT.Copy), t, *am_free[1])
                    b.free = [u]
                    tm.append(u)
                oo = ob.t[:, hd * P:hd * P + P]
                for i in range(8):
                    t = mm(oo, AM[:, i * P:i * P + P], VB[:, tt, hd * P:hd * P + P], i == 0, i == 7 and tt == 0,
                           tm + tvb + ob.free, inc=(i == 7))
                if tt == 1:
                    t = mm(oo, AM2[:, 0:P], VB[:, 0, hd * P:hd * P + P], False, True, [], inc=True)
                am_free = [[t], [t]]
            obv = ob.t[:, :].rearrange("p (h d) -> p h d", h=4)
            y = SS[:, tt, :]
            yv = y.rearrange("p (h d) -> p h d", h=4)
            a = act(lambda e, y=y, ob=ob: e.activation(y, ob.t[:, :], ACT.Square), t)
            ss = small[:, 112 + 4 * tt:116 + 4 * tt]
            u = dve(lambda e, ss=ss, yv=yv: e.tensor_reduce(ss, yv, AX.X, ALU.add), a)
            u = inv_rms(ss, ss, P, u)
            u = dve(lambda e, ss=ss, yv=yv, obv=obv: e.tensor_tensor(
                yv, obv, bc(ss.rearrange("p (h o) -> p h o", o=1), [P, 4, P]), ALU.mult), u)
            ob.free = [u]
            ob.held = False
            u = dve(lambda e, y=y, tt=tt: e.tensor_tensor(y, y, OG[:, tt, :], ALU.mult), u, tog[tt])
            b = take()
            for hd in range(4):
                t = tr(b.t[:, hd * P:hd * P + P], SS[:, tt, hd * P:hd * P + P], ident, [u] + b.free, inc=(hd == 3))
            o = catT[:, 4:8, tt * P:tt * P + P]
            x = b.t[:, :].rearrange("p (m t) -> p m t", m=4)
            u = act(lambda e, o=o, x=x: e.activation(o.hi, x, ACT.Copy, scale=vcol("g_gla")), t)
            u = dve(lambda e, o=o, x=x: e.scalar_tensor_tensor(out=o.lo, in0=x, scalar=vcol("g_gla"), in1=o.hi.bitcast(F32),
                                                              op0=ALU.mult, op1=ALU.subtract), u)
            b.free = [u]
            tob += [u]

        scale = float(P) ** -0.5
        toa = []
        ss_free = [[u], [u]]
        pt_free = [[], []]
        for hd in range(4):
            b = take()
            for tt in range(2):
                t = mm(b.t[:, tt * 256:tt * 256 + 256], QKT[:, hd, tt * P:tt * P + P], QKT[:, 4 + hd, :], True, True,
                       tq + b.free, inc=(tt == 1))
            y = SS[:, hd % 2, :]
            yv = y.rearrange("p (t n) -> p t n", t=2)
            mx = small[:, 128 + 2 * hd:130 + 2 * hd]
            sm = small[:, 136 + 2 * hd:138 + 2 * hd]
            u = dve(lambda e, y=y, b=b: e.tensor_tensor(y, b.t[:, :], SEL, ALU.add), t, *tsel, *ss_free[hd % 2])
            b.free = [u]
            u = dve(lambda e, mx=mx, yv=yv: e.tensor_reduce(mx, yv, AX.X, ALU.max), u)
            u = dve(lambda e, mx=mx: e.tensor_scalar(mx, mx, -scale, None, ALU.mult), u)
            us = []
            for tt in range(2):
                us.append(act(lambda e, yv=yv, tt=tt, mx=mx, sm=sm: e.activation(
                    yv[:, tt, :], yv[:, tt, :], ACT.Exp, bias=mx[:, tt:tt + 1], scale=scale,
                    accum_out=sm[:, tt:tt + 1]), u))
            u = dve(lambda e, sm=sm: e.reciprocal(sm, sm), *us)
            u = dve(lambda e, sm=sm, yv=yv: e.tensor_tensor(yv, yv, bc(sm.rearrange("p (t o) -> p t o", o=1), [P, 2, 256]),
                                                            ALU.mult), u)
            b = take()
            for i, (tt, kb) in enumerate(((0, 0), (1, 0), (1, 1))):
                t = tr(b.t[:, i * P:i * P + P], yv[:, tt, kb * P:kb * P + P], ident, [u] + b.free, inc=(i == 2))
            ss_free[hd % 2] = [t]
            pt = PT[:, hd % 2, :]
            u = act(lambda e, pt=pt, b=b: e.activation(pt, b.t[:, 0:384], ACT.Copy), t, *pt_free[hd % 2])
            b.free = [u]
            b = take()
            t = mm(b.t[:, 0:256], VA[:, 0, hd * P:hd * P + P], pt[:, 0:256], True, False, [u] + tva + b.free)
            t = mm(b.t[:, P:256], VA[:, 1, hd * P:hd * P + P], pt[:, 256:384], False, True, [], inc=True)
            pt_free[hd % 2] = [t]
            toa.append(cat_evac(b, hd, t))

        th = add_h(out_tok(lambda k: catT[:, k, :], 4, lambda k: [toa[k]] if k < 4 else tob, 8))
        th = mlp("g_ffn0", th, "f")

        A = Area("c")
        QT = A(2048).rearrange("p (k t) -> p k t", k=8)
        KT = A(2048).rearrange("p (k t) -> p k t", k=8)
        VC = A(2048).rearrange("p (t n) -> p t n", t=2)
        QN = A(2048).rearrange("p (j n) -> p j n", j=4)
        NZ = 4
        ZB = [[A(384) for _ in range(3)] for _ in range(NZ)]
        tn = norm_T("g_mix1", th, nTa, 0)
        gs = small[:, 144:145]
        tgs = dve(lambda e: e.tensor_scalar(gs, vcol("gq_c"), float(P) ** -0.5, None, ALU.mult), TV)
        tqk = [[], []]
        qn_free = [[] for _ in range(4)]

        def turn(j, half, tt, n, u):
            b = take()
            for hd in range(4):
                t = tr(b.t[:, hd * P:hd * P + P], QN[:, n, hd * P:hd * P + P], ident, [u] + b.free, inc=(hd == 3))
            qn_free[n] = [t]
            dst = (QT, KT)[j][:, half * 4:half * 4 + 4, tt * P:tt * P + P]
            g = gs if j == 0 else vcol("gk_c")
            v = act(lambda e: e.activation(dst, b.t[:, :].rearrange("p (m t) -> p m t", m=4), ACT.Copy, scale=g), t, tgs)
            b.free = [v]
            tqk[half].append(v)

        todo = []
        n = 0
        for half in range(2):
            for j in range(2):
                done = todo
                todo = []
                pr = proj_tok(tn)
                for tt, (b, t) in enumerate(pr):
                    q = QN[:, n % 4, :]
                    qv = q.rearrange("p (h d) -> p h d", h=4)
                    ss = small[:, 148 + 4 * n:152 + 4 * n]
                    a = act(lambda e, q=q, b=b: e.activation(q, b.t[:, :], ACT.Square), t, *qn_free[n % 4])
                    u = dve(lambda e, qv=qv, ss=ss: e.tensor_reduce(ss, qv, AX.X, ALU.add), a)
                    u = inv_rms(ss, ss, P, u)
                    u = dve(lambda e, qv=qv, ss=ss, b=b: e.tensor_tensor(
                        qv, b.t[:, :].rearrange("p (h d) -> p h d", h=4),
                        bc(ss.rearrange("p (h o) -> p h o", o=1), [P, 4, P]), ALU.mult), u)
                    drop(b, u)
                    todo.append((j, half, tt, n % 4, u))
                    n += 1
                for x in done:
                    turn(*x)
        tv = [[], []]
        sm = const("smask")
        ones = const("ones")
        z_free = [[] for _ in range(NZ)]
        tc_ = []
        st = {}

        def stick_1(hd):
            Z, E1, LL = ZB[hd % NZ]
            b = take()
            t = mm(b.t[:, 0:256], KT[:, hd, 0:P], QT[:, hd, :], True, True, tqk[hd // 4] + b.free)
            t = mm(b.t[:, 256:384], KT[:, hd, P:256], QT[:, hd, P:256], True, True, [], inc=True)
            u = dve(lambda e: e.tensor_tensor(Z, b.t[:, 0:384], sm, ALU.add), t, TC, *z_free[hd % NZ])
            b.free = [u]
            u = act(lambda e: e.activation(E1, Z, ACT.Abs), u)
            u = act(lambda e: e.activation(E1, E1, ACT.Exp, scale=-1.0), u)
            st[hd] = act(lambda e: e.activation(E1, E1, ACT.Ln, bias=1.0), u)

        def stick_2(hd):
            Z, E1, LL = ZB[hd % NZ]
            u = dve(lambda e: e.scalar_tensor_tensor(out=LL, in0=Z, scalar=0.0, in1=E1, op0=ALU.max, op1=ALU.add), st[hd])
            b = take()
            t = mm(b.t[:, 0:256], tri, LL[:, 0:256], True, False, [u, TC] + b.free)
            t = mm(b.t[:, P:256], ones, LL[:, 256:384], False, True, [])
            t = mm(b.t[:, 256:384], tri, LL[:, 256:384], True, True, [], inc=True)
            u = dve(lambda e: e.tensor_tensor(Z, Z, b.t[:, 0:384], ALU.subtract), t)
            b.free = [u]
            st[hd] = act(lambda e: e.activation(LL, Z, ACT.Exp), u)

        def stick_3(hd):
            Z, E1, LL = ZB[hd % NZ]
            b = take()
            t = mm(b.t[:, 0:256], VC[:, 0, hd * P:hd * P + P], LL[:, 0:256], True, False, [st[hd]] + tv[hd // 4] + b.free)
            t = mm(b.t[:, P:256], VC[:, 1, hd * P:hd * P + P], LL[:, 256:384], False, True, [], inc=True)
            z_free[hd % NZ] = [t]
            tc_.append(cat_evac(b, hd, t))

        def stick_step(i):
            if 0 <= i - 3 < 8:
                stick_3(i - 3)
            if 0 <= i - 1 < 8:
                stick_2(i - 1)
            if i < 8:
                stick_1(i)

        for half in range(2):
            pr = proj_tok(tn)
            if half == 0:
                for x in todo:
                    turn(*x)
            for tt, (b, t) in enumerate(pr):
                u = act(lambda e, tt=tt, b=b, half=half: e.activation(VC[:, tt, half * 512:half * 512 + 512], b.t[:, :],
                                                                      ACT.Copy), t)
                drop(b, u)
                tv[half].append(u)
            if half == 0:
                for i in range(4):
                    stick_step(i)
        for i in range(4, 11):
            stick_step(i)
        th = add_h(out_tok(lambda k: catT[:, k, :], 4, lambda k: [tc_[k]], 8))
        dma(lambda e: e.dma_start(meta, MT), [], s_g)
        TM = (s_g, 16)
        tmeta = []

        def meta_norm(up_done):
            ms, mr = small[0:META, 8:9], small[0:META, 9:10]
            a = act(lambda e: e.activation(mnorm, meta, ACT.Square, accum_out=ms), TM)
            t = act(lambda e: e.activation(mr, ms, ACT.Ln, bias=eps[0:META, :], scale=1.0 / D), TV, a)
            t = act(lambda e: e.activation(mr, mr, ACT.Exp, scale=-0.5), t)
            u = dve(lambda e: e.tensor_scalar(mnorm, meta, mr, None, ALU.mult), t)
            b = take()
            for k in range(8):
                t = tr(b.t[:, k * META:k * META + META], mnorm[:, k * P:k * P + P], ident[0:META, 0:META], [u] + b.free,
                       inc=(k == 7))
            u = dve(lambda e: e.tensor_tensor(mtmp, b.t[:, 0:P].rearrange("p (k t) -> p k t", k=8),
                                              bc(vcol("g_mix_pre", 0, 8).rearrange("p (k o) -> p k o", o=1), [P, 8, META]),
                                              ALU.mult), t)
            b.free = [u]
            o = nT2[:, :, 0:META]
            a = act(lambda e: e.activation(o.hi, mtmp, ACT.Copy), u, up_done)
            tmeta.append(dve(lambda e: e.tensor_tensor(o.lo, mtmp, o.hi.bitcast(F32), ALU.subtract), a))

        th = mlp("g_ffn1", th, "g", meta_norm)

        A = Area("b")
        HT_ = A(8 * L2)
        HT = HT_.rearrange("p (k t) -> p k t", k=8)
        SQ = A(2 * L2).rearrange("p (j t) -> p j t", j=2)
        RS = A(L2)
        o_ffn = A.at
        TMP = A(2 * L2).rearrange("p (j t) -> p j t", j=2)
        UT = A(4 * L2).rearrange("p (k t) -> p k t", k=4)
        GT = A(16 * N2).rearrange("p (k t) -> p k t", k=16)
        CG = A(4 * N2).rearrange("p (k t) -> p k t", k=4)
        CV = A(4 * N2).rearrange("p (k t) -> p k t", k=4)
        FT = A.pair(4 * N2).view("p (k t) -> p k t", k=4)
        YB = A.pair(4 * N2).view("p (k t) -> p k t", k=4)
        cm = A(2 * L2)[0:META, :]
        P1s = [A(3 * 256).rearrange("p (t n) -> p t n", t=3) for _ in range(2)]
        dlx = A(4 * L2)
        MG = Pair(at("mhi", 8 * N2, o_xn, F32R), at("mlo", 8 * N2, o_clo, F32R)).view("p (k t) -> p k t", k=8)
        th_all = th[0] + th[1]
        dma(lambda e: e.dma_start(cm, CM), th_all, s_d)
        dma(lambda e: e.dma_start(dlx, DL), th_all, s_d)
        TD = (s_d, 32)
        tn = [x + tmeta for x in norm_T("g_mix_pre", th, nT2, META)]
        t_ht = []

        def residual_T(q):
            b = take()
            for kk in range(2):
                for tt in range(2):
                    t = tr(b.t[:, kk * 256 + tt * P:kk * 256 + tt * P + P], h[:, tt, (2 * q + kk) * P:(2 * q + kk + 1) * P],
                           ident, th_all + b.free, inc=(kk == 1 and tt == 1))
            u = act(lambda e: e.activation(HT[:, 2 * q:2 * q + 2, META:L2],
                                           b.t[:, :].rearrange("p (k t) -> p k t", k=2), ACT.Copy), t)
            b.free = [u]
            t_ht.append(u)

        def residual_meta():
            b = take()
            for k in range(8):
                t = tr(b.t[:, k * META:k * META + META], meta[:, k * P:k * P + P], ident[0:META, 0:META], [TM] + b.free,
                       inc=(k == 7))
            u = act(lambda e: e.activation(HT[:, :, 0:META], b.t[:, 0:P].rearrange("p (k t) -> p k t", k=8), ACT.Copy),
                    t, *th_all)
            b.free = [u]
            t_ht.append(u)

        sq_free = [[], []]

        class ColNorm:

            def __init__(self):
                self.b = take(True)
                self.k = 0
                self.sq = None

            def square(self, x, *ready):
                k = self.k
                s2 = SQ[:, k % 2, 0:N2]
                self.sq = (k, s2, act(lambda e: e.activation(s2, x, ACT.Square), *ready, *sq_free[k % 2]))
                self.k += 1
                return self.sq[2]

            def add(self):
                k, s2, a = self.sq
                t = mm(self.b.t[:, 0:N2], ones, s2, k == 0, k == 7, [a, TC] + self.b.free, inc=True)
                sq_free[k % 2] = [t]
                self.t = t

            def done(self, *free):
                u = act(lambda e: e.activation(RS[:, 0:N2], self.b.t[:, 0:N2], ACT.Ln, bias=eps, scale=1.0 / D), self.t,
                        *free)
                drop(self.b, u)
                return act(lambda e: e.activation(RS[:, 0:N2], RS[:, 0:N2], ACT.Exp, scale=-0.5), u)

        tmp_free = [[], []]

        def split(x, o, j, *ready):
            a = act(lambda e: e.activation(o.hi, x, ACT.Copy), *ready)
            return dve(lambda e: e.tensor_tensor(o.lo, x, o.hi.bitcast(F32), ALU.subtract), a)

        def norm_cols(gname, c0, ready):
            out = []
            for k in range(8):
                x = TMP[:, k % 2, 0:L2 - c0]
                u = dve(lambda e, k=k, x=x: e.scalar_tensor_tensor(out=x, in0=HT[:, k, c0:L2], scalar=vcol(gname, k),
                                                                  in1=RS[:, 0:L2 - c0], op0=ALU.mult, op1=ALU.mult),
                        *ready, *tmp_free[k % 2])
                u = split(x, nT2[:, k, c0:L2], k % 2, u)
                tmp_free[k % 2] = [u]
                out.append([u])
            return out

        def proj_feat(w, c, ready, tk, c0, kn=8, rhs=None):
            b = take()
            for k in range(kn):
                r = nT2[:, k, c0:L2] if rhs is None else rhs[:, k, :]
                t = mm3(b.t[:, 0:L2 - c0], w[:, k, c:c + P], r, k == 0, k == kn - 1, [tk] + ready[k] + b.free,
                        inc=(k == kn - 1))
            return b, t

        def feat_blocks(blocks, per, kn, ready, c0, rhs=None):
            for m in range(blocks):
                if m % per == 0:
                    w, tk, i = use(kn)
                b, t = proj_feat(w, m % per * P, ready, tk, c0, kn, rhs)
                if m % per == per - 1:
                    released[i] = t
                yield m, b, t

        tu = []
        for m, b, t in feat_blocks(4, 2, 8, tn, 0):
            u = act(lambda e, b=b, m=m: e.activation(UT[:, m, :], b.t[:, 0:L2], ACT.Copy), t)
            b.free = [u]
            tu.append(u)
            residual_T(m)
        residual_meta()
        tcg = []
        for m, b, t in feat_blocks(4, 2, 8, tn, X0):
            u = act(lambda e, b=b, m=m: e.activation(CG[:, m, :], b.t[:, 0:N2], ACT.Copy), t)
            b.free = [u]
            tcg.append(u)
        tcv = []
        for m, b, t in feat_blocks(4, 2, 8, tn, X0):
            u = dve(lambda e, b=b, m=m: e.tensor_tensor(CG[:, m, :], CG[:, m, :], b.t[:, 0:N2], ALU.mult), t, tcg[m])
            b.free = [u]
            u = act(lambda e, m=m: e.activation(CV[:, m, :], CG[:, m, :], ACT.Identity, bias=vcol("conv_b_mix", m),
                                                scale=vcol("conv_w_mix", 4 + m)), u)
            u = dve(lambda e, m=m: e.scalar_tensor_tensor(out=CV[:, m, 1:N2], in0=CG[:, m, 0:N2 - 1],
                                                          scalar=vcol("conv_w_mix", m), in1=CV[:, m, 1:N2],
                                                          op0=ALU.mult, op1=ALU.add), u)
            u = dve(lambda e, m=m: e.scalar_tensor_tensor(out=CV[:, m, 0:N2 - 1], in0=CG[:, m, 1:N2],
                                                          scalar=vcol("conv_w_mix", 8 + m), in1=CV[:, m, 0:N2 - 1],
                                                          op0=ALU.mult, op1=ALU.add), u)
            tcv.append(u)
        tyb = []
        for m, b, t in feat_blocks(4, 2, 8, tn, X0):
            u = dve(lambda e, b=b, m=m: e.tensor_tensor(CV[:, m, :], CV[:, m, :], b.t[:, 0:N2], ALU.mult), t, tcv[m])
            b.free = [u]
            tyb.append([split(CV[:, m, :], YB[:, m, :], 0, u)])
        dftc = const("dftc")
        dl = dlx.rearrange("p (t j l) -> p t j l", t=2, j=2)
        cmv = cm.rearrange("p (j l) -> p j l", j=2)
        p1_free = [[], []]
        p1_done = {}
        tft = []

        def dft_channels(g):
            P1 = P1s[g % 2]
            us = []
            for i, (c, n) in enumerate(((META, P), (META + P, P), (0, META))):
                b = take()
                t = mm(b.t[0:n, 0:256], UT[:, g, c:c + n], dftc, True, True, [tu[g], TC] + b.free, inc=True)
                u = act(lambda e, b=b, n=n, i=i: e.activation(P1[0:n, i, :], b.t[0:n, 0:256], ACT.Copy), t, *p1_free[g % 2])
                b.free = [u]
                us.append(u)
            p1_done[g] = us

        def dft_positions(g):
            P1 = P1s[g % 2]
            b = take()
            n = 0
            for i in range(3):
                for j in range(2):
                    kp = P if i < 2 else META
                    rhs = dl[:, i, j, X0:L2] if i < 2 else cmv[:, j, X0:L2]
                    t = mm(b.t[:, 0:N2], P1[0:kp, i, j * P:j * P + P], rhs, n == 0, n == 5, p1_done[g] + [TD] + b.free,
                           inc=(n == 5))
                    n += 1
            p1_free[g % 2] = [t]
            u = split(b.t[:, 0:N2], FT[:, g, :], 0, t)
            b.free = [u]
            tft.append([u])

        op("act", lambda e: e.preload_act_table_set("sigmoid_and_others"), [], inc=False)
        tgt = []
        for g, b, t in feat_blocks(16, 2, 8, tn, X0):
            u = act(lambda e, b=b, g=g: e.activation(GT[:, g, :], b.t[:, 0:N2], ACT.Sigmoid, bias=vcol("b_gates", g)), t)
            b.free = [u]
            tgt.append(u)
            if g % 4 == 0:
                dft_channels(g // 4)
            if g % 4 == 2:
                dft_positions(g // 4)
        op("act", lambda e: e.preload_act_table_set("natural_log_exp_and_others"), [], inc=False)
        tga = []
        for m, b, t in feat_blocks(8, 4, 4, tft, X0, FT):
            u = dve(lambda e, b=b, m=m: e.tensor_tensor(GT[:, m, :], GT[:, m, :], b.t[:, 0:N2], ALU.mult), t, tgt[m])
            b.free = [u]
            tga.append(u)
        tmg = []
        for m, b, t in feat_blocks(8, 4, 4, tyb, X0, YB):
            u = dve(lambda e, b=b, m=m: e.tensor_tensor(GT[:, 8 + m, :], GT[:, 8 + m, :], b.t[:, 0:N2], ALU.mult), t,
                    tgt[8 + m])
            b.free = [u]
            u = dve(lambda e, m=m: e.tensor_tensor(GT[:, m, :], GT[:, m, :], GT[:, 8 + m, :], ALU.add), u, tga[m])
            tmg.append([split(GT[:, m, :], MG[:, m, :], 0, u)])
        tmx = []
        cn = ColNorm()
        for g, b, t in feat_blocks(8, 2, 8, tmg, X0, MG):
            if g:
                cn.add()
            u = cn.square(b.t[:, 0:N2], t)
            u = act(lambda e, b=b, g=g: e.activation(GT[:, 8 + g, :], b.t[:, 0:N2], ACT.Copy, scale=vcol("g_mix_post", g)), u)
            b.free = [u]
            tmx.append(u)
        cn.add()
        tr_ = cn.done()
        th2 = []
        cn = ColNorm()
        for k in range(8):
            u = dve(lambda e, k=k: e.tensor_tensor(GT[:, 8 + k, :], GT[:, 8 + k, :], RS[:, 0:N2], ALU.mult), tr_, tmx[k])
            u = dve(lambda e, k=k: e.tensor_tensor(HT[:, k, X0:L2], HT[:, k, X0:L2], GT[:, 8 + k, :], ALU.add), u, *t_ht)
            th2.append(u)
            cn.square(HT[:, k, X0:L2], u)
            cn.add()
        tr_ = cn.done(u)
        tn = norm_cols("g_ffn_pre", X0, [tr_])
        t_h = []

        def residual_back(tt, c):
            b = take()
            for m in range(4):
                t = tr(b.t[:, m * P:m * P + P], HT[:, c * 4 + m, META + tt * P:META + tt * P + P], ident,
                       th2 + b.free, inc=(m == 3))
            u = act(lambda e: e.activation(h[:, tt, c * 512:c * 512 + 512], b.t[:, :], ACT.Copy), t)
            b.free = [u]
            t_h.append(u)

        A = Area("e")
        A.at = o_ffn
        ffp = A.pair(22 * S)
        A(64)
        ff = ffp.view("p (k t) -> p k t", k=22)
        UPB = [[A(S), A(S)] for _ in range(4)]
        gp = A(D)
        s_gp = sem("s_gp")
        dma(lambda e: e.dma_start(gp, GP), tn[7], s_gp)
        up_free = [[] for _ in range(4)]
        tf = []
        op("act", lambda e: e.preload_act_table_set("gelu_apprx_tanh_and_others"), [*tn[7]], inc=False)
        prods = {}

        def ff_mul(n):
            x, y, a, v = prods[n]
            u = dve(lambda e: e.tensor_tensor(x, x, y, ALU.mult), a, v)
            prods[n] = act(lambda e: e.activation(ff.hi[:, n, :], x, ACT.Copy), u)

        def ff_rest(n):
            x = UPB[n % 4][0]
            u = dve(lambda e: e.tensor_tensor(ff.lo[:, n, :], x, ff.hi[:, n, :].bitcast(F32), ALU.subtract), prods[n])
            up_free[n % 4] = [u]
            tf.append(u)

        for n in range(22):
            w, tk, i = use(8)
            bufs = UPB[n % 4]
            us = []
            for av in range(2):
                b, t = proj_feat(w, av * P, tn, tk, X0)
                ch = av * 22 + n
                o = bufs[av]
                u = act(lambda e, b=b, ch=ch, o=o: e.activation(o, b.t[:, 2:N2], ACT.Identity,
                                                                bias=vcol("conv_b_ffn", ch),
                                                                scale=vcol("conv_w_ffn", 44 + ch)), t, *up_free[n % 4])
                u = dve(lambda e, b=b, ch=ch, o=o: e.scalar_tensor_tensor(
                    out=o, in0=b.t[:, 1:N2 - 1], scalar=vcol("conv_w_ffn", ch), in1=o, op0=ALU.mult, op1=ALU.add), u)
                u = dve(lambda e, b=b, ch=ch, o=o: e.scalar_tensor_tensor(
                    out=o[:, 0:S - 1], in0=b.t[:, 3:N2], scalar=vcol("conv_w_ffn", 88 + ch), in1=o[:, 0:S - 1],
                    op0=ALU.mult, op1=ALU.add), u)
                b.free = [u]
                us.append(u)
                if av == 0 and n:
                    ff_mul(n - 1)
            released[i] = t
            a = act(lambda e, o=bufs[0]: e.activation(o, o, ACT.Gelu_apprx_tanh), us[0])
            prods[n] = (bufs[0], bufs[1], a, us[1])
            if n:
                ff_rest(n - 1)
            if 1 <= n <= 4:
                residual_back((n - 1) // 2, (n - 1) % 2)
        ff_mul(21)
        ff_rest(21)
        op("act", lambda e: e.preload_act_table_set("natural_log_exp_and_others"), [tf[21]], inc=False)
        bs = out_tok(lambda k: ff[:, k, :], 11, lambda k: [tf[k]], 22)
        for tt in range(2):
            us = []
            for c in range(2):
                us.append(act(lambda e, tt=tt, c=c: e.activation(xn[:, tt, c * 512:c * 512 + 512], bs[2 * tt + c].t[:, :],
                                                                 ACT.Square, accum_out=small[:, 240 + 2 * tt + c:241 + 2 * tt + c]),
                              bs[2 * tt + c].token))
            u = dve(lambda e, tt=tt: e.tensor_tensor(small[:, 244 + tt:245 + tt], small[:, 240 + 2 * tt:241 + 2 * tt],
                                                     small[:, 241 + 2 * tt:242 + 2 * tt], ALU.add), *us)
            rs = small[:, 246 + tt:247 + tt]
            u = inv_rms(small[:, 244 + tt:245 + tt], rs, D, u)
            for c in range(2):
                o = xn[:, tt, c * 512:c * 512 + 512]
                v = dve(lambda e, tt=tt, c=c, o=o, rs=rs: e.scalar_tensor_tensor(
                    out=o, in0=bs[2 * tt + c].t[:, :], scalar=rs, in1=gp[:, c * 512:c * 512 + 512], op0=ALU.mult,
                    op1=ALU.mult), u, (s_gp, 16))
                v = dve(lambda e, tt=tt, c=c, o=o: e.tensor_tensor(o, o, h[:, tt, c * 512:c * 512 + 512], ALU.add), v, *t_h)
                dma(lambda e, tt=tt, c=c, o=o: e.dma_start(OUT[tt * P:tt * P + P, c * 512:c * 512 + 512], o), [v], s_o)
        assert used[0] == len(sizes)

        def run(eng, name):
            seen = {}
            for waits, fn, inc in queues[name]:
                need = {}
                for tok in waits:
                    s, v = tok
                    need[id(s)] = (s, max(v, need.get(id(s), (s, 0))[1]))
                for key, (s, v) in need.items():
                    if seen.get(key, 0) < v:
                        eng.wait_ge(s, v)
                        seen[key] = v
                ins = fn(eng)
                if inc:
                    ins.then_inc(*inc)

        block = ctx.enter_context(nc.Block())

        @block.sync
        def _(eng):
            run(eng, "sp")
            eng.wait_ge(s_o, 64)

        @block.scalar
        def _(eng):
            run(eng, "act")

        @block.vector
        def _(eng):
            run(eng, "dve")

        @block.gpsimd
        def _(eng):
            run(eng, "pool")

        @block.tensor
        def _(eng):
            run(eng, "pe")


def weight_stream(a):
    out = []

    def kn(w, k0=0, k1=None):
        n = w.shape[1]
        return w.reshape(-1, P, n).transpose(1, 0, 2)

    def put(t):
        out.append(np.ascontiguousarray(t).reshape(-1))

    def cols(w, lo, hi):
        put(kn(w[:, lo:hi]))

    def rows(w, per=2):
        k = w.shape[0] // P
        for i in range(0, k, per):
            put(kn(w[i * P:(i + per) * P]))

    def quarter(w, lo, hi):
        for i in range(2):
            put(kn(w[i * 512:i * 512 + 512, lo:hi]))

    w = a["w_in_ab"][0]
    quarter(w, 1536, 2048)
    put(np.concatenate([kn(w[:, 3144:3160]), kn(w[:, 2048:2120])], axis=2))
    cols(w, 2120, 2376)
    cols(w, 2376, 2632)
    for c in (0, 512, 1024, 2632, 3160):
        quarter(w, c, c + 512)
    rows(a["w_out_ab"][0])

    def mlp(l):
        for i in range(16):
            cols(a["w_up"][l], i * 256, i * 256 + 256)
        rows(a["w_down"][l])

    mlp(0)
    for i in (0, 2, 1, 3, 4, 5):
        quarter(a["w_in_c"][0], i * 512, i * 512 + 512)
    rows(a["w_out_c"][0])
    mlp(1)
    w = a["w_in_2"][0]
    for c in (0, 512, 1536, 1024, 2048, 2560, 3072, 3584):
        cols(w, c, c + 256)
        cols(w, c + 256, c + 512)
    for w in (a["w_fourier_2"][0], a["w_conv_out_2"][0]):
        cols(w, 0, 512)
        cols(w, 512, 1024)
    w = a["w_out_2"][0]
    for c in range(0, 1024, 256):
        cols(w, c, c + 256)
    w = a["w_up_2"][0]
    for i in range(22):
        put(np.concatenate([kn(w[:, i * P:i * P + P]), kn(w[:, 2816 + i * P:2816 + i * P + P])], axis=2))
    rows(a["w_down_2"][0])
    return np.concatenate(out)


def vectors(a):
    v = np.zeros((P, NVEC), np.float32)

    def put(name, x):
        o, n = VEC[name]
        v[:, o:o + n] = np.asarray(x).reshape(-1, P).T

    for l in range(2):
        put(f"g_mix{l}", a["g_mix"][l])
        put(f"g_ffn{l}", a["g_ffn"][l])
    put("b_gate", a["b_gate"][0])
    put("g_gla", a["g_gla"][0])
    put("gq_c", a["gq_c"][0])
    put("gk_c", a["gk_c"][0])
    put("g_mix_pre", a["g_mix_pre_2"][0])
    put("b_gates", a["b_gates_2"][0])
    put("conv_w_mix", a["conv_w_mix_2"][0])
    put("conv_b_mix", a["conv_b_mix_2"][0])
    put("g_mix_post", a["g_mix_post_2"][0])
    put("g_ffn_pre", a["g_ffn_pre_2"][0])
    put("conv_w_ffn", a["conv_w_ffn_2"][0])
    put("conv_b_ffn", a["conv_b_ffn_2"][0])
    v[:, VEC["ident"][0]:VEC["ident"][0] + P] = np.eye(P, dtype=np.float32)
    v[:, VEC["eps"][0]] = EPS
    for name, key in (("gq_row", "gq_a"), ("gk_row", "gk_a")):
        o, n = VEC[name]
        v[:, o:o + n] = np.broadcast_to(a[key][0][None, :], (P, P))
    return v


def kernel(**inputs):
    import concourse.bacc as bacc
    from concourse.bass_utils import run_bass_kernel_spmd

    a = {k: np.asarray(v) for k, v in inputs.items()}
    c, dlx, cm, tri = constants()
    arrays = {
        "w_stream": weight_stream(a),
        "vectors": vectors(a),
        "consts": c,
        "consts_x": dlx,
        "consts_m": cm,
        "tri": tri,
        "x_rows": np.ascontiguousarray(a["x"][0]),
        "meta_rows": np.ascontiguousarray(a["meta_tokens_2"]),
        "gate_up": np.ascontiguousarray(a["w_gate_up"][0]),
        "g_post": np.ascontiguousarray(np.broadcast_to(a["g_ffn_post_2"][0][None, :], (P, D))),
    }
    nc = bacc.Bacc("TRN2", target_bir_lowering=False, num_devices=1)
    args = [nc.dram_tensor(k, v.shape, F32, kind="ExternalInput").ap() for k, v in arrays.items()]
    out = nc.dram_tensor("out_rows", (S, D), F32, kind="ExternalOutput").ap()
    block_kernel(nc, *args, out)
    r = run_bass_kernel_spmd(nc, [arrays], core_ids=[0])
    return r.results[0]["out_rows"].reshape(1, S, D)
```

```python
from contextlib import ExitStack

import numpy as np

import concourse.bass as bass
from concourse import mybir

ALU = mybir.AluOpType
ACT = mybir.ActivationFunctionType
AX = mybir.AxisListType
F32 = mybir.dt.float32
F32R = mybir.dt.float32r

P = 128
D = 1024
S = 256
EPS = 1e-6
META = 16
L2 = META + S
X0 = 14
N2 = L2 - X0
SLOT = 2048
NSLOT = 3
AHEAD = 2
BIGNEG = -1.0e30

VEC_COLS = [
    ("g_ffn0", 8), ("g_mix1", 8), ("g_ffn1", 8), ("b_gate", 2), ("g_gla", 1),
    ("gq_c", 1), ("gk_c", 1), ("g_mix_pre", 8), ("b_gates", 16), ("conv_w_mix", 12),
    ("conv_b_mix", 4), ("g_mix_post", 8), ("g_ffn_pre", 8), ("conv_w_ffn", 132), ("conv_b_ffn", 44),
    ("gq_row", 128), ("gk_row", 128), ("g_mix0", 8), ("eps", 1),
    ("ident", 128),
]
CST_COLS = [
    ("ones", 128), ("cosA", 32), ("sinA", 32), ("cosI", 16), ("sinI", 16),
    ("inval", 512), ("gmask", 1024), ("smask", 384), ("dftc", 256),
]


def offsets(cols):
    out, at = {}, 0
    for name, n in cols:
        out[name] = (at, n)
        at += n
    return out, at


VEC, NVEC = offsets(VEC_COLS)
CST, NCST = offsets(CST_COLS)


def tile_sizes():
    n = [2048] * 2 + [704] + [2048] * 12
    n += [2048] * (4 + 32)
    n += [2048] * (12 + 4 + 32)
    n += [2048] * (16 + 2 + 2 + 4 + 22 + 11)
    return n


def constants():
    c = np.zeros((P, NCST), np.float32)

    def put(name, a):
        o, n = CST[name]
        c[:, o:o + n] = a.reshape(P, n)

    put("ones", np.ones((P, P), np.float32))
    pos = np.arange(S, dtype=np.float32)
    for tag, rot in (("A", 32), ("I", 16)):
        half = rot // 2
        inv = np.power(np.float32(500000.0), -np.arange(half, dtype=np.float32) * np.float32(2.0) / np.float32(rot))
        ang = (pos[:, None] * inv[None, :].astype(np.float32)).astype(np.float32).astype(np.float64)
        put("cos" + tag, np.cos(ang).astype(np.float32).reshape(2, P, half).transpose(1, 0, 2))
        put("sin" + tag, np.sin(ang).astype(np.float32).reshape(2, P, half).transpose(1, 0, 2))
    t = np.arange(S)
    limit = (t // 64 + 1) * 64
    inval = np.where(t[None, :] < limit[:, None], 0.0, -1.0e37).astype(np.float32)
    put("inval", inval.reshape(2, P, S).transpose(1, 0, 2))
    s, t = np.arange(P)[:, None], np.arange(P)[None, :]
    masks = []
    for hs in (64, 32, 16, 8, 4, 2, 1):
        masks.append((s // (2 * hs) == t // (2 * hs)) & (s % (2 * hs) < hs) & (t % (2 * hs) >= hs))
    masks.append(s == t)
    put("gmask", np.stack(masks, 1).astype(np.float32))
    tri = np.where(s < t, 0.0, BIGNEG).astype(np.float32)
    put("smask", np.concatenate([tri, np.zeros((P, P), np.float32), tri], 1))
    k = np.outer(np.arange(P), np.arange(P)) % P
    scale = 1.0 / np.sqrt(L2 * P)
    put("dftc", np.concatenate([np.cos(2 * np.pi * k / P), np.sin(2 * np.pi * k / P)], 1).astype(np.float32))
    k = np.outer(np.arange(L2), np.arange(L2)) % L2
    dl = np.stack([np.cos(2 * np.pi * k / L2), -np.sin(2 * np.pi * k / L2)], 1) * scale
    dl = dl.astype(np.float32)
    dlx = np.ascontiguousarray(dl[META:].reshape(2, P, 2, L2).transpose(1, 0, 2, 3).reshape(P, 4 * L2))
    tri_s = (s >= t).astype(np.float32)
    return c, dlx, np.ascontiguousarray(dl[:META].reshape(META, 2 * L2)), tri_s


class Bank:

    clock = 0

    def __init__(self, t):
        self.t = t
        self.held = False
        self.free = []

    @property
    def free(self):
        return self.tokens

    @free.setter
    def free(self, tokens):
        self.tokens = tokens
        self.touch()

    def touch(self):
        Bank.clock += 1
        self.used = Bank.clock


class Pair:

    def __init__(self, hi, lo):
        self.hi = hi
        self.lo = lo

    def __getitem__(self, i):
        return Pair(self.hi[i], self.lo[i])

    def view(self, pattern, **kw):
        return Pair(self.hi.rearrange(pattern, **kw), self.lo.rearrange(pattern, **kw))


def block_kernel(nc, W, V, C, DL, CM, TRI, X, MT, WG, GP, OUT):
    ctx = ExitStack()
    with ctx:
        base = -(-nc.sbuf_base // 64) * 64
        end = nc.sbuf_usable_end
        ctx.enter_context(nc.sbuf_tensor("arena", [P, (end - base) // 4 - 32], F32))
        place = [base]

        def at(name, n, off, dt=F32):
            assert off + 4 * n <= end, (name, off + 4 * n, end)
            return nc.alloc_sbuf_tensor_at(name, [P, n], dt, offset=off)[:, :]

        def sb(name, n, dt=F32):
            off = place[0]
            place[0] += -(-4 * n // 32) * 32
            return at(name, n, off, dt)

        def sem(name):
            return ctx.enter_context(nc.semaphore(name))

        queues = {k: [] for k in ("pe", "act", "dve", "pool", "sp")}
        sems = {k: sem("s_" + k) for k in ("pe", "act", "dve", "pool")}
        count = {k: 0 for k in sems}

        def op(e, fn, waits, inc=True):
            tok = None
            if inc:
                count[e] += 1
                tok = (sems[e], count[e])
            queues[e].append((list(waits), fn, (sems[e], 1) if inc else None))
            return tok

        def dve(fn, *waits):
            return op("dve", fn, waits)

        def act(fn, *waits):
            return op("act", fn, waits)

        def pool(fn, *waits):
            return op("pool", fn, waits)

        def dma(fn, waits, s, q="sp"):
            queues[q].append((list(waits), fn, (s, 16)))

        def mm(out, lhsT, rhs, start, stop, waits=(), inc=False):
            return op("pe", lambda e: e.matmul(out, lhsT, rhs, start=start, stop=stop), waits, inc)

        def mm3(out, lhsT, rhs, start, stop, waits=(), inc=False):
            mm(out, lhsT.hi, rhs.hi, start, False, waits)
            mm(out, lhsT.hi, rhs.lo, False, False)
            return mm(out, lhsT.lo, rhs.hi, False, stop, (), inc)

        def tr(out, in_, idn, waits=(), inc=False):
            return op("pe", lambda e: e.transpose(out, in_, idn), waits, inc)

        banks = [Bank(ctx.enter_context(nc.psum_tensor(f"bank{i}", [P, 512], F32))) for i in range(8)]

        def take(hold=False):
            b = min((b for b in banks if not b.held), key=lambda b: b.used)
            b.held = hold
            b.touch()
            return b

        raw = [sb(f"raw{i}", SLOT) for i in range(NSLOT)]
        whi = [sb(f"whi{i}", SLOT, F32R) for i in range(NSLOT)]
        wlo = [sb(f"wlo{i}", SLOT, F32R) for i in range(NSLOT)]
        s_raw = [sem(f"s_raw{i}") for i in range(NSLOT)]
        split_done = []
        released = {}
        sizes = tile_sizes()
        starts = [0]
        for n in sizes:
            starts.append(starts[-1] + n * P)
        used = [0]

        def stage(i):
            j, n = i % NSLOT, sizes[i]
            src = W[starts[i]:starts[i + 1]].rearrange("(p n) -> p n", p=P)
            dma(lambda e: e.dma_start(raw[j][:, 0:n], src), split_done[i - NSLOT] if i >= NSLOT else [], s_raw[j])

        def split_tile(i):
            j, n = i % NSLOT, sizes[i]
            landed = (s_raw[j], 16 * (i // NSLOT + 1))
            free = [released[i - NSLOT]] if i >= NSLOT else []
            if i < 2:
                ds = []
                for c in range(0, n, 512):
                    landed = (s_w if i == 0 and c >= 1024 else s_raw[j], 16)
                    a = act(lambda e, c=c: e.activation(whi[j][:, c:c + 512], raw[j][:, c:c + 512], ACT.Copy), landed)
                    ds.append(dve(lambda e, c=c: e.tensor_tensor(wlo[j][:, c:c + 512], raw[j][:, c:c + 512],
                                                                 whi[j][:, c:c + 512].bitcast(F32), ALU.subtract),
                                  a, landed))
                split_done.append(ds)
                stage(i + NSLOT)
                return
            a = act(lambda e: e.activation(whi[j][:, 0:n], raw[j][:, 0:n], ACT.Copy), landed, *free)
            m = n // 2
            split_done.append([
                rest(lambda e, lo=lo, hi=hi: e.tensor_tensor(wlo[j][:, lo:hi], raw[j][:, lo:hi], whi[j][:, lo:hi].bitcast(F32),
                                                             ALU.subtract), a, landed, *free)
                for rest, lo, hi in ((dve, 0, m), (pool, m, n))])
            if i + NSLOT < len(sizes):
                stage(i + NSLOT)

        def use(k):
            i = used[0]
            used[0] += 1
            while len(split_done) < min(i + 1 + AHEAD, len(sizes)):
                split_tile(len(split_done))
            j, n = i % NSLOT, sizes[i]
            w = Pair(whi[j][:, 0:n], wlo[j][:, 0:n]).view("p (k n) -> p k n", k=k)
            return w, split_done[i], i

        h = sb("h", 2 * D).rearrange("p (t n) -> p t n", t=2)
        nrm = Pair(sb("nhi", 8 * L2, F32R), sb("nlo", 8 * L2, F32R))
        nTa = nrm[:, 0:8 * S].view("p (k t) -> p k t", k=8)
        nT2 = nrm.view("p (k t) -> p k t", k=8)
        o_xn = place[0]
        xn_ = sb("xn", 8 * N2)
        xn = xn_[:, 0:2 * D].rearrange("p (t n) -> p t n", t=2)
        o_clo = place[0]
        clo_ = sb("clo", 8 * S, F32R)
        place[0] = o_clo + -(-8 * N2 * 4 // 32) * 32
        catT = Pair(at("chi", 8 * S, o_xn, F32R), clo_).view("p (k t) -> p k t", k=8)
        vec = sb("vec", NVEC)
        cst = sb("cst", NCST)
        tri = sb("tri_sb", P)
        small = sb("small", 256)
        rows = sb("rows", 32)
        room = place[0]

        class Area:

            def __init__(self, tag):
                self.at = room
                self.tag = tag
                self.n = 0

            def __call__(self, n, dt=F32):
                self.n += 1
                a = at(f"{self.tag}{self.n}", n, self.at, dt)
                self.at += -(-4 * n // 32) * 32
                return a

            def pair(self, n):
                return Pair(self(n, F32R), self(n, F32R))

        def vcol(name, i=0, n=1):
            o = VEC[name][0] + i
            return vec[:, o:o + n]

        def const(name):
            o, n = CST[name]
            return cst[:, o:o + n]

        ident = vcol("ident", 0, P)
        eps = vcol("eps")

        s_c = sem("s_c")
        s_o = sem("s_o")
        s_g = sem("s_g")
        s_d = sem("s_d")
        A = Area("a")
        wg = A(256)[0:16, :]
        s_v = sem("s_v")
        s_x = [[sem(f"s_x{tt}{c}") for c in range(2)] for tt in range(2)]
        o_id = VEC["g_mix0"][0]
        s_i = sem("s_i")
        s_w = sem("s_w")
        dma(lambda e: e.dma_start(vec[:, o_id:NVEC], V[:, o_id:NVEC]), [], s_i, "act")
        TX = [[[(s_x[tt][c], 16)] for c in range(2)] for tt in range(2)]
        TI = (s_i, 16)
        TV = (s_v, 16)
        first = W[0:starts[1]].rearrange("(p n) -> p n", p=P)
        for c in range(2):
            for tt in range(2):
                dma(lambda e, tt=tt, c=c: e.dma_start(h[:, tt, c * 512:c * 512 + 512],
                                                      X[tt * P:tt * P + P, c * 512:c * 512 + 512]), [], s_x[tt][c])
            dma(lambda e, c=c: e.dma_start(raw[0][:, c * 1024:c * 1024 + 1024], first[:, c * 1024:c * 1024 + 1024]), [],
                s_w if c else s_raw[0])
            if c == 0:
                dma(lambda e: e.dma_start(vec[:, 0:o_id], V[:, 0:o_id]), [], s_v, "act")
        for i in range(1, NSLOT):
            stage(i)
        dma(lambda e: e.dma_start(cst, C), [], s_c)
        dma(lambda e: e.dma_start(wg, WG), [], s_c)
        dma(lambda e: e.dma_start(tri, TRI), [], s_c)
        TC = (s_c, 48)

        def inv_rms(ss, rs, n, *waits):
            t = act(lambda e: e.activation(rs, ss, ACT.Ln, bias=eps, scale=1.0 / n), TV, *waits)
            return act(lambda e: e.activation(rs, rs, ACT.Exp, scale=-0.5), t)

        def bc(ap, shape):
            return ap.to_broadcast(shape)

        def evac_T(b, q, gname, dst, c0, out):
            xs = [b.t[:, 0:256], b.t[:, 256:512]]
            gain = TI if gname == "g_mix0" else TV
            for kk, x in enumerate(xs):
                o = dst[:, 2 * q + kk, c0:c0 + S]
                u = act(lambda e, k=2 * q + kk, x=x, o=o: e.activation(o.hi, x, ACT.Copy, scale=vcol(gname, k)), b.token, gain)
            for kk, x in enumerate(xs):
                o = dst[:, 2 * q + kk, c0:c0 + S]
                v = dve(lambda e, k=2 * q + kk, x=x, o=o: e.scalar_tensor_tensor(
                    out=o.lo, in0=x, scalar=vcol(gname, k), in1=o.hi.bitcast(F32),
                    op0=ALU.mult, op1=ALU.subtract), u, gain)
                out.append([v])
            drop(b, v)

        def norm_T(gname, ready, dst, c0, between):
            ts = []
            for tt in range(2):
                a = act(lambda e, tt=tt: e.activation(xn[:, tt, :], h[:, tt, :], ACT.Square,
                                                      accum_out=small[:, tt:tt + 1]), *ready[tt])
                r = inv_rms(small[:, tt:tt + 1], small[:, 2 + tt:3 + tt], D, a)
                ts.append(dve(lambda e, tt=tt: e.tensor_scalar(xn[:, tt, :], h[:, tt, :], small[:, 2 + tt:3 + tt],
                                                               None, ALU.mult), r))
            out = []
            between()
            bs = [take(True) for _ in range(4)]
            for tt in range(2):
                for q, b in enumerate(bs):
                    for kk in range(2):
                        t = tr(b.t[:, kk * 256 + tt * P:kk * 256 + tt * P + P],
                               xn[:, tt, (2 * q + kk) * P:(2 * q + kk + 1) * P], ident,
                               [ts[tt], TI] + b.free, inc=(kk == 1))
                    b.token = t
            for q, b in enumerate(bs):
                evac_T(b, q, gname, dst, c0, out)
            return out

        class Turn:

            made = 0

            def __init__(self, gname):
                self.gname = gname
                self.tn = []
                c = 8 * Turn.made
                Turn.made += 1
                self.ss, self.lnrs, self.rs, self.rs2 = (rows[:, c + 2 * i:c + 2 * i + 2] for i in range(4))

            def half(self, c, ready):
                bs = [take(True), take(True)]
                for tt in range(2):
                    for i, b in enumerate(bs):
                        for kk in range(2):
                            k = 4 * c + 2 * i + kk
                            t = tr(b.t[:, kk * 256 + tt * P:kk * 256 + tt * P + P], h[:, tt, k * P:k * P + P], ident,
                                   ready[tt][c] + [TI] + b.free, inc=(kk == 1))
                        b.token = t
                for i, b in enumerate(bs):
                    evac_T(b, 2 * c + i, self.gname, nTa, 0, self.tn)

            def rest(self, ready):
                self.half(1, ready)
                self.stats(ready)

            def stats(self, ready):
                us = []
                for tt in range(2):
                    us.append(act(lambda e, tt=tt: e.activation(xn[:, tt, :], h[:, tt, :], ACT.Square,
                                                                accum_out=self.ss[:, tt:tt + 1]),
                                  *ready[tt][0], *ready[tt][1]))
                u = act(lambda e: e.activation(self.ss, self.ss, ACT.Ln, bias=eps, scale=1.0 / D), TV, *us)
                a = act(lambda e: e.activation(self.lnrs, self.ss, ACT.Copy, scale=-0.5), u)
                b = act(lambda e: e.activation(self.rs, self.ss, ACT.Exp, scale=-0.5), u)
                c = act(lambda e: e.activation(self.rs2, self.ss, ACT.Exp, scale=-1.0), u)
                self.trs = [a, b, c]
                return self

        def inv_rms_row(ss, n, turn, tt, *waits):
            t = act(lambda e: e.activation(ss, ss, ACT.Ln, bias=eps, scale=1.0 / n), TV, *waits)
            return act(lambda e: e.activation(ss, ss, ACT.Exp, bias=turn.lnrs[:, tt:tt + 1], scale=-0.5), t, *turn.trs)

        def proj_tok(tn, between=None, inner=None):
            bs = [take(True), take(True)]
            for half in range(2):
                w, tk, i = use(4)
                for tt in range(2):
                    for kk in range(4):
                        k = half * 4 + kk
                        t = mm3(bs[tt].t[:, :], nTa[:, k, tt * P:tt * P + P], w[:, kk, :], k == 0, k == 7,
                                (tk if i > 1 else tk[kk:kk + 1]) + tn[k] + bs[tt].free, inc=(kk == 3))
                    bs[tt].token = t
                    if half == 0 and tt == 0 and inner:
                        inner()
                released[i] = t
                if half == 0 and between:
                    between()
            return [(b, b.token) for b in bs]

        def drop(b, *toks):
            b.free = list(toks)
            b.held = False

        def out_tok(lhs, ntile, ready, n_k, before=None, order=(0, 1, 2, 3), done=None, mid=None):
            bs = [take(True) for _ in range(4)]
            for it in range(ntile):
                if before:
                    before(it)
                w, tk, i = use(2)
                last = it == ntile - 1
                seq = [(kk, j) for j in order for kk in range(2)] if last else [(kk, j) for kk in range(2) for j in range(4)]
                for kk, j in seq:
                    k = it * 2 + kk
                    tt, c = j // 2, j % 2
                    if last and mid and (kk, j) == (0, order[3]):
                        mid()
                    t = mm3(bs[j].t[:, :], lhs(k)[:, tt * P:tt * P + P], w[:, kk, c * 512:c * 512 + 512],
                            k == 0, k == n_k - 1, tk + ready(k) + bs[j].free, inc=(kk == 1))
                    bs[j].token = t
                    if last and done and kk == 1:
                        done(j, bs[j])
                released[i] = t
            return bs

        def out_h(lhs, ntile, ready, n_k, gname, before=None, factor=None):
            turn = Turn(gname) if gname else None
            th = [[None, None], [None, None]]

            def done(j, b):
                tt, c = j // 2, j % 2
                o = h[:, tt, c * 512:c * 512 + 512]
                if factor:
                    u = dve(lambda e: e.scalar_tensor_tensor(out=o, in0=b.t[:, :], scalar=factor.rs2[:, tt:tt + 1], in1=o,
                                                             op0=ALU.mult, op1=ALU.add), b.token, *factor.trs)
                else:
                    u = dve(lambda e: e.tensor_tensor(o, o, b.t[:, :], ALU.add), b.token)
                drop(b, u)
                th[tt][c] = [u]

            out_tok(lhs, ntile, ready, n_k, before, (0, 2, 1, 3), done, (lambda: turn.half(0, th)) if turn else None)
            return th, turn

        def cat_evac(b, hd, t):
            o, x = catT[:, hd, :], b.t[:, 0:256]
            u = act(lambda e: e.activation(o.hi, x, ACT.Copy), t)
            u = dve(lambda e: e.tensor_tensor(o.lo, x, o.hi.bitcast(F32), ALU.subtract), u)
            b.free = [u]
            return u

        def mlp(turn, ready, tag, gnext, within=None, after_up=None):
            A = Area(tag)
            ffp = A.pair(32 * S)
            sq = [A(512), A(512)]
            sq_free = [[], []]
            ff = ffp.view("p (k t) -> p k t", k=32)
            tn = turn.tn
            tf = []

            def rest(m, a):
                o = ffp[:, m * 512:m * 512 + 512]
                u = dve(lambda e, x=sq[m % 2]: e.tensor_tensor(x, x, x, ALU.mult), a)
                u = dve(lambda e, o=o, x=sq[m % 2]: e.tensor_tensor(o.lo, x, o.hi.bitcast(F32), ALU.subtract), u)
                sq_free[m % 2] = [u]
                tf.extend([u, u])

            last = None
            for m in range(16):
                w, tk, i = use(8)
                x = sq[m % 2]
                if m == 0:
                    bs = [take(True), take(True)]
                    for n in range(4):
                        b, c = bs[n % 2], n % 2
                        for k in range(n // 2 * 4, n // 2 * 4 + 4):
                            t = mm3(b.t[:, 0:256], w[:, k, c * P:c * P + P], nTa[:, k, :], k == 0, k == 7,
                                    tk + tn[k] + b.free, inc=(k == 7))
                        b.token = t
                        if n == 0:
                            turn.rest(ready)
                    for c, b in enumerate(bs):
                        u = act(lambda e, b=b, c=c, x=x: e.activation(x[:, c * 256:c * 256 + 256], b.t[:, 0:256], ACT.Relu),
                                b.token)
                        drop(b, u)
                else:
                    b = take()
                    for c in range(2):
                        for k in range(8):
                            t = mm3(b.t[:, c * 256:c * 256 + 256], w[:, k, c * P:c * P + P], nTa[:, k, :], k == 0, k == 7,
                                    tk + tn[k] + b.free, inc=(k == 7))
                    u = act(lambda e, b=b, x=x: e.activation(x, b.t[:, :], ACT.Relu), t, *sq_free[m % 2])
                    b.free = [u]
                released[i] = t
                a = act(lambda e, m=m, x=sq[m % 2]: e.activation(ffp.hi[:, m * 512:m * 512 + 512], x, ACT.Square), u)
                if last:
                    rest(*last)
                last = (m, a)
                if m == 6 and within:
                    within()
            rest(*last)
            if after_up:
                after_up(t)
            return out_h(lambda k: ff[:, k, :], 16, lambda k: [tf[k]], 32, gnext, None, turn)

        IQ = A(2 * 576)
        IKD = A(256)
        IQT = A(1024).rearrange("p (b t) -> p b t", b=4)
        IKT = A(256)
        RL = A(1024).rearrange("p (j n) -> p j n", j=2)
        SC = A(512).rearrange("p (t n) -> p t n", t=2)
        SEL = A(512)
        SELv = SEL.rearrange("p (t n) -> p t n", t=2)
        QKT = A(2048).rearrange("p (k t) -> p k t", k=8)
        VA = A(1024).rearrange("p (t n) -> p t n", t=2)
        VB = A(1024).rearrange("p (t n) -> p t n", t=2)
        OG = A(1024).rearrange("p (t n) -> p t n", t=2)
        QK0 = A(1024).rearrange("p (j n) -> p j n", j=2)
        BB = A(512)
        DE = A(512)
        SS = A(1024).rearrange("p (j n) -> p j n", j=2)
        PT = A(768).rearrange("p (j n) -> p j n", j=2)
        AM = A(512)
        AM2 = IQ[:, 0:256]
        YN = A(1024).rearrange("p (j n) -> p j n", j=2)
        DEs = [DE, A(512)]
        RT = SS.rearrange("p j n -> p (j n)")
        GL = A(256)
        DG = GL
        RSB = A(256)
        IQv = IQ.rearrange("p (t h d) -> p t h d", t=2, h=9)
        QA = xn.rearrange("p t (h d) -> p t h d", h=8)
        QKE = A(8 * 512).rearrange("p (l n) -> p l n", l=8)

        op("act", lambda e: e.preload_act_table_set("natural_log_exp_and_others"), [], inc=False)
        tam = pool(lambda e: e.memset(AM, 0.0))
        turn = Turn("g_mix0")
        turn.half(0, TX)
        split_tile(0)
        turn.half(1, TX)
        split_tile(1)
        turn.stats(TX)
        tn, ra = turn.tn, turn
        ones = const("ones")
        tdg = [dve(lambda e, tt=tt: e.tensor_scalar(DG[:, tt * P:tt * P + P], ident, ra.rs[:, tt:tt + 1], None, ALU.mult),
                   TI, *ra.trs) for tt in range(2)]

        def row_factors():
            b = take()
            t = mm(b.t[:, 0:256], ones, DG, True, True, [*tdg, TC] + b.free, inc=True)
            u = act(lambda e: e.activation(RSB, b.t[:, 0:256], ACT.Copy), t)
            b.free = [u]
            return u

        cp = []
        for tt, (b, t) in enumerate(proj_tok(tn)):
            u = act(lambda e, tt=tt, b=b: e.activation(IQ[:, tt * 576:tt * 576 + 512], b.t[:, :], ACT.Copy,
                                                       scale=ra.rs[:, tt:tt + 1]), t, *ra.trs)
            drop(b, u)
            cp.append(u)
        trsb = row_factors()
        w, tk, i = use(8)
        IW = small[:, 16:32]
        b = take()
        for k in range(8):
            t = mm3(b.t[0:88, 0:256], w[:, k, :], nTa[:, k, :], k == 0, k == 7, tk + tn[k] + b.free, inc=(k == 7))
        released[i] = t
        tgl = dve(lambda e, b=b: e.tensor_tensor(GL[0:88, :], b.t[0:88, 0:256], RSB[0:88, :], ALU.mult), t, trsb)
        b.free = [tgl]

        def key_turn():
            b = take()
            for tt in range(2):
                t = tr(b.t[:, tt * 88:tt * 88 + 88], GL[0:88, tt * P:tt * P + P], ident[0:88, 0:88], [tgl, TI] + b.free,
                       inc=(tt == 1))
            x = b.t[:, 0:176].rearrange("p (t n) -> p t n", t=2)
            u = act(lambda e: e.activation(IQ.rearrange("p (t n) -> p t n", t=2)[:, :, 512:576], x[:, :, 16:80], ACT.Copy), t)
            v = act(lambda e: e.activation(IW.rearrange("p (t n) -> p t n", t=2), x[:, :, 80:88], ACT.Copy,
                                           scale=8.0 ** -0.5), t)
            b.free = [v]
            return u, v

        tqk = []
        for j in range(2):
            if j == 1:
                tkey, tiw = key_turn()
            b = take()
            w, tk, i = use(8)
            for p in range(2):
                for k in range(8):
                    t = mm3(b.t[:, p * 256:p * 256 + 256], w[:, k, p * P:p * P + P], nTa[:, k, :], k == 0, k == 7,
                            tk + tn[k] + b.free, inc=(k == 7))
            released[i] = t
            u = dve(lambda e, b=b, j=j: e.scalar_tensor_tensor(
                out=QK0[:, j, :].rearrange("p (j t) -> p j t", j=2), in0=b.t[:, :].rearrange("p (j t) -> p j t", j=2),
                scalar=0.125 if j == 0 else 1.0, in1=bc(RSB.rearrange("p (o t) -> p o t", o=1), [P, 2, S]),
                op0=ALU.mult, op1=ALU.mult), t, trsb)
            b.free = [u]
            tqk.append(u)
        def rope(view, H, half, cname, sname, ready):
            cs = bc(const(cname).rearrange("p (t o n) -> p t o n", t=2, o=1), [P, 2, H, half])
            sn = bc(const(sname).rearrange("p (t o n) -> p t o n", t=2, o=1), [P, 2, H, half])
            n = 2 * H * half
            tmp = [RT[:, i * 256:i * 256 + n].rearrange("p (t h n) -> p t h n", t=2, h=H) if n <= 256 else None
                   for i in range(4)]
            x1 = view[:, :, :, 0:half]
            x2 = view[:, :, :, half:2 * half]
            a = dve(lambda e: e.tensor_tensor(tmp[0], x1, cs, ALU.mult), *ready)
            b_ = dve(lambda e: e.tensor_tensor(tmp[1], x2, sn, ALU.mult), *ready)
            c_ = dve(lambda e: e.tensor_tensor(tmp[2], x2, cs, ALU.mult), *ready)
            d_ = dve(lambda e: e.tensor_tensor(tmp[3], x1, sn, ALU.mult), *ready)
            f = dve(lambda e: e.tensor_tensor(x1, tmp[0], tmp[1], ALU.subtract), a, b_, d_)
            g = dve(lambda e: e.tensor_tensor(x2, tmp[2], tmp[3], ALU.add), c_, d_)
            return [f, g]

        tro = rope(IQv, 9, 8, "cosI", "sinI", cp + [tkey, TC])
        tik = []
        for tt in range(2):
            for j in range(2):
                tik.append(dve(lambda e, tt=tt, j=j: e.tensor_copy(IKD[:, tt * P + j * 64:tt * P + j * 64 + 64],
                                                                   IQ[:, tt * 576 + 512:tt * 576 + 576]), *tro))

        b = take()
        for p in range(2):
            t = mm(b.t[:, p * 256:p * 256 + 256], wg[:, p * P:p * P + P], GL[0:16, :], True, True,
                   [tgl, TC] + b.free, inc=True)
        us = []
        for p in range(2):
            us.append(act(lambda e, p=p, b=b: e.activation(BB[:, p * 256:p * 256 + 256], b.t[:, p * 256:p * 256 + 256],
                                                           ACT.Identity, bias=vcol("b_gate", p)), t))
        b.free = us
        u = act(lambda e: e.activation(DE, BB, ACT.Abs), *us)
        u = act(lambda e: e.activation(DE, DE, ACT.Exp, scale=-1.0), u)
        u = act(lambda e: e.activation(DE, DE, ACT.Ln, bias=1.0), u)
        u = dve(lambda e: e.scalar_tensor_tensor(out=DE, in0=BB, scalar=0.0, in1=DE, op0=ALU.min, op1=ALU.subtract), u)
        tb = []
        for p in range(2):
            tb.append(dve(lambda e, p=p: e.tensor_tensor_scan(
                BB[:, p * 256:p * 256 + 256], DE[:, p * 256:p * 256 + 256], DE[:, p * 256:p * 256 + 256], 0.0,
                ALU.add, ALU.bypass), u))

        def level(l, hs):
            nb = 256 // hs
            de = DEs[l % 2]
            bv = BB.rearrange("p (b u s) -> p b u s", u=2, s=hs)
            dv = de.rearrange("p (b u s) -> p b u s", u=2, s=hs)
            mid = bc(bv[:, :, 0, hs - 1:hs], [P, nb, hs])
            free = tlev[l - 2] if l >= 2 else []
            u1 = dve(lambda e: e.tensor_tensor(dv[:, :, 1, :], bv[:, :, 1, :], mid, ALU.subtract), *tb, *free)
            u2 = dve(lambda e: e.tensor_tensor(dv[:, :, 0, :], mid, bv[:, :, 0, :], ALU.subtract), *tb, *free)
            a = act(lambda e: e.activation(de, de, ACT.Exp, scale=1.0 / 16.0), u1, u2)

            def rest():
                tl = []
                for j, side in ((0, 1), (1, 0)):
                    ov = QKE[:, l, :].rearrange("p (b u s) -> p b u s", u=2, s=hs)[:, :, side, :]
                    iv = QK0[:, j, :].rearrange("p (b u s) -> p b u s", u=2, s=hs)[:, :, side, :]
                    tl.append(dve(lambda e, ov=ov, iv=iv, side=side: e.tensor_tensor(ov, iv, dv[:, :, side, :], ALU.mult),
                                  a, *tqk))
                tlev[l] = tl
            return rest

        tlev = {}
        open_level = []

        def levels(lo, hi):
            for l in range(lo, hi):
                r = level(l, 128 >> l)
                if open_level:
                    open_level.pop()()
                open_level.append(r)

        tiq = []

        def idx_turn():
            for tt in range(2):
                b = take()
                for m in range(4):
                    t = tr(b.t[:, m * P:m * P + P], IQ[:, tt * 576 + m * P:tt * 576 + m * P + P], ident,
                           tro + b.free, inc=(m == 3))
                u = act(lambda e, tt=tt, b=b: e.activation(IQT[:, :, tt * P:tt * P + P],
                                                           b.t[:, :].rearrange("p (m t) -> p m t", m=4), ACT.Copy), t)
                b.free = [u]
                tiq.append(u)
            b = take()
            for tt in range(2):
                t = tr(b.t[:, tt * P:tt * P + P], IKD[:, tt * P:tt * P + P], ident, tik + b.free, inc=(tt == 1))
            u = act(lambda e: e.activation(IKT, b.t[:, 0:256], ACT.Copy), t)
            b.free = [u]
            tiq.append(u)

        tsc = [[], []]
        rl_free = [[], []]

        def idx_scores(n):
            tt, m2, e2 = n // 4, n // 2 % 2, n % 2
            b = take()
            for j in range(2):
                t = mm(b.t[:, j * 256:j * 256 + 256], IQT[e2 * 64:e2 * 64 + 64, 2 * m2 + j, tt * P:tt * P + P],
                       IKT[e2 * 64:e2 * 64 + 64, :], True, True, tiq + b.free, inc=(j == 1))
            rl = RL[:, n % 2, :]
            a = act(lambda e: e.activation(rl, b.t[:, :], ACT.Relu, scale=0.125), t, *rl_free[n % 2])
            b.free = [a]
            for j in range(2):
                hd = 2 * (2 * m2 + j) + e2
                acc = SC[:, tt, :]
                o = CST["inval"][0] + tt * 256
                in1 = cst[:, o:o + 256] if hd == 0 else acc
                tsc[tt] = [dve(lambda e, j=j, hd=hd, in1=in1: e.scalar_tensor_tensor(
                    out=acc, in0=rl[:, j * 256:j * 256 + 256], scalar=IW[:, tt * 8 + hd:tt * 8 + hd + 1],
                    in1=in1, op0=ALU.mult, op1=ALU.add), a, tiw, TC, *tsc[tt])]
            rl_free[n % 2] = tsc[tt]

        tsel = [pool(lambda e: e.memset(SEL[:, P:256], BIGNEG))]

        def best(lo, hi):
            us = tsc
            wks = [SC[:, tt, 0:P * (tt + 1)] for tt in range(2)]
            for r in range(lo, hi):
                for tt in range(2):
                    m8 = small[:, 48 + 8 * ((2 * r + tt) % 8):56 + 8 * ((2 * r + tt) % 8)]
                    us[tt] = [dve(lambda e, wk=wks[tt], m8=m8: e.max(m8, wk), *us[tt])]
                for tt in range(2):
                    m8 = small[:, 48 + 8 * ((2 * r + tt) % 8):56 + 8 * ((2 * r + tt) % 8)]
                    us[tt] = [dve(lambda e, wk=wks[tt], m8=m8: e.match_replace(wk, m8, wk, -3.0e38), *us[tt])]
            for tt in range(2 if hi == 8 else 0):
                o = SELv[:, tt, 0:P * (tt + 1)]
                tsel.append(dve(lambda e, wk=wks[tt], o=o: e.tensor_scalar(o, wk, -2.0e38, BIGNEG, ALU.is_gt, ALU.mult),
                                *us[tt]))

        def scores(lo, hi):
            for n in range(lo, hi):
                idx_scores(n)

        idx_turn()
        levels(0, 3)
        qa_ready = []
        ssA = small[:, 32:48].rearrange("p (j t h) -> p j t h", j=2, t=2)
        for j, grow in enumerate(("gq_row", "gk_row")):
            for tt, (b, t) in enumerate(proj_tok(tn, (lambda: scores(0, 4)) if j == 0 else (lambda: best(0, 4)))):
                q = QA[:, tt, 4 * j:4 * j + 4, :]
                a = act(lambda e, q=q, b=b, tt=tt: e.activation(q, b.t[:, :].rearrange("p (h d) -> p h d", h=4), ACT.Square,
                                                                scale=ra.rs[:, tt:tt + 1]), t)
                sq = ssA[:, j, tt, :]
                u = dve(lambda e, q=q, sq=sq: e.tensor_reduce(sq, q, AX.X, ALU.add), a)
                u = inv_rms_row(sq, P, ra, tt, u)
                u = dve(lambda e, q=q, sq=sq, b=b: e.tensor_tensor(
                    q, b.t[:, :].rearrange("p (h d) -> p h d", h=4),
                    bc(sq.rearrange("p (h o) -> p h o", o=1), [P, 4, P]), ALU.mult), u)
                drop(b, u)
                g = VEC[grow][0]
                u = dve(lambda e, q=q, g=g: e.tensor_tensor(
                    q, q, bc(vec[:, g:g + P].rearrange("p (o d) -> p o d", o=1), [P, 4, P]), ALU.mult), u)
                qa_ready.append(u)
            if j == 0:
                scores(4, 8)
                levels(3, 4)
        tva = []
        for tt, (b, t) in enumerate(proj_tok(tn, lambda: best(4, 8))):
            u = act(lambda e, tt=tt, b=b: e.activation(VA[:, tt, :], b.t[:, :], ACT.Copy, scale=ra.rs[:, tt:tt + 1]), t)
            drop(b, u)
            tva.append(u)
        tqr = rope(QA, 8, 16, "cosA", "sinA", qa_ready + [TC])
        levels(4, 5)
        tq = []

        def qk_turn():
            for tt in range(2):
                for j in range(2):
                    b = take()
                    for hd in range(4):
                        t = tr(b.t[:, hd * P:hd * P + P], QA[:, tt, 4 * j + hd, :], ident, tqr + b.free, inc=(hd == 3))
                    u = act(lambda e, b=b, j=j, tt=tt: e.activation(QKT[:, 4 * j:4 * j + 4, tt * P:tt * P + P],
                                                                    b.t[:, :].rearrange("p (m t) -> p m t", m=4),
                                                                    ACT.Copy), t)
                    b.free = [u]
                    tq.append(u)

        def later():
            qk_turn()
            levels(5, 7)

        tog = []
        pr = proj_tok(tn, later)
        levels(7, 8)
        open_level.pop()()
        op("act", lambda e: e.preload_act_table_set("sigmoid_and_others"), [], inc=False)
        for tt, (b, t) in enumerate(pr):
            g = OG[:, tt, :]
            u = act(lambda e, g=g, b=b, tt=tt: e.activation(g, b.t[:, :], ACT.Sigmoid, scale=ra.rs[:, tt:tt + 1]), t)
            u = dve(lambda e, g=g, b=b, tt=tt: e.scalar_tensor_tensor(out=g, in0=b.t[:, :], scalar=ra.rs[:, tt:tt + 1], in1=g,
                                                                      op0=ALU.mult, op1=ALU.mult), u)
            drop(b, u)
            tog.append(u)
        op("act", lambda e: e.preload_act_table_set("natural_log_exp_and_others"), [], inc=False)

        tob = []
        am_free = [[], []]
        am_done = {}
        gm = const("gmask").bitcast(mybir.dt.uint32)
        ob_bank = {}
        ob_norm = {}

        def gla_1(n):
            tt, hd = n // 4, n % 4
            p, lo = hd // 2, hd % 2 * 64
            am = AM[:, n % 2 * 256:n % 2 * 256 + 256]
            tm, bs, ts = [], [], []
            for half in range(2):
                b = take()
                for i in range(4):
                    l = half * 4 + i + 1
                    c = p * 256 + tt * P
                    kx = QKE[lo:lo + 64, l, c:c + P] if l < 8 else QK0[lo:lo + 64, 1, c:c + P]
                    qx = QKE[lo:lo + 64, l, c:c + P] if l < 8 else QK0[lo:lo + 64, 0, c:c + P]
                    t = mm(b.t[:, i * P:i * P + P], kx, qx, True, True,
                           (tlev[l] if l < 8 else tqk) + b.free, inc=(i == 3))
                bs.append(b)
                ts.append(t)
            us = [[tam, *am_free[n % 2]] for _ in range(2)]
            for i in range(4):
                for half in range(2):
                    x, m = bs[half].t[:, i * P:i * P + P], gm[:, (half * 4 + i) * P:(half * 4 + i + 1) * P]
                    o = am[:, half * P:half * P + P]
                    us[half] = [dve(lambda e, x=x, m=m, o=o: e.copy_predicated(o, m, x), ts[half], TC, *us[half])]
            for half in range(2):
                bs[half].free = us[half]
                tm += us[half]
            if tt == 1:
                b = take()
                t = mm(b.t[:, 0:P], QKE[lo:lo + 64, 0, p * 256:p * 256 + P],
                       QKE[lo:lo + 64, 0, p * 256 + P:p * 256 + 256], True, True, tlev[0] + b.free, inc=True)
                u = act(lambda e: e.activation(AM2[:, n % 2 * P:n % 2 * P + P], b.t[:, 0:P], ACT.Copy), t,
                        *am_free[n % 2])
                b.free = [u]
                tm.append(u)
            am_done[n] = tm

        def gla_2(n):
            tt, hd = n // 4, n % 4
            if hd == 0:
                ob_bank[tt] = take(hold=True)
            ob, am = ob_bank[tt], AM[:, n % 2 * 256:n % 2 * 256 + 256]
            oo = ob.t[:, hd * P:hd * P + P]
            for i in range(2):
                t = mm(oo, am[:, i * P:i * P + P], VB[:, tt, hd * P:hd * P + P], i == 0, i == 1 and tt == 0,
                       am_done[n] + tvb + ob.free, inc=(i == 1))
            if tt == 1:
                t = mm(oo, AM2[:, n % 2 * P:n % 2 * P + P], VB[:, 0, hd * P:hd * P + P], False, True, [], inc=True)
            am_free[n % 2] = [t]
            if hd < 3:
                return
            ob_norm[tt] = act(lambda e: e.activation(YN[:, tt, :], ob.t[:, :], ACT.Square), t)

        def norm_1(tt):
            ss = small[:, 112 + 4 * tt:116 + 4 * tt]
            yv = YN[:, tt, :].rearrange("p (h d) -> p h d", h=4)
            u = dve(lambda e: e.tensor_reduce(ss, yv, AX.X, ALU.add), ob_norm[tt])
            ob_norm[tt] = inv_rms(ss, ss, P, u)

        def norm_2(tt):
            ob = ob_bank[tt]
            ss = small[:, 112 + 4 * tt:116 + 4 * tt]
            y = YN[:, tt, :]
            u = dve(lambda e: e.tensor_tensor(y.rearrange("p (h d) -> p h d", h=4),
                                              ob.t[:, :].rearrange("p (h d) -> p h d", h=4),
                                              bc(ss.rearrange("p (h o) -> p h o", o=1), [P, 4, P]), ALU.mult), ob_norm[tt])
            drop(ob, u)
            ob_norm[tt] = dve(lambda e: e.tensor_tensor(y, y, OG[:, tt, :], ALU.mult), u, tog[tt])

        def gla_3(tt):
            b = take()
            for hd in range(4):
                t = tr(b.t[:, hd * P:hd * P + P], YN[:, tt, hd * P:hd * P + P], ident, [ob_norm[tt]] + b.free,
                       inc=(hd == 3))
            o = catT[:, 4:8, tt * P:tt * P + P]
            x = b.t[:, :].rearrange("p (m t) -> p m t", m=4)
            u = act(lambda e: e.activation(o.hi, x, ACT.Copy, scale=vcol("g_gla")), t)
            u = dve(lambda e: e.scalar_tensor_tensor(out=o.lo, in0=x, scalar=vcol("g_gla"), in1=o.hi.bitcast(F32),
                                                     op0=ALU.mult, op1=ALU.subtract), u)
            b.free = [u]
            tob.append(u)

        scale = float(P) ** -0.5
        toa = []
        ss_free = [tqr, tqr]
        pt_free = [[], []]
        prob = {}

        def att_1(hd):
            b = take()
            for tt in range(2):
                t = mm(b.t[:, tt * 256:tt * 256 + 256], QKT[:, hd, tt * P:tt * P + P], QKT[:, 4 + hd, :], True, True,
                       tq + b.free, inc=(tt == 1))
            y = SS[:, hd % 2, :]
            yv = y.rearrange("p (t n) -> p t n", t=2)
            mx = small[:, 128 + 2 * hd:130 + 2 * hd]
            sm = small[:, 136 + 2 * hd:138 + 2 * hd]
            u = dve(lambda e: e.tensor_tensor(y, b.t[:, :], SEL, ALU.add), t, *tsel, *ss_free[hd % 2])
            b.free = [u]
            u = dve(lambda e: e.tensor_reduce(mx, yv, AX.X, ALU.max), u)
            u = dve(lambda e: e.tensor_scalar(mx, mx, -scale, None, ALU.mult), u)
            us = []
            for tt in range(2):
                us.append(act(lambda e, tt=tt: e.activation(
                    yv[:, tt, :], yv[:, tt, :], ACT.Exp, bias=mx[:, tt:tt + 1], scale=scale,
                    accum_out=sm[:, tt:tt + 1]), u))
            prob[hd] = us

        def att_2(hd):
            yv = SS[:, hd % 2, :].rearrange("p (t n) -> p t n", t=2)
            sm = small[:, 136 + 2 * hd:138 + 2 * hd]
            u = dve(lambda e: e.reciprocal(sm, sm), *prob[hd])
            prob[hd] = dve(lambda e: e.tensor_tensor(yv, yv, bc(sm.rearrange("p (t o) -> p t o", o=1), [P, 2, 256]),
                                                     ALU.mult), u)

        def att_3(hd):
            yv = SS[:, hd % 2, :].rearrange("p (t n) -> p t n", t=2)
            b = take()
            for i, (tt, kb) in enumerate(((0, 0), (1, 0), (1, 1))):
                t = tr(b.t[:, i * P:i * P + P], yv[:, tt, kb * P:kb * P + P], ident, [prob[hd]] + b.free,
                       inc=(i == 2))
            ss_free[hd % 2] = [t]
            prob[hd] = act(lambda e: e.activation(PT[:, hd % 2, :], b.t[:, 0:384], ACT.Copy), t, *pt_free[hd % 2])
            b.free = [prob[hd]]

        def att_4(hd):
            pt = PT[:, hd % 2, :]
            b = take()
            t = mm(b.t[:, 0:256], VA[:, 0, hd * P:hd * P + P], pt[:, 0:256], True, False, [prob[hd]] + tva + b.free)
            t = mm(b.t[:, P:256], VA[:, 1, hd * P:hd * P + P], pt[:, 256:384], False, True, [], inc=True)
            pt_free[hd % 2] = [t]
            toa.append(cat_evac(b, hd, t))

        def heads(i):
            if i < 8:
                gla_1(i)
            if 3 <= i < 7:
                att_3(i - 3)
            if 4 <= i < 8:
                att_4(i - 4)
            if i >= 1:
                gla_2(i - 1)
            if 2 <= i < 6:
                att_2(i - 2)
            if 1 <= i < 5:
                att_1(i - 1)
            if i == 5:
                norm_1(0)
            if i == 6:
                norm_2(0)
            if i == 7:
                gla_3(0)
            if i == 8:
                norm_1(1)
                norm_2(1)

        tvb = []
        for tt, (b, t) in enumerate(proj_tok(tn, lambda: heads(0))):
            u = act(lambda e, tt=tt, b=b: e.activation(VB[:, tt, :], b.t[:, :], ACT.Copy, scale=ra.rs[:, tt:tt + 1]), t)
            drop(b, u)
            tvb.append(u)
        for i in range(1, 9):
            heads(i)

        th, turn = out_h(lambda k: catT[:, k, :], 4, lambda k: [toa[k]] if k < 4 else tob, 8, "g_ffn0",
                         lambda it: gla_3(1) if it == 1 else None)
        th, turn = mlp(turn, th, "f", "g_mix1")

        A = Area("c")
        QT = A(2048).rearrange("p (k t) -> p k t", k=8)
        KT = A(2048).rearrange("p (k t) -> p k t", k=8)
        VC = A(2048).rearrange("p (t n) -> p t n", t=2)
        QN = A(2048).rearrange("p (j n) -> p j n", j=4)
        NZ = 6
        ZB = [[A(384) for _ in range(3)] for _ in range(NZ)]
        tn, rc = turn.tn, turn
        gs = small[:, 144:145]
        tgs = dve(lambda e: e.tensor_scalar(gs, vcol("gq_c"), float(P) ** -0.5, None, ALU.mult), TV)
        tqk = [[], []]
        qn_free = [[] for _ in range(4)]

        def turn(j, half, tt, n, u):
            b = take()
            for hd in range(4):
                t = tr(b.t[:, hd * P:hd * P + P], QN[:, n, hd * P:hd * P + P], ident, [u] + b.free, inc=(hd == 3))
            qn_free[n] = [t]
            dst = (QT, KT)[j][:, half * 4:half * 4 + 4, tt * P:tt * P + P]
            g = gs if j == 0 else vcol("gk_c")
            v = act(lambda e: e.activation(dst, b.t[:, :].rearrange("p (m t) -> p m t", m=4), ACT.Copy, scale=g), t, tgs)
            b.free = [v]
            tqk[half].append(v)

        sm = const("smask")
        z_free = [[] for _ in range(NZ)]
        tc_ = []
        tv = [[], []]
        st = {}

        sticked = []

        def stick(i):
            if 0 <= i - 3 < 8:
                Z, E1, LL = ZB[(i - 3) % NZ]
                st[i - 3] = act(lambda e, LL=LL, Z=Z: e.activation(LL, Z, ACT.Exp), st[i - 3])
            if 0 <= i - 2 < 8:
                Z2, E1, LL2 = ZB[(i - 2) % NZ]
                u2 = dve(lambda e, Z=Z2, E1=E1, LL=LL2: e.scalar_tensor_tensor(out=LL, in0=Z, scalar=0.0, in1=E1, op0=ALU.max,
                                                                              op1=ALU.add), st[i - 2])
            if 0 <= i - 5 < 8:
                tc_.append(cat_evac(*sticked.pop()))
            if 0 <= i - 4 < 8:
                hd = i - 4
                LL = ZB[hd % NZ][2]
                b4 = take()
                t = mm(b4.t[:, 0:256], VC[:, 0, hd * P:hd * P + P], LL[:, 0:256], True, False,
                       [st[hd]] + tv[hd // 4] + b4.free)
                t4 = mm(b4.t[:, P:256], VC[:, 1, hd * P:hd * P + P], LL[:, 256:384], False, True, [], inc=True)
                z_free[hd % NZ] = [t4]
                sticked.append((b4, hd, t4))
            if 0 <= i - 2 < 8:
                b = take()
                t = mm(b.t[:, 0:256], tri, LL2[:, 0:256], True, False, [u2, TC] + b.free)
                t = mm(b.t[:, P:256], ones, LL2[:, 256:384], False, True, [])
                t = mm(b.t[:, 256:384], tri, LL2[:, 256:384], True, True, [], inc=True)
                st[i - 2] = dve(lambda e, Z=Z2, b=b: e.tensor_tensor(Z, Z, b.t[:, 0:384], ALU.subtract), t)
                b.free = [st[i - 2]]
            if i < 8:
                Z, E1, LL = ZB[i % NZ]
                b = take()
                t = mm(b.t[:, 0:256], KT[:, i, 0:P], QT[:, i, :], True, True, tqk[i // 4] + b.free)
                t = mm(b.t[:, 256:384], KT[:, i, P:256], QT[:, i, P:256], True, True, [], inc=True)
                u = dve(lambda e, Z=Z, b=b: e.tensor_tensor(Z, b.t[:, 0:384], sm, ALU.add), t, TC, *z_free[i % NZ])
                b.free = [u]
                u = act(lambda e, Z=Z, E1=E1: e.activation(E1, Z, ACT.Abs), u)
                u = act(lambda e, E1=E1: e.activation(E1, E1, ACT.Exp, scale=-1.0), u)
                st[i] = act(lambda e, E1=E1: e.activation(E1, E1, ACT.Ln, bias=1.0), u)
        todo = []

        def turns():
            while todo:
                turn(*todo.pop(0))

        def normed(j, half, pr):
            for tt, (b, t) in enumerate(pr):
                n = (2 * half + j) * 2 + tt
                q = QN[:, n % 4, :]
                qv = q.rearrange("p (h d) -> p h d", h=4)
                ss = small[:, 148 + 4 * n:152 + 4 * n]
                a = act(lambda e, q=q, b=b, tt=tt: e.activation(q, b.t[:, :], ACT.Square, scale=rc.rs[:, tt:tt + 1]), t,
                        *rc.trs, *qn_free[n % 4])
                u = dve(lambda e, qv=qv, ss=ss: e.tensor_reduce(ss, qv, AX.X, ALU.add), a)
                u = inv_rms_row(ss, P, rc, tt, u)
                u = dve(lambda e, qv=qv, ss=ss, b=b: e.tensor_tensor(
                    qv, b.t[:, :].rearrange("p (h d) -> p h d", h=4),
                    bc(ss.rearrange("p (h o) -> p h o", o=1), [P, 4, P]), ALU.mult), u)
                drop(b, u)
                todo.append((j, half, tt, n % 4, u))

        def values(half, pr):
            for tt, (b, t) in enumerate(pr):
                u = act(lambda e, tt=tt, b=b: e.activation(VC[:, tt, half * 512:half * 512 + 512], b.t[:, :], ACT.Copy,
                                                           scale=rc.rs[:, tt:tt + 1]), t)
                drop(b, u)
                tv[half].append(u)

        normed(0, 0, proj_tok(tn, None, lambda: rc.rest(th)))
        pr = proj_tok(tn)
        turns()
        normed(1, 0, pr)
        pr = proj_tok(tn)
        turns()
        normed(0, 1, pr)
        pr = proj_tok(tn)
        turns()
        normed(1, 1, pr)
        pr = proj_tok(tn, lambda: stick(0))
        turns()
        stick(1)
        values(0, pr)
        values(1, proj_tok(tn, lambda: stick(2)))
        for i in (3, 4, 5, 6, 7):
            stick(i)

        def more_sticks(it):
            for i in ((), (8,), (9, 10), (11, 12))[it]:
                stick(i)

        th, turn = out_h(lambda k: catT[:, k, :], 4, lambda k: [tc_[k]], 8, "g_ffn1", more_sticks)
        o_meta = (end - 4 * (2 * D + 8 * META)) // 32 * 32
        meta = at("meta", D, o_meta)[0:META, :]
        mnorm = at("mnorm", D, o_meta + 4 * D)[0:META, :]
        mtmp = at("mtmp", 8 * META, o_meta + 8 * D).rearrange("p (k t) -> p k t", k=8)
        dma(lambda e: e.dma_start(meta, MT), th[1][1], s_g)
        TM = (s_g, 16)
        tmr, tmeta = [], []

        def meta_rows():
            ms, mr = small[0:META, 8:9], small[0:META, 9:10]
            a = act(lambda e: e.activation(mnorm, meta, ACT.Square, accum_out=ms), TM)
            t = act(lambda e: e.activation(mr, ms, ACT.Ln, bias=eps[0:META, :], scale=1.0 / D), TV, a)
            t = act(lambda e: e.activation(mr, mr, ACT.Exp, scale=-0.5), t)
            tmr.append(dve(lambda e: e.tensor_scalar(mnorm, meta, mr, None, ALU.mult), t))

        def meta_norm(up_done):
            b = take()
            for k in range(8):
                t = tr(b.t[:, k * META:k * META + META], mnorm[:, k * P:k * P + P], ident[0:META, 0:META], tmr + b.free,
                       inc=(k == 7))
            u = dve(lambda e: e.tensor_tensor(mtmp, b.t[:, 0:P].rearrange("p (k t) -> p k t", k=8),
                                              bc(vcol("g_mix_pre", 0, 8).rearrange("p (k o) -> p k o", o=1), [P, 8, META]),
                                              ALU.mult), t)
            b.free = [u]
            o = nT2[:, :, 0:META]
            a = act(lambda e: e.activation(o.hi, mtmp, ACT.Copy), u, up_done)
            tmeta.append(dve(lambda e: e.tensor_tensor(o.lo, mtmp, o.hi.bitcast(F32), ALU.subtract), a))

        th, _ = mlp(turn, th, "g", None, meta_rows, meta_norm)
        th = [x[0] + x[1] for x in th]

        A = Area("b")
        HT_ = A(8 * L2)
        HT = HT_.rearrange("p (k t) -> p k t", k=8)
        SQ = A(2 * L2).rearrange("p (j t) -> p j t", j=2)
        RS = A(L2)
        o_ffn = A.at
        A(2 * L2)
        UT = A(4 * L2).rearrange("p (k t) -> p k t", k=4)
        GT = A(16 * N2).rearrange("p (k t) -> p k t", k=16)
        CG = A(4 * N2).rearrange("p (k t) -> p k t", k=4)
        CV = A(4 * N2).rearrange("p (k t) -> p k t", k=4)
        FT = A.pair(4 * N2).view("p (k t) -> p k t", k=4)
        YB = A.pair(4 * N2).view("p (k t) -> p k t", k=4)
        cm = A(2 * L2)[0:META, :]
        P1s = [A(3 * 256).rearrange("p (t n) -> p t n", t=3) for _ in range(2)]
        dlx = A(4 * L2)
        assert A.at <= o_meta
        MG = Pair(at("mhi", 8 * N2, o_xn, F32R), at("mlo", 8 * N2, o_clo, F32R)).view("p (k t) -> p k t", k=8)
        th_all = th[0] + th[1]
        dma(lambda e: e.dma_start(cm, CM), th_all, s_d)
        dma(lambda e: e.dma_start(dlx, DL), th_all, s_d)
        TD = (s_d, 32)
        t_ht = []

        t_res = []

        def residual_T():
            for q in range(4):
                b = take(True)
                for kk in range(2):
                    for tt in range(2):
                        t = tr(b.t[:, kk * 256 + tt * P:kk * 256 + tt * P + P], h[:, tt, (2 * q + kk) * P:(2 * q + kk + 1) * P],
                               ident, th_all + b.free, inc=(kk == 1 and tt == 1))
                t_res.append((q, b, t))

        def residual_copy():
            for q, b, t in t_res:
                u = act(lambda e, q=q, b=b: e.activation(HT[:, 2 * q:2 * q + 2, META:L2],
                                                         b.t[:, :].rearrange("p (k t) -> p k t", k=2), ACT.Copy), t)
                drop(b, u)
                t_ht.append(u)

        def residual_meta():
            b = take()
            for k in range(8):
                t = tr(b.t[:, k * META:k * META + META], meta[:, k * P:k * P + P], ident[0:META, 0:META], [TM] + b.free,
                       inc=(k == 7))
            u = act(lambda e: e.activation(HT[:, :, 0:META], b.t[:, 0:P].rearrange("p (k t) -> p k t", k=8), ACT.Copy),
                    t, *th_all)
            b.free = [u]
            t_ht.append(u)

        tn = [x + tmeta for x in norm_T("g_mix_pre", th, nT2, META, residual_T)]
        residual_copy()
        sq_free = [[], []]

        class ColNorm:

            def __init__(self):
                self.b = take(True)
                self.k = 0
                self.sq = None

            def square(self, x, *ready):
                k = self.k
                s2 = SQ[:, k % 2, 0:N2]
                self.sq = (k, s2, act(lambda e: e.activation(s2, x, ACT.Square), *ready, *sq_free[k % 2]))
                self.k += 1
                return self.sq[2]

            def add(self):
                k, s2, a = self.sq
                t = mm(self.b.t[:, 0:N2], ones, s2, k == 0, k == 7, [a, TC] + self.b.free, inc=True)
                sq_free[k % 2] = [t]
                self.t = t

            def done(self, *free):
                u = act(lambda e: e.activation(RS[:, 0:N2], self.b.t[:, 0:N2], ACT.Ln, bias=eps, scale=1.0 / D), self.t,
                        *free)
                drop(self.b, u)
                return act(lambda e: e.activation(RS[:, 0:N2], RS[:, 0:N2], ACT.Exp, scale=-0.5), u)

        def split(x, o, *ready):
            a = act(lambda e: e.activation(o.hi, x, ACT.Copy), *ready)
            return dve(lambda e: e.tensor_tensor(o.lo, x, o.hi.bitcast(F32), ALU.subtract), a)

        def norm_cols(gname, c0, ready):
            out = []
            us = []
            for k in range(9):
                if k < 8:
                    x = GT[:, k, 0:L2 - c0]
                    us.append(dve(lambda e, k=k, x=x: e.scalar_tensor_tensor(
                        out=x, in0=HT[:, k, c0:L2], scalar=vcol(gname, k), in1=RS[:, 0:L2 - c0], op0=ALU.mult, op1=ALU.mult),
                        *ready))
                if k:
                    out.append([split(GT[:, k - 1, 0:L2 - c0], nT2[:, k - 1, c0:L2], us[k - 1])])
            return out

        def proj_feat(w, c, ready, tk, c0, kn=8, rhs=None):
            b = take()
            for k in range(kn):
                r = nT2[:, k, c0:L2] if rhs is None else rhs[:, k, :]
                t = mm3(b.t[:, 0:L2 - c0], w[:, k, c:c + P], r, k == 0, k == kn - 1, tk + ready[k] + b.free,
                        inc=(k == kn - 1))
            return b, t

        def feat_blocks(blocks, per, kn, ready, c0, rhs=None):
            for m in range(blocks):
                if m % per == 0:
                    w, tk, i = use(kn)
                b, t = proj_feat(w, m % per * P, ready, tk, c0, kn, rhs)
                if m % per == per - 1:
                    released[i] = t
                yield m, b, t

        tu = []
        for m, b, t in feat_blocks(4, 2, 8, tn, 0):
            u = act(lambda e, b=b, m=m: e.activation(UT[:, m, :], b.t[:, 0:L2], ACT.Copy), t)
            b.free = [u]
            tu.append(u)
        residual_meta()
        tcg = []
        for m, b, t in feat_blocks(4, 2, 8, tn, X0):
            u = act(lambda e, b=b, m=m: e.activation(CG[:, m, :], b.t[:, 0:N2], ACT.Copy), t)
            b.free = [u]
            tcg.append(u)
        tcv = []
        for m, b, t in feat_blocks(4, 2, 8, tn, X0):
            u = dve(lambda e, b=b, m=m: e.tensor_tensor(CG[:, m, :], CG[:, m, :], b.t[:, 0:N2], ALU.mult), t, tcg[m])
            b.free = [u]
            u = act(lambda e, m=m: e.activation(CV[:, m, :], CG[:, m, :], ACT.Identity, bias=vcol("conv_b_mix", m),
                                                scale=vcol("conv_w_mix", 4 + m)), u)
            u = dve(lambda e, m=m: e.scalar_tensor_tensor(out=CV[:, m, 1:N2], in0=CG[:, m, 0:N2 - 1],
                                                          scalar=vcol("conv_w_mix", m), in1=CV[:, m, 1:N2],
                                                          op0=ALU.mult, op1=ALU.add), u)
            u = dve(lambda e, m=m: e.scalar_tensor_tensor(out=CV[:, m, 0:N2 - 1], in0=CG[:, m, 1:N2],
                                                          scalar=vcol("conv_w_mix", 8 + m), in1=CV[:, m, 0:N2 - 1],
                                                          op0=ALU.mult, op1=ALU.add), u)
            tcv.append(u)
        tyb = []
        for m, b, t in feat_blocks(4, 2, 8, tn, X0):
            u = dve(lambda e, b=b, m=m: e.tensor_tensor(CV[:, m, :], CV[:, m, :], b.t[:, 0:N2], ALU.mult), t, tcv[m])
            b.free = [u]
            tyb.append([split(CV[:, m, :], YB[:, m, :], u)])
        dftc = const("dftc")
        dl = dlx.rearrange("p (t j l) -> p t j l", t=2, j=2)
        cmv = cm.rearrange("p (j l) -> p j l", j=2)
        p1_free = [[], []]
        p1_done = {}
        tft = []

        def dft_channels(g):
            P1 = P1s[g % 2]
            us = []
            for i, (c, n) in enumerate(((META, P), (META + P, P), (0, META))):
                b = take()
                t = mm(b.t[0:n, 0:256], UT[:, g, c:c + n], dftc, True, True, [tu[g], TC] + b.free, inc=True)
                u = act(lambda e, b=b, n=n, i=i: e.activation(P1[0:n, i, :], b.t[0:n, 0:256], ACT.Copy), t, *p1_free[g % 2])
                b.free = [u]
                us.append(u)
            p1_done[g] = us

        def dft_positions(g):
            P1 = P1s[g % 2]
            b = take()
            n = 0
            for i in range(3):
                for j in range(2):
                    kp = P if i < 2 else META
                    rhs = dl[:, i, j, X0:L2] if i < 2 else cmv[:, j, X0:L2]
                    t = mm(b.t[:, 0:N2], P1[0:kp, i, j * P:j * P + P], rhs, n == 0, n == 5, p1_done[g] + [TD] + b.free,
                           inc=(n == 5))
                    n += 1
            p1_free[g % 2] = [t]
            u = split(b.t[:, 0:N2], FT[:, g, :], t)
            b.free = [u]
            tft.append([u])

        op("act", lambda e: e.preload_act_table_set("sigmoid_and_others"), [], inc=False)
        tgt = []
        for g, b, t in feat_blocks(16, 2, 8, tn, X0):
            u = act(lambda e, b=b, g=g: e.activation(GT[:, g, :], b.t[:, 0:N2], ACT.Sigmoid, bias=vcol("b_gates", g)), t)
            b.free = [u]
            tgt.append(u)
            if g % 4 == 0:
                dft_channels(g // 4)
            if g % 4 == 2:
                dft_positions(g // 4)
        op("act", lambda e: e.preload_act_table_set("natural_log_exp_and_others"), [], inc=False)
        tga, tmg, late = [], [], []

        def merged_lo():
            while late:
                o, x, a = late.pop()
                tmg.append([dve(lambda e: e.tensor_tensor(o.lo, x, o.hi.bitcast(F32), ALU.subtract), a)])

        for part in range(2):
            for m, b, t in feat_blocks(4, 4, 4, tft, X0, FT):
                m += 4 * part
                u = dve(lambda e, b=b, m=m: e.tensor_tensor(GT[:, m, :], GT[:, m, :], b.t[:, 0:N2], ALU.mult), t, tgt[m])
                b.free = [u]
                tga.append(u)
                merged_lo()
            for m, b, t in feat_blocks(4, 4, 4, tyb, X0, YB):
                m += 4 * part
                u = dve(lambda e, b=b, m=m: e.tensor_tensor(GT[:, 8 + m, :], GT[:, 8 + m, :], b.t[:, 0:N2], ALU.mult), t,
                        tgt[8 + m])
                b.free = [u]
                merged_lo()
                u = dve(lambda e, m=m: e.tensor_tensor(GT[:, m, :], GT[:, m, :], GT[:, 8 + m, :], ALU.add), u, tga[m])
                a = act(lambda e, m=m: e.activation(MG.hi[:, m, :], GT[:, m, :], ACT.Copy), u)
                late.append((MG[:, m, :], GT[:, m, :], a))
        merged_lo()
        tmx = []
        cn = ColNorm()
        for g, b, t in feat_blocks(8, 2, 8, tmg, X0, MG):
            if g:
                cn.add()
            u = cn.square(b.t[:, 0:N2], t)
            u = act(lambda e, b=b, g=g: e.activation(GT[:, 8 + g, :], b.t[:, 0:N2], ACT.Copy, scale=vcol("g_mix_post", g)), u)
            b.free = [u]
            tmx.append(u)
        cn.add()
        tr_ = cn.done()
        th2 = []
        cn = ColNorm()
        for k in range(8):
            u = dve(lambda e, k=k: e.tensor_tensor(GT[:, 8 + k, :], GT[:, 8 + k, :], RS[:, 0:N2], ALU.mult), tr_, tmx[k])
            u = dve(lambda e, k=k: e.tensor_tensor(HT[:, k, X0:L2], HT[:, k, X0:L2], GT[:, 8 + k, :], ALU.add), u, *t_ht)
            th2.append(u)
            cn.square(HT[:, k, X0:L2], u)
            cn.add()
        tr_ = cn.done(u)
        tn = norm_cols("g_ffn_pre", X0, [tr_])
        t_h = []

        def residual_back(tt, c):
            b = take()
            for m in range(4):
                t = tr(b.t[:, m * P:m * P + P], HT[:, c * 4 + m, META + tt * P:META + tt * P + P], ident,
                       th2 + b.free, inc=(m == 3))
            u = act(lambda e: e.activation(h[:, tt, c * 512:c * 512 + 512], b.t[:, :], ACT.Copy), t)
            b.free = [u]
            t_h.append(u)

        A = Area("e")
        A.at = o_ffn
        ffp = A.pair(22 * S)
        A(64)
        ff = ffp.view("p (k t) -> p k t", k=22)
        UPB = [[A(S), A(S)] for _ in range(4)]
        gp = A(D)
        s_gp = sem("s_gp")
        dma(lambda e: e.dma_start(gp, GP), tn[7], s_gp)
        up_free = [[] for _ in range(4)]
        tf = []
        op("act", lambda e: e.preload_act_table_set("gelu_apprx_tanh_and_others"), [], inc=False)
        prods = {}

        def ff_mul(n):
            x, y, a, v = prods[n]
            u = dve(lambda e: e.tensor_tensor(x, x, y, ALU.mult), a, v)
            prods[n] = act(lambda e: e.activation(ff.hi[:, n, :], x, ACT.Copy), u)

        def ff_rest(n):
            x = UPB[n % 4][0]
            u = dve(lambda e: e.tensor_tensor(ff.lo[:, n, :], x, ff.hi[:, n, :].bitcast(F32), ALU.subtract), prods[n])
            up_free[n % 4] = [u]
            tf.append(u)

        for n in range(22):
            w, tk, i = use(8)
            bufs = UPB[n % 4]
            us = []
            for av in range(2):
                b, t = proj_feat(w, av * P, tn, tk, X0)
                ch = av * 22 + n
                o = bufs[av]
                u = act(lambda e, b=b, ch=ch, o=o: e.activation(o, b.t[:, 2:N2], ACT.Identity,
                                                                bias=vcol("conv_b_ffn", ch),
                                                                scale=vcol("conv_w_ffn", 44 + ch)), t, *up_free[n % 4])
                u = dve(lambda e, b=b, ch=ch, o=o: e.scalar_tensor_tensor(
                    out=o, in0=b.t[:, 1:N2 - 1], scalar=vcol("conv_w_ffn", ch), in1=o, op0=ALU.mult, op1=ALU.add), u)
                u = dve(lambda e, b=b, ch=ch, o=o: e.scalar_tensor_tensor(
                    out=o[:, 0:S - 1], in0=b.t[:, 3:N2], scalar=vcol("conv_w_ffn", 88 + ch), in1=o[:, 0:S - 1],
                    op0=ALU.mult, op1=ALU.add), u)
                b.free = [u]
                us.append(u)
                if av == 0 and n:
                    ff_mul(n - 1)
            released[i] = t
            if n == 21:
                split_tile(len(split_done))
            a = act(lambda e, o=bufs[0]: e.activation(o, o, ACT.Gelu_apprx_tanh), us[0])
            prods[n] = (bufs[0], bufs[1], a, us[1])
            if n:
                ff_rest(n - 1)
            if 1 <= n <= 4:
                residual_back((n - 1) // 2, (n - 1) % 2)
        ff_mul(21)
        ff_rest(21)
        def before(it):
            if it == 4:
                op("act", lambda e: e.preload_act_table_set("natural_log_exp_and_others"), [], inc=False)

        bs = out_tok(lambda k: ff[:, k, :], 11, lambda k: [tf[k]], 22, before)
        YG = [A(D) for _ in range(2)]
        us = [[], []]
        yg = [[], []]

        def take_out(tt, c):
            b = bs[2 * tt + c]
            k = 240 + 2 * tt + c
            o = YG[tt][:, c * 512:c * 512 + 512]
            u = act(lambda e: e.activation(xn[:, tt, c * 512:c * 512 + 512], b.t[:, :], ACT.Square,
                                           accum_out=small[:, k:k + 1]), b.token)
            us[tt].append(u)
            yg[tt].append(dve(lambda e: e.tensor_tensor(o, b.t[:, :], gp[:, c * 512:c * 512 + 512], ALU.mult), u, (s_gp, 16)))

        def row_rms(tt):
            k = 240 + 2 * tt
            u = dve(lambda e: e.tensor_tensor(small[:, 244 + tt:245 + tt], small[:, k:k + 1], small[:, k + 1:k + 2], ALU.add),
                    *us[tt])
            return inv_rms(small[:, 244 + tt:245 + tt], small[:, 246 + tt:247 + tt], D, u)

        def put_out(tt, r):
            for c in range(2):
                o = YG[tt][:, c * 512:c * 512 + 512]
                v = dve(lambda e, c=c, o=o: e.scalar_tensor_tensor(
                    out=o, in0=o, scalar=small[:, 246 + tt:247 + tt], in1=h[:, tt, c * 512:c * 512 + 512], op0=ALU.mult,
                    op1=ALU.add), r, yg[tt][c], *t_h)
                dma(lambda e, c=c, o=o: e.dma_start(OUT[tt * P:tt * P + P, c * 512:c * 512 + 512], o), [v], s_o)

        take_out(0, 0)
        take_out(0, 1)
        r0 = row_rms(0)
        take_out(1, 0)
        put_out(0, r0)
        take_out(1, 1)
        put_out(1, row_rms(1))
        assert used[0] == len(sizes)

        def run(eng, name):
            seen = {}
            for waits, fn, inc in queues[name]:
                need = {}
                for tok in waits:
                    s, v = tok
                    need[id(s)] = (s, max(v, need.get(id(s), (s, 0))[1]))
                for key, (s, v) in need.items():
                    if seen.get(key, 0) < v:
                        eng.wait_ge(s, v)
                        seen[key] = v
                ins = fn(eng)
                if inc:
                    ins.then_inc(*inc)

        block = ctx.enter_context(nc.Block())

        @block.sync
        def _(eng):
            run(eng, "sp")
            eng.wait_ge(s_o, 64)

        @block.scalar
        def _(eng):
            run(eng, "act")

        @block.vector
        def _(eng):
            run(eng, "dve")

        @block.gpsimd
        def _(eng):
            run(eng, "pool")

        @block.tensor
        def _(eng):
            run(eng, "pe")


def weight_stream(a):
    out = []

    def kn(w, k0=0, k1=None):
        n = w.shape[1]
        return w.reshape(-1, P, n).transpose(1, 0, 2)

    def put(t):
        out.append(np.ascontiguousarray(t).reshape(-1))

    def cols(w, lo, hi):
        put(kn(w[:, lo:hi]))

    def rows(w, per=2):
        k = w.shape[0] // P
        for i in range(0, k, per):
            put(kn(w[i * P:(i + per) * P]))

    def quarter(w, lo, hi):
        for i in range(2):
            put(kn(w[i * 512:i * 512 + 512, lo:hi]))

    w = a["w_in_ab"][0]
    quarter(w, 1536, 2048)
    put(np.concatenate([kn(w[:, 3144:3160]), kn(w[:, 2048:2120])], axis=2))
    cols(w, 2120, 2376)
    cols(w, 2376, 2632)
    for c in (0, 512, 1024, 3160, 2632):
        quarter(w, c, c + 512)
    rows(a["w_out_ab"][0])

    def mlp(l):
        for i in range(16):
            cols(a["w_up"][l], i * 256, i * 256 + 256)
        rows(a["w_down"][l])

    mlp(0)
    for i in (0, 2, 1, 3, 4, 5):
        quarter(a["w_in_c"][0], i * 512, i * 512 + 512)
    rows(a["w_out_c"][0])
    mlp(1)
    w = a["w_in_2"][0]
    for c in (0, 512, 1536, 1024, 2048, 2560, 3072, 3584):
        cols(w, c, c + 256)
        cols(w, c + 256, c + 512)
    for c in (0, 512):
        cols(a["w_fourier_2"][0], c, c + 512)
        cols(a["w_conv_out_2"][0], c, c + 512)
    w = a["w_out_2"][0]
    for c in range(0, 1024, 256):
        cols(w, c, c + 256)
    w = a["w_up_2"][0]
    for i in range(22):
        put(np.concatenate([kn(w[:, i * P:i * P + P]), kn(w[:, 2816 + i * P:2816 + i * P + P])], axis=2))
    rows(a["w_down_2"][0])
    return np.concatenate(out)


def vectors(a):
    v = np.zeros((P, NVEC), np.float32)

    def put(name, x):
        o, n = VEC[name]
        v[:, o:o + n] = np.asarray(x).reshape(-1, P).T

    for l in range(2):
        put(f"g_mix{l}", a["g_mix"][l])
        put(f"g_ffn{l}", a["g_ffn"][l])
    put("b_gate", a["b_gate"][0])
    put("g_gla", a["g_gla"][0])
    put("gq_c", a["gq_c"][0])
    put("gk_c", a["gk_c"][0])
    put("g_mix_pre", a["g_mix_pre_2"][0])
    put("b_gates", a["b_gates_2"][0])
    put("conv_w_mix", a["conv_w_mix_2"][0])
    put("conv_b_mix", a["conv_b_mix_2"][0])
    put("g_mix_post", a["g_mix_post_2"][0])
    put("g_ffn_pre", a["g_ffn_pre_2"][0])
    put("conv_w_ffn", a["conv_w_ffn_2"][0])
    put("conv_b_ffn", a["conv_b_ffn_2"][0])
    v[:, VEC["ident"][0]:VEC["ident"][0] + P] = np.eye(P, dtype=np.float32)
    v[:, VEC["eps"][0]] = EPS
    for name, key in (("gq_row", "gq_a"), ("gk_row", "gk_a")):
        o, n = VEC[name]
        v[:, o:o + n] = np.broadcast_to(a[key][0][None, :], (P, P))
    return v


def kernel(**inputs):
    import concourse.bacc as bacc
    from concourse.bass_utils import run_bass_kernel_spmd

    a = {k: np.asarray(v) for k, v in inputs.items()}
    c, dlx, cm, tri = constants()
    arrays = {
        "w_stream": weight_stream(a),
        "vectors": vectors(a),
        "consts": c,
        "consts_x": dlx,
        "consts_m": cm,
        "tri": tri,
        "x_rows": np.ascontiguousarray(a["x"][0]),
        "meta_rows": np.ascontiguousarray(a["meta_tokens_2"]),
        "gate_up": np.ascontiguousarray(a["w_gate_up"][0]),
        "g_post": np.ascontiguousarray(np.broadcast_to(a["g_ffn_post_2"][0][None, :], (P, D))),
    }
    nc = bacc.Bacc("TRN2", target_bir_lowering=False, num_devices=1)
    args = [nc.dram_tensor(k, v.shape, F32, kind="ExternalInput").ap() for k, v in arrays.items()]
    out = nc.dram_tensor("out_rows", (S, D), F32, kind="ExternalOutput").ap()
    block_kernel(nc, *args, out)
    r = run_bass_kernel_spmd(nc, [arrays], core_ids=[0])
    return r.results[0]["out_rows"].reshape(1, S, D)
```
